# Optimizing a Trainium2 kernel written in Bass

```python
import jax, jax.numpy as jnp
from jax import lax
import numpy as np
import math

D_MODEL = 1024
BATCH = 1
SEQ = 512
DEPTH = 1

CHUNK = 64
HEAD_DIM = 64
H_SB = 8
H_CH = 8
W_SB = H_SB * HEAD_DIM
W_CH = H_CH * HEAD_DIM
MIX_WIDTH = W_SB + W_CH
LOOKBACK = 8
BAND = (LOOKBACK + 1) * CHUNK
REL_CLIP = 128
Q_BLOCK = 128
D_FF = 2816
PLE_DIM = 256
EPS = 1e-6
NEG_INF = -1e30


def rms_norm(x, g):
    xf = x.astype(jnp.float32)
    y = xf * lax.rsqrt(jnp.mean(xf * xf, axis=-1, keepdims=True) + EPS)
    return (y * g.astype(jnp.float32)).astype(x.dtype)

def swiglu(x, w_gate, w_up, w_down):
    return (jax.nn.silu(x @ w_gate) * (x @ w_up)) @ w_down

def split_heads(t, n_heads):
    b, s, _ = t.shape
    return t.reshape(b, s, n_heads, HEAD_DIM).transpose(0, 2, 1, 3)

def merge_heads(t):
    b, h, s, d = t.shape
    return t.transpose(0, 2, 1, 3).reshape(b, s, h * d)

def stick_breaking_attention(q, k, v):
    b, h, s, d = q.shape
    nq = s // Q_BLOCK
    scale = d ** -0.5
    q_blocks = q.reshape(b, h, nq, Q_BLOCK, d).transpose(2, 0, 1, 3, 4)
    starts = jnp.arange(nq, dtype=jnp.int32) * Q_BLOCK
    key_pos = jnp.arange(s, dtype=jnp.int32)

    def one_block(args):
        q_blk, start = args
        z = jnp.einsum('bhqd,bhkd->bhqk', q_blk, k,
                       preferred_element_type=jnp.float32) * scale
        q_pos = start + jnp.arange(Q_BLOCK, dtype=jnp.int32)
        before = key_pos[None, :] < q_pos[:, None]
        log_fail = jnp.where(before, jax.nn.log_sigmoid(-z), 0.0)
        later = lax.cumsum(log_fail, axis=3, reverse=True) - log_fail
        log_a = jax.nn.log_sigmoid(z) + later
        a = jnp.where(before, jnp.exp(jnp.where(before, log_a, 0.0)), 0.0)
        return jnp.einsum('bhqk,bhkd->bhqd', a.astype(v.dtype), v)

    out = lax.map(one_block, (q_blocks, starts))
    return out.transpose(1, 2, 0, 3, 4).reshape(b, h, s, d)

def rel_bias_index():
    i = np.arange(CHUNK)[:, None]
    j = np.arange(BAND)[None, :]
    dist = i + LOOKBACK * CHUNK - j
    return jnp.asarray(np.clip(dist, -REL_CLIP, REL_CLIP) + REL_CLIP, dtype=jnp.int32)

def chunk_band_attention(q, k, v, rel_bias):
    b, h, s, d = q.shape
    nc = s // CHUNK
    scale = d ** -0.5
    qc = q.reshape(b, h, nc, CHUNK, d)

    def band(t):
        tc = t.reshape(b, h, nc, CHUNK, d)
        tp = jnp.pad(tc, ((0, 0), (0, 0), (LOOKBACK, 0), (0, 0), (0, 0)))
        return jnp.concatenate([tp[:, :, w:w + nc] for w in range(LOOKBACK + 1)], axis=3)

    kb, vb = band(k), band(v)
    bias = rel_bias.astype(jnp.float32)[:, rel_bias_index()]
    z = jnp.einsum('bhnqd,bhnkd->bhnqk', qc, kb,
                   preferred_element_type=jnp.float32) * scale + bias[None, :, None]
    slot_chunk = jnp.arange(BAND, dtype=jnp.int32) // CHUNK
    chunk_id = jnp.arange(nc, dtype=jnp.int32)
    valid = (chunk_id[:, None] + slot_chunk[None, :] - LOOKBACK) >= 0
    z = jnp.where(valid[None, None, :, None, :], z, NEG_INF)
    prob = jax.nn.softmax(z, axis=-1)
    o = jnp.einsum('bhnqk,bhnkd->bhnqd', prob.astype(vb.dtype), vb)
    return o.reshape(b, h, s, d)

def first_inputs(seed: int = 0) -> dict:
    key = jax.random.key(seed)
    ks = jax.random.split(key, 24)
    f32 = jnp.float32

    def w(k, shape, fan_in):
        return jax.random.normal(k, shape, f32) * (fan_in ** -0.5)

    def gain(k, n):
        return 1.0 + 0.05 * jax.random.normal(k, (DEPTH, n), f32)

    return {
        "x": jax.random.normal(ks[0], (BATCH, SEQ, D_MODEL), f32),
        "p": jax.random.normal(ks[1], (DEPTH, BATCH, SEQ, PLE_DIM), f32),
        "g_ffn1_pre": gain(ks[2], D_MODEL),
        "g_ffn1_post": gain(ks[3], D_MODEL),
        "w_ffn1_gate": w(ks[4], (DEPTH, D_MODEL, D_FF), D_MODEL),
        "w_ffn1_up": w(ks[5], (DEPTH, D_MODEL, D_FF), D_MODEL),
        "w_ffn1_down": w(ks[6], (DEPTH, D_FF, D_MODEL), D_FF),
        "g_mix_pre": gain(ks[7], D_MODEL),
        "g_mix_post": gain(ks[8], D_MODEL),
        "w_in": w(ks[9], (DEPTH, D_MODEL, 3 * MIX_WIDTH), D_MODEL),
        "g_out_sb": gain(ks[10], W_SB),
        "g_out_ch": gain(ks[11], W_CH),
        "rel_bias": 0.02 * jax.random.normal(ks[12], (DEPTH, H_CH, 2 * REL_CLIP + 1), f32),
        "w_out": w(ks[13], (DEPTH, MIX_WIDTH, D_MODEL), MIX_WIDTH),
        "g_ffn2_pre": gain(ks[14], D_MODEL),
        "g_ffn2_post": gain(ks[15], D_MODEL),
        "w_ffn2_gate": w(ks[16], (DEPTH, D_MODEL, D_FF), D_MODEL),
        "w_ffn2_up": w(ks[17], (DEPTH, D_MODEL, D_FF), D_MODEL),
        "w_ffn2_down": w(ks[18], (DEPTH, D_FF, D_MODEL), D_FF),
        "w_ple_proj": w(ks[19], (DEPTH, PLE_DIM, D_MODEL), PLE_DIM),
        "w_ple_gate": w(ks[20], (DEPTH, D_MODEL, D_MODEL), D_MODEL),
        "g_ple_post": gain(ks[21], D_MODEL),
    }

def first_block(x, p, g_ffn1_pre, g_ffn1_post, w_ffn1_gate, w_ffn1_up, w_ffn1_down,
              g_mix_pre, g_mix_post, w_in, g_out_sb, g_out_ch, rel_bias, w_out,
              g_ffn2_pre, g_ffn2_post, w_ffn2_gate, w_ffn2_up, w_ffn2_down,
              w_ple_proj, w_ple_gate, g_ple_post):
    h = x
    for i in range(DEPTH):
        f = swiglu(rms_norm(h, g_ffn1_pre[i]), w_ffn1_gate[i], w_ffn1_up[i], w_ffn1_down[i])
        h = h + 0.5 * rms_norm(f, g_ffn1_post[i])

        u = rms_norm(h, g_mix_pre[i])
        qkv = u @ w_in[i]
        q_a, k_a, v_a, q_b, k_b, v_b = jnp.split(
            qkv, np.cumsum([W_SB, W_SB, W_SB, W_CH, W_CH])[:5].tolist(), axis=-1)
        o_a = stick_breaking_attention(split_heads(q_a, H_SB), split_heads(k_a, H_SB),
                                       split_heads(v_a, H_SB))
        o_b = chunk_band_attention(split_heads(q_b, H_CH), split_heads(k_b, H_CH),
                                   split_heads(v_b, H_CH), rel_bias[i])
        mixed = jnp.concatenate([rms_norm(merge_heads(o_a), g_out_sb[i]),
                                 rms_norm(merge_heads(o_b), g_out_ch[i])], axis=-1)
        h = h + rms_norm(mixed @ w_out[i], g_mix_post[i])

        f = swiglu(rms_norm(h, g_ffn2_pre[i]), w_ffn2_gate[i], w_ffn2_up[i], w_ffn2_down[i])
        h = h + 0.5 * rms_norm(f, g_ffn2_post[i])

        e = (p[i] @ w_ple_proj[i]) * jax.nn.sigmoid(h @ w_ple_gate[i])
        h = h + rms_norm(e, g_ple_post[i])
    return h


DEPTH_2 = 4

N_MIXERS = 4
CONV_WIDTH = 1024
CONV_K = 3
FOX_HEADS = 8
FOX_HEAD_DIM = 128
FOX_WIDTH = FOX_HEADS * FOX_HEAD_DIM
GDN_HEADS = 8
GDN_HEAD_DIM = 128
GDN_WIDTH = GDN_HEADS * GDN_HEAD_DIM
GDN_CONV_K = 4
GDN_CHUNK = 64
SWA_HEADS = 16
SWA_KV_HEADS = 4
SWA_GROUP = SWA_HEADS // SWA_KV_HEADS
SWA_HEAD_DIM = 64
SWA_WIDTH = SWA_HEADS * SWA_HEAD_DIM
SWA_KV_WIDTH = SWA_KV_HEADS * SWA_HEAD_DIM
WINDOW = 128
ROPE_THETA = 10000.0

N_CONV_LAYERS = (DEPTH_2 + 3) // 4
N_FOX_LAYERS = (DEPTH_2 + 2) // 4
N_GDN_LAYERS = (DEPTH_2 + 1) // 4
N_SWA_LAYERS = DEPTH_2 // 4


def rms_norm_2(x, w):
    x32 = x.astype(jnp.float32)
    y = x32 * lax.rsqrt(jnp.mean(x32 * x32, axis=-1, keepdims=True) + EPS)
    return (y * w.astype(jnp.float32)).astype(x.dtype)

def causal_conv(u, w):
    K = w.shape[0]
    S = u.shape[1]
    up = jnp.pad(u, ((0, 0), (K - 1, 0), (0, 0)))
    out = up[:, 0:S] * w[0]
    for k in range(1, K):
        out = out + up[:, k:k + S] * w[k]
    return out

def rope(x, positions):
    d = x.shape[-1]
    half = d // 2
    inv_freq = ROPE_THETA ** (-jnp.arange(half, dtype=jnp.float32) / half)
    ang = positions.astype(jnp.float32)[..., None] * inv_freq
    cos = jnp.cos(ang)[:, :, None, :]
    sin = jnp.sin(ang)[:, :, None, :]
    x32 = x.astype(jnp.float32)
    x1, x2 = x32[..., :half], x32[..., half:]
    return jnp.concatenate([x1 * cos - x2 * sin, x2 * cos + x1 * sin], axis=-1).astype(x.dtype)

def conv_mixer(h, w_in, w_conv, w_out):
    proj = h @ w_in
    b_gate, c_gate, v, z = jnp.split(proj, 4, axis=-1)
    y = b_gate * causal_conv(c_gate * v, w_conv)
    return (y * jax.nn.silu(z)) @ w_out

def fox_mixer(h, w_in, b_f, w_out):
    B_, S, _ = h.shape
    H, d = FOX_HEADS, FOX_HEAD_DIM
    proj = h @ w_in
    q, k, v, z, f_logit = jnp.split(proj, [FOX_WIDTH, 2 * FOX_WIDTH, 3 * FOX_WIDTH, 4 * FOX_WIDTH], axis=-1)
    q = q.reshape(B_, S, H, d)
    k = k.reshape(B_, S, H, d)
    v = v.reshape(B_, S, H, d)
    log_f = jax.nn.log_sigmoid((f_logit + b_f).astype(jnp.float32))
    c = jnp.cumsum(log_f, axis=1)
    c_keys = c.transpose(0, 2, 1)
    nblk = S // Q_BLOCK
    q_blocks = q.reshape(B_, nblk, Q_BLOCK, H, d).transpose(1, 0, 2, 3, 4)
    c_blocks = c.reshape(B_, nblk, Q_BLOCK, H).transpose(1, 0, 3, 2)
    scale = 1.0 / math.sqrt(d)
    k_pos = jnp.arange(S)

    def block(args):
        i, q_i, c_i = args
        s = jnp.einsum('bqhd,bkhd->bhqk', q_i, k).astype(jnp.float32) * scale
        decay = c_i[..., :, None] - c_keys[:, :, None, :]
        q_pos = i * Q_BLOCK + jnp.arange(Q_BLOCK)
        mask = k_pos[None, :] <= q_pos[:, None]
        logits = jnp.where(mask, s + decay, -jnp.inf)
        p = jax.nn.softmax(logits, axis=-1)
        return jnp.einsum('bhqk,bkhd->bqhd', p.astype(v.dtype), v)

    o = lax.map(block, (jnp.arange(nblk), q_blocks, c_blocks))
    o = o.transpose(1, 0, 2, 3, 4).reshape(B_, S, FOX_WIDTH)
    return (o * jax.nn.silu(z)) @ w_out

def chunk_gated_delta(q, k, v, g, beta):
    B_, S, H, dk = q.shape
    dv = v.shape[-1]
    C = GDN_CHUNK
    n = S // C
    f32 = jnp.float32

    def chunks(t):
        return t.astype(f32).reshape(B_, n, C, H, -1).transpose(0, 3, 1, 2, 4)

    q, k, v = chunks(q), chunks(k), chunks(v)
    beta = beta.astype(f32).reshape(B_, n, C, H).transpose(0, 3, 1, 2)
    g_cum = jnp.cumsum(g.astype(f32).reshape(B_, n, C, H).transpose(0, 3, 1, 2), axis=-1)
    k_beta = k * beta[..., None]
    v_beta = v * beta[..., None]
    idx = jnp.arange(C)
    causal = idx[:, None] >= idx[None, :]
    strict = idx[:, None] > idx[None, :]
    diff = g_cum[..., :, None] - g_cum[..., None, :]
    decay = jnp.where(causal, jnp.exp(jnp.where(causal, diff, 0.0)), 0.0)
    L = jnp.where(strict, jnp.einsum('bhnid,bhnjd->bhnij', k_beta, k) * decay, 0.0)
    eye = jnp.eye(C, dtype=f32)
    T = lax.linalg.triangular_solve(eye + L, jnp.broadcast_to(eye, L.shape), left_side=True, lower=True, unit_diagonal=True)
    u = T @ v_beta
    w = T @ (k_beta * jnp.exp(g_cum)[..., None])
    qk = jnp.where(causal, jnp.einsum('bhnid,bhnjd->bhnij', q, k) * decay, 0.0)
    g_last = g_cum[..., -1]
    k_dec = k * jnp.exp(g_last[..., None] - g_cum)[..., None]
    q_dec = q * jnp.exp(g_cum)[..., None]

    def to_scan(t):
        return jnp.moveaxis(t, 2, 0)

    def step(state, xs):
        qd, kd, u_c, w_c, qk_c, gl = xs
        v_new = u_c - w_c @ state
        o = qd @ state + qk_c @ v_new
        state = state * jnp.exp(gl)[..., None, None] + jnp.einsum('bhck,bhcv->bhkv', kd, v_new)
        return state, o

    state0 = jnp.zeros((B_, H, dk, dv), f32)
    xs = (to_scan(q_dec), to_scan(k_dec), to_scan(u), to_scan(w), to_scan(qk), to_scan(g_last))
    _, o = lax.scan(step, state0, xs)
    return o.transpose(1, 0, 3, 2, 4).reshape(B_, S, H, dv)

def gdn_mixer(h, w_in, w_conv, a_log, dt_bias, w_onorm, w_out):
    B_, S, _ = h.shape
    H, d = GDN_HEADS, GDN_HEAD_DIM
    proj = h @ w_in
    qkv, z, beta_logit, a_logit = jnp.split(proj, [3 * GDN_WIDTH, 4 * GDN_WIDTH, 4 * GDN_WIDTH + H], axis=-1)
    qkv = jax.nn.silu(causal_conv(qkv, w_conv))
    q, k, v = jnp.split(qkv, 3, axis=-1)
    q = q.reshape(B_, S, H, d).astype(jnp.float32)
    k = k.reshape(B_, S, H, d).astype(jnp.float32)
    v = v.reshape(B_, S, H, d)
    q = q * lax.rsqrt(jnp.sum(q * q, axis=-1, keepdims=True) + EPS) * (1.0 / math.sqrt(d))
    k = k * lax.rsqrt(jnp.sum(k * k, axis=-1, keepdims=True) + EPS)
    beta = jax.nn.sigmoid(beta_logit.astype(jnp.float32))
    g = -jnp.exp(a_log.astype(jnp.float32)) * jax.nn.softplus(a_logit.astype(jnp.float32) + dt_bias.astype(jnp.float32))
    o = chunk_gated_delta(q, k, v, g, beta)
    o = o * lax.rsqrt(jnp.mean(o * o, axis=-1, keepdims=True) + EPS) * w_onorm.astype(jnp.float32)
    o = o.reshape(B_, S, GDN_WIDTH).astype(h.dtype)
    return (o * jax.nn.silu(z)) @ w_out

def swa_mixer(h, positions, w_in, sinks, w_out):
    B_, S, _ = h.shape
    Hk, G, d = SWA_KV_HEADS, SWA_GROUP, SWA_HEAD_DIM
    proj = h @ w_in
    q, k, v, z = jnp.split(proj, [SWA_WIDTH, SWA_WIDTH + SWA_KV_WIDTH, SWA_WIDTH + 2 * SWA_KV_WIDTH], axis=-1)
    q = rope(q.reshape(B_, S, SWA_HEADS, d), positions)
    k = rope(k.reshape(B_, S, Hk, d), positions)
    v = v.reshape(B_, S, Hk, d)
    W = WINDOW
    nblk = S // W
    qb = q.reshape(B_, nblk, W, Hk, G, d)

    def band(t):
        tb = t.reshape(B_, nblk, W, Hk, d)
        prev = jnp.pad(tb, ((0, 0), (1, 0), (0, 0), (0, 0), (0, 0)))[:, :-1]
        return jnp.concatenate([prev, tb], axis=2)

    kk, vv = band(k), band(v)
    s = jnp.einsum('bnqhgd,bnkhd->bnhgqk', qb, kk).astype(jnp.float32) * (1.0 / math.sqrt(d))
    q_idx = jnp.arange(W)[:, None] + W
    k_idx = jnp.arange(2 * W)[None, :]
    rel = q_idx - k_idx
    blk = jnp.arange(nblk)[:, None, None]
    mask = (rel >= 0) & (rel < WINDOW) & (blk * W + k_idx - W >= 0)
    logits = jnp.where(mask[None, :, None, None, :, :], s, -jnp.inf)
    sink = sinks.astype(jnp.float32).reshape(1, 1, Hk, G, 1, 1)
    m = jnp.maximum(jnp.max(logits, axis=-1, keepdims=True), sink)
    e = jnp.exp(logits - m)
    p = e / (jnp.sum(e, axis=-1, keepdims=True) + jnp.exp(sink - m))
    o = jnp.einsum('bnhgqk,bnkhd->bnqhgd', p.astype(vv.dtype), vv).reshape(B_, S, SWA_WIDTH)
    return (o * jax.nn.silu(z)) @ w_out

def second_inputs(seed: int = 0) -> dict:
    key = jax.random.key(seed)
    ks = jax.random.split(key, 24)
    f32 = jnp.float32
    D = D_MODEL

    def lin(k, shape):
        return jax.random.normal(k, shape, f32) * (shape[-2] ** -0.5)

    x = jax.random.normal(ks[0], (BATCH, SEQ, D), f32)
    offset = jax.random.randint(ks[1], (BATCH, 1), 0, 1024, dtype=jnp.int32)
    positions = offset + jnp.arange(SEQ, dtype=jnp.int32)[None, :]
    norm_w = 1.0 + 0.1 * jax.random.normal(ks[2], (DEPTH_2, D), f32)
    final_norm_w = 1.0 + 0.1 * jax.random.normal(ks[3], (D,), f32)
    conv_w_in = lin(ks[4], (N_CONV_LAYERS, D, 4 * CONV_WIDTH))
    conv_w_conv = jax.random.normal(ks[5], (N_CONV_LAYERS, CONV_K, CONV_WIDTH), f32) * (CONV_K ** -0.5)
    conv_w_out = lin(ks[6], (N_CONV_LAYERS, CONV_WIDTH, D))
    fox_w_in = lin(ks[7], (N_FOX_LAYERS, D, 4 * FOX_WIDTH + FOX_HEADS))
    fox_b_f = jax.random.uniform(ks[8], (N_FOX_LAYERS, FOX_HEADS), f32, 1.0, 5.0)
    fox_w_out = lin(ks[9], (N_FOX_LAYERS, FOX_WIDTH, D))
    gdn_w_in = lin(ks[10], (N_GDN_LAYERS, D, 4 * GDN_WIDTH + 2 * GDN_HEADS))
    gdn_w_conv = jax.random.normal(ks[11], (N_GDN_LAYERS, GDN_CONV_K, 3 * GDN_WIDTH), f32) * (GDN_CONV_K ** -0.5)
    gdn_a_log = jnp.log(jax.random.uniform(ks[12], (N_GDN_LAYERS, GDN_HEADS), f32, 1.0, 16.0))
    dt = jnp.exp(jax.random.uniform(ks[13], (N_GDN_LAYERS, GDN_HEADS), f32, math.log(1e-3), math.log(1e-1)))
    gdn_dt_bias = dt + jnp.log(-jnp.expm1(-dt))
    gdn_norm_w = 1.0 + 0.1 * jax.random.normal(ks[14], (N_GDN_LAYERS, GDN_HEAD_DIM), f32)
    gdn_w_out = lin(ks[15], (N_GDN_LAYERS, GDN_WIDTH, D))
    swa_w_in = lin(ks[16], (N_SWA_LAYERS, D, 2 * SWA_WIDTH + 2 * SWA_KV_WIDTH))
    swa_sinks = 0.5 * jax.random.normal(ks[17], (N_SWA_LAYERS, SWA_HEADS), f32)
    swa_w_out = lin(ks[18], (N_SWA_LAYERS, SWA_WIDTH, D))
    return {"x": x, "positions": positions, "norm_w": norm_w, "final_norm_w": final_norm_w,
            "conv_w_in": conv_w_in, "conv_w_conv": conv_w_conv, "conv_w_out": conv_w_out,
            "fox_w_in": fox_w_in, "fox_b_f": fox_b_f, "fox_w_out": fox_w_out,
            "gdn_w_in": gdn_w_in, "gdn_w_conv": gdn_w_conv, "gdn_a_log": gdn_a_log, "gdn_dt_bias": gdn_dt_bias,
            "gdn_norm_w": gdn_norm_w, "gdn_w_out": gdn_w_out,
            "swa_w_in": swa_w_in, "swa_sinks": swa_sinks, "swa_w_out": swa_w_out}

def second_block(x, positions, norm_w, final_norm_w, conv_w_in, conv_w_conv, conv_w_out,
              fox_w_in, fox_b_f, fox_w_out, gdn_w_in, gdn_w_conv, gdn_a_log, gdn_dt_bias,
              gdn_norm_w, gdn_w_out, swa_w_in, swa_sinks, swa_w_out):
    for i in range(DEPTH_2):
        h = rms_norm_2(x, norm_w[i])
        kind, j = i % N_MIXERS, i // N_MIXERS
        if kind == 0:
            y = conv_mixer(h, conv_w_in[j], conv_w_conv[j], conv_w_out[j])
        elif kind == 1:
            y = fox_mixer(h, fox_w_in[j], fox_b_f[j], fox_w_out[j])
        elif kind == 2:
            y = gdn_mixer(h, gdn_w_in[j], gdn_w_conv[j], gdn_a_log[j], gdn_dt_bias[j], gdn_norm_w[j], gdn_w_out[j])
        else:
            y = swa_mixer(h, positions, swa_w_in[j], swa_sinks[j], swa_w_out[j])
        x = x + y.astype(x.dtype)
    return rms_norm_2(x, final_norm_w)


def setup_inputs(seed=0):
    out = dict(first_inputs(seed))
    for name, value in second_inputs(seed + 1).items():
        if name != "x":
            out[name + "_2"] = value
    return out


def reference(
    x, p, g_ffn1_pre, g_ffn1_post, w_ffn1_gate, w_ffn1_up, w_ffn1_down, g_mix_pre, g_mix_post,
    w_in, g_out_sb, g_out_ch, rel_bias, w_out, g_ffn2_pre, g_ffn2_post, w_ffn2_gate, w_ffn2_up,
    w_ffn2_down, w_ple_proj, w_ple_gate, g_ple_post, positions_2, norm_w_2, final_norm_w_2,
    conv_w_in_2, conv_w_conv_2, conv_w_out_2, fox_w_in_2, fox_b_f_2, fox_w_out_2, gdn_w_in_2,
    gdn_w_conv_2, gdn_a_log_2, gdn_dt_bias_2, gdn_norm_w_2, gdn_w_out_2, swa_w_in_2,
    swa_sinks_2, swa_w_out_2,
):
    x = first_block(
        x, p, g_ffn1_pre, g_ffn1_post, w_ffn1_gate, w_ffn1_up, w_ffn1_down, g_mix_pre,
        g_mix_post, w_in, g_out_sb, g_out_ch, rel_bias, w_out, g_ffn2_pre, g_ffn2_post,
        w_ffn2_gate, w_ffn2_up, w_ffn2_down, w_ple_proj, w_ple_gate, g_ple_post,
    )
    return second_block(
        x, positions_2, norm_w_2, final_norm_w_2, conv_w_in_2, conv_w_conv_2, conv_w_out_2,
        fox_w_in_2, fox_b_f_2, fox_w_out_2, gdn_w_in_2, gdn_w_conv_2, gdn_a_log_2,
        gdn_dt_bias_2, gdn_norm_w_2, gdn_w_out_2, swa_w_in_2, swa_sinks_2, swa_w_out_2,
    )


_drawn_inputs = setup_inputs


def setup_inputs(seed=0):
    import zlib

    import numpy as np

    out = dict(_drawn_inputs(seed))
    spreads = {}
    factors = {'rel_bias': 6.57, 'g_ffn2_post': 3.311, 'swa_sinks_2': 30.22}
    for name, (base, spread) in spreads.items():
        noise = np.random.default_rng([zlib.crc32(name.encode()), seed]).standard_normal(out[name].shape)
        drawn = base * np.exp(spread * noise) if base else spread * noise
        out[name] = __import__('jax').numpy.asarray(drawn.astype(out[name].dtype))
    for name, factor in factors.items():
        out[name] = (out[name] * factor).astype(out[name].dtype)
    return out
```

```python
from contextlib import ExitStack

import numpy as np
import concourse.bass as bass
from concourse import mybir

F32 = mybir.dt.float32
F32R = mybir.dt.float32r
I32 = mybir.dt.int32
ALU = mybir.AluOpType
ACT = mybir.ActivationFunctionType
AX_X = mybir.AxisListType.X

P = 128
SEQ = 512
D = 1024
DB = D // P
TB = SEQ // P
D_FF = 2816
FB = D_FF // P
FH = FB // 2
PLE = 256
EPS = 1e-6
NEG = -1e30
REL = 128
HD = 64
H8 = 8
RAW = 4
SPLIT = 2
BAND_W = SEQ + P


def kernel_program(nc, I, out):
    top = ExitStack()
    with top:
        def sem(name):
            return top.enter_context(nc.semaphore(name))

        def sb(name, shape, dt=F32, ctx=top):
            return ctx.enter_context(nc.sbuf_tensor(name, shape, dt))

        def rows(w, kb0=0, kbn=None):
            v = w.rearrange("(k p) n -> p k n", p=P)
            return v if kbn is None else v[:, kb0:kb0 + kbn, :]

        w1g, w1u, w1d = (I[n][0] for n in ("w_ffn1_gate", "w_ffn1_up", "w_ffn1_down"))
        w2g, w2u, w2d = (I[n][0] for n in ("w_ffn2_gate", "w_ffn2_up", "w_ffn2_down"))
        conv_in, conv_out = I["conv_w_in_2"][0], I["conv_w_out_2"][0]
        fox_in, fox_out = I["fox_w_in_2"][0], I["fox_w_out_2"][0]
        gdn_in, gdn_out = I["gdn_w_in_2"][0], I["gdn_w_out_2"][0]
        swa_in, swa_out = I["swa_w_in_2"][0], I["swa_w_out_2"][0]

        def ffn_up_src(wg, wu):
            g, u = rows(wg), rows(wu)
            return lambda i, j: [(0, P, (g, u)[j % 2], i * (2 * P) + (j // 2) * P)]

        def ffn_down_src(wd):
            v = [rows(wd, 0, FH), rows(wd, FH, FH)]
            return lambda i, j: [(0, P, v[j % 2], i * (2 * P) + (j // 2) * P)]

        def plain_src(w):
            v = rows(w)
            return lambda i, j: [(0, P, v, i * (4 * P) + j * P)]

        def ple_src():
            g, q = rows(I["w_ple_gate"][0]), rows(I["w_ple_proj"][0])
            return lambda i, j: [(0, P, (g, q)[j % 2], i * (2 * P) + (j // 2) * P)]

        def conv_src():
            v = rows(conv_in)
            return lambda i, j: [(0, P, v, i * P + j * D)]

        def fox_src():
            v = rows(fox_in)

            def src(i, j):
                if isinstance(i, int) and i == 8:
                    return [(0, H8, v, 4 * D), (H8, P - H8, v, 0)]
                return [(0, P, v, i * (4 * P) + j * P)]
            return src

        def gdn_src():
            v = rows(gdn_in)

            def src(i, j):
                if isinstance(i, int) and i == 8:
                    return [(0, H8, v, 4 * D), (H8, 32 - H8, v, 0), (32, H8, v, 4 * D + H8), (32 + H8, P - 32 - H8, v, 0)]
                return [(0, P, v, i * (4 * P) + j * P)]
            return src

        def swa_cols(b):
            kvp, m = b // 4, b % 4
            return (8 * kvp + m) * HD, (8 * kvp + 4 + m) * HD

        def swa_src():
            v = rows(swa_in)

            def src(i, j):
                k = 4 * i + j
                if k < 8:
                    a, b = swa_cols(k)
                    return [(0, HD, v, a), (HD, HD, v, b)]
                if k < 12:
                    return [(0, P, v, D + (k - 8) * P)]
                a, b = swa_cols(k - 12)
                return [(0, HD, v, D + 512 + a), (HD, HD, v, D + 512 + b)]
            return src

        stages = [
            ("ffn1_up", 2 * FB, DB, ffn_up_src(w1g, w1u)),
            ("ffn1_down", 2 * DB, FH, ffn_down_src(w1d)),
            ("mix_in", 24, DB, plain_src(I["w_in"][0])),
            ("mix_out", DB, DB, plain_src(I["w_out"][0])),
            ("ffn2_up", 2 * FB, DB, ffn_up_src(w2g, w2u)),
            ("ffn2_down", 2 * DB, FH, ffn_down_src(w2d)),
            ("ple", 2 * DB, DB, ple_src()),
            ("conv_in", 4 * DB, DB, conv_src()),
            ("conv_out", DB, DB, plain_src(conv_out)),
            ("fox_in", 4 * DB + 1, DB, fox_src()),
            ("fox_out", DB, DB, plain_src(fox_out)),
            ("gdn_in", 4 * DB + 1, DB, gdn_src()),
            ("gdn_out", DB, DB, plain_src(gdn_out)),
            ("swa_in", 20, DB, swa_src()),
            ("swa_out", DB, DB, plain_src(swa_out)),
        ]
        swa_out_halves = swa_out.rearrange("(h d) n -> d h n", d=HD)

        sources = {s[0]: s[3] for s in stages}
        tile_stage, first = [], {}
        loaded_at, slot_count = [], [0] * RAW
        for name, n, kb, src in stages:
            first[name] = len(tile_stage)
            for k in range(n):
                slot = len(tile_stage) % RAW
                n_dma = 4 if name == "swa_out" else len(src(k // 4, k % 4))
                slot_count[slot] += 16 * n_dma
                loaded_at.append(slot_count[slot])
                tile_stage.append((name, k, kb if not (name == "ple" and k % 2) else PLE // P))
        n_tiles = len(tile_stage)
        tiles_of = {s[0]: s[1] for s in stages}

        h = sb("h", [P, DB, SEQ])
        xh = sb("xh", [P, DB, SEQ], F32R)
        xl = sb("xl", [P, DB, SEQ], F32R)
        F = sb("F", [P, DB, SEQ])
        raw = [sb(f"raw{s}", [P, FH, P]) for s in range(RAW)]
        wh = [sb(f"wh{s}", [P, FH, P], F32R) for s in range(SPLIT)]
        wl = [sb(f"wl{s}", [P, FH, P], F32R) for s in range(SPLIT)]
        acc = sb("acc", [P, SEQ])
        sq = sb("sq", [P, 2, SEQ])
        ms = sb("ms", [P, SEQ])
        rstd = sb("rstd", [P, SEQ])
        ident = sb("ident", [P, P])
        ones = sb("ones", [P, P])
        vA = sb("vA", [P, P])
        vB = sb("vB", [P, 97])
        half = sb("half", [P, 2, DB])
        ps = [top.enter_context(nc.psum_tensor(f"ps{b}", [P, SEQ], F32)) for b in range(8)]
        STAT = 7

        loaded = [sem(f"loaded{s}") for s in range(RAW)]
        hi_done, lo_done, tile_done = sem("hi_done"), sem("lo_done"), sem("tile_done")

        def wait(eng, s, v):
            if not isinstance(v, int) or v > 0:
                eng.wait_ge(s, v)

        def load(sp, name, i, j, k_ahead=0, split_at=None):
            t0 = first[name]
            if isinstance(i, int):
                t = t0 + 4 * i + j + k_ahead
                if t >= n_tiles:
                    return
                name, k, kb = tile_stage[t]
                i, j = k // 4, k % 4
                slot = t % RAW
            else:
                j += k_ahead
                slot, kb = (t0 + j) % RAW, tile_stage[t0 + j][2]
                i, j = i + j // 4, j % 4
            if name == "swa_out":
                if split_at is not None:
                    sp.wait_ge(lo_done, split_at)
                n0 = (4 * i + j) * P
                for kvp in range(2):
                    for upper in range(2):
                        h0 = 8 * kvp + 4 * upper
                        sp.dma_start(raw[slot][upper * HD:upper * HD + HD, 4 * kvp:4 * kvp + 4, :],
                                     swa_out_halves[:, h0:h0 + 4, n0:n0 + P]).then_inc(loaded[slot], 16)
                return
            parts = [(c0, w, view, c if isinstance(c, int) else sp.snap(c)) for c0, w, view, c in sources[name](i, j)]
            if split_at is not None:
                sp.wait_ge(lo_done, split_at)
            for c0, w, view, c in parts:
                sp.dma_start(raw[slot][:, 0:kb, c0:c0 + w], view[:, :, bass.ds(c, w)]).then_inc(loaded[slot], 16)

        def tile_at(name, i, j, ahead):
            t0 = first[name]
            if isinstance(i, int):
                t = t0 + 4 * i + j + ahead
                if t >= n_tiles:
                    return None
                return t % RAW, t % SPLIT, tile_stage[t][2], t, loaded_at[t]
            s = t0 + j + ahead
            return s % RAW, s % SPLIT, tile_stage[s][2], i * 4 + s, i * 16 + loaded_at[s]

        def split_hi(act, name, i, j, ahead=2):
            at = tile_at(name, i, j, ahead)
            if at is None:
                return
            r, s, kb, t, got = at
            act.wait_ge(loaded[r], got)
            wait(act, tile_done, t - SPLIT + 1)
            nc.scalar.activation(wh[s][:, 0:kb, :], raw[r][:, 0:kb, :], ACT.Copy).then_inc(hi_done, 1)

        def split_lo(dve, name, i, j, ahead=2):
            at = tile_at(name, i, j, ahead)
            if at is None:
                return
            r, s, kb, t, got = at
            dve.wait_ge(loaded[r], got)
            dve.wait_ge(hi_done, t + 1)
            nc.vector.tensor_tensor(wl[s][:, 0:kb, :], raw[r][:, 0:kb, :], wh[s][:, 0:kb, :].bitcast(F32),
                                    ALU.subtract).then_inc(lo_done, 1)

        def load_steps(sp, name):
            def body(i, j):
                load(sp, name, i, j, RAW, i * 4 + (first[name] + j + 1))
            steps(sp, name, body)

        def steps(eng, name, body, loop_end=None):
            n = tiles_of[name]
            full = n // 4
            if full < 4 or name == "swa_in":
                for k in range(n):
                    body(k // 4, k % 4)
                return
            for j in range(4):
                body(0, j)
            end = full - 1 if loop_end is None else loop_end
            with eng.Fori(1, end) as i:
                for j in range(4):
                    body(i, j)
            for k in range(4 * end, n):
                body(k // 4, k % 4)

        def mm3(pe, o, s, kb, x_hi, x_lo, start, stop):
            pe.matmul(o, wh[s][:, kb, :], x_hi, start=start, stop=False)
            pe.matmul(o, wh[s][:, kb, :], x_lo, start=False, stop=False)
            return pe.matmul(o, wl[s][:, kb, :], x_hi, start=False, stop=stop)

        xs_hi, xs_lo = sem("x_hi_done"), sem("x_lo_done")
        h_new = sem("h_new")
        f_scaled = sem("f_scaled")
        sq_done, acc_done = sem("sq_done"), sem("acc_done")
        stat_mm, ms_done, inv_done, rstd_done = sem("stat_mm"), sem("ms_done"), sem("inv_done"), sem("rstd_done")
        evac = sem("psum_evacuated")
        n = dict(x=0, h=0, fs=0, sq=0, acc=0, stat=0, ev=0, units=0, groups=0)

        def rstd_pe(pe, acc_at):
            pe.wait_ge(acc_done, acc_at)
            pe.matmul(ps[STAT][:, :], ones[:, :], acc[:, :], start=True, stop=True).then_inc(stat_mm, 1)

        def rstd_dve(dve, at, width):
            dve.wait_ge(stat_mm, at + 1)
            nc.vector.tensor_scalar(ms[:, :], ps[STAT][:, :], 1.0 / width, EPS, ALU.mult, ALU.add).then_inc(ms_done, 1)
            dve.wait_ge(ms_done, at + 1)
            nc.vector.reciprocal(ms[:, :], ms[:, :]).then_inc(inv_done, 1)

        def rstd_act(act, at):
            act.wait_ge(inv_done, at + 1)
            nc.scalar.activation(rstd[:, :], ms[:, :], ACT.Sqrt).then_inc(rstd_done, 1)

        class Prologue:

            def __init__(self, gain=None, update=None, squares=True):
                self.gain, self.update, self.squares = gain, update, squares
                self.x0, self.h0, self.fs0 = n["x"], n["h"], n["fs"]
                self.sq0, self.acc0, self.stat0 = n["sq"], n["acc"], n["stat"]
                n["x"] += DB
                if update is not None:
                    n["h"] += DB
                    n["fs"] += DB
                if squares:
                    n["sq"] += DB
                    n["acc"] += DB

            def act(self, act):
                for b in range(DB):
                    if self.update is not None:
                        act.wait_ge(h_new, self.h0 + b + 1)
                    g = 1.0 if self.gain is None else self.gain[:, b:b + 1]
                    nc.scalar.activation(xh[:, b, :], h[:, b, :], ACT.Copy, scale=g).then_inc(xs_hi, 1)
                if self.squares:
                    for b in range(DB):
                        if b >= 2:
                            act.wait_ge(acc_done, self.acc0 + b - 1)
                        nc.scalar.activation(sq[:, b % 2, :], h[:, b, :], ACT.Square).then_inc(sq_done, 1)

            def dve(self, dve):
                for b in range(DB):
                    if self.update is not None:
                        nc.vector.tensor_tensor(F[:, b, :], F[:, b, :], rstd[:, :], ALU.mult).then_inc(f_scaled, 1)
                        dve.wait_ge(f_scaled, self.fs0 + b + 1)
                        nc.vector.scalar_tensor_tensor(out=h[:, b, :], in0=F[:, b, :], scalar=self.update[:, b:b + 1],
                                                       in1=h[:, b, :], op0=ALU.mult, op1=ALU.add).then_inc(h_new, 1)
                        if b == 0:
                            continue
                        self.low(dve, b - 1)
                    else:
                        self.low(dve, b)
                if self.update is not None:
                    self.low(dve, DB - 1)

            def low(self, dve, b):
                dve.wait_ge(xs_hi, self.x0 + b + 1)
                if self.gain is None:
                    nc.vector.tensor_tensor(xl[:, b, :], h[:, b, :], xh[:, b, :].bitcast(F32),
                                            ALU.subtract).then_inc(xs_lo, 1)
                else:
                    nc.vector.scalar_tensor_tensor(out=xl[:, b, :], in0=h[:, b, :], scalar=self.gain[:, b:b + 1],
                                                   in1=xh[:, b, :].bitcast(F32), op0=ALU.mult,
                                                   op1=ALU.subtract).then_inc(xs_lo, 1)

            def pool(self, pool):
                if self.squares:
                    sum_squares(pool, self.sq0, self.acc0)

        def sum_squares(pool, sq0, acc0, m=DB):
            for b in range(m):
                pool.wait_ge(sq_done, sq0 + b + 1)
                if b == 0:
                    nc.gpsimd.tensor_copy(acc[:, :], sq[:, 0, :]).then_inc(acc_done, 1)
                else:
                    pool.wait_ge(acc_done, acc0 + b)
                    nc.gpsimd.tensor_tensor(acc[:, :], acc[:, :], sq[:, b % 2, :], ALU.add).then_inc(acc_done, 1)

        def pe_tiles(pe, name, x_hi, x_lo, ev0, pro=None, parts=1, stat_after=None, y_at=None, kb0=0):
            banks = 4 // parts

            def body(i, j):
                r, s, kb, t, got = tile_at(name, i, j, 0)
                part = j % parts
                bank = (j // parts) % banks
                o = i * banks + j // parts
                pe.wait_ge(lo_done, t + 1)
                if part == 0:
                    wait(pe, evac, ev0 + o - banks + 1)
                head = isinstance(i, int) and i == 0 and j < 1
                for b in range(kb):
                    if head and pro is not None:
                        pe.wait_ge(xs_lo, pro.x0 + b + 1)
                    if head and y_at is not None:
                        pe.wait_ge(y_at[0], y_at[1] + b + 1)
                    xb = part * FH + b if parts == 2 else b
                    last = mm3(pe, ps[bank][:, :], s, b, x_hi[:, xb, :], x_lo[:, xb, :],
                               part == 0 and b == 0, part == parts - 1 and b == kb - 1)
                last.then_inc(tile_done, 1)
                if stat_after and isinstance(i, int) and 4 * i + j == stat_after[0]:
                    rstd_pe(pe, stat_after[1])
            steps(pe, name, body)

        def in_proj(name, gain, dst, update=None, acc_at=None, scale_dve=None, tails=(), evac_dve=None, evac_act=None,
                    loop_end=None, copy_steps=None):
            pro = Prologue(gain, update, squares=acc_at is None)
            st = n["stat"]
            n["stat"] += 1
            ev0 = n["ev"]
            n["ev"] += tiles_of[name]
            t0 = first[name]
            tails = dict(tails)
            with nc.Block() as block:
                @block.sync
                def _(sp):
                    if "sp" in tails:
                        tails["sp"](sp)
                    load_steps(sp, name)

                @block.gpsimd
                def _(pool):
                    pro.pool(pool)
                    if "pool" in tails:
                        tails["pool"](pool)

                @block.scalar
                def _(act):
                    if acc_at is not None:
                        rstd_act(act, st)
                    pro.act(act)

                    def body(i, j):
                        split_hi(act, name, i, j)
                        if acc_at is None and isinstance(i, int) and i == 0 and j == 0:
                            rstd_act(act, st)
                        if evac_act is not None:
                            evac_act(act, i, j, ev0)
                    steps(act, name, body, loop_end)
                    if "act" in tails:
                        tails["act"](act, ev0)

                @block.vector
                def _(dve):
                    if acc_at is not None:
                        rstd_dve(dve, st, D)
                    pro.dve(dve)

                    def body(i, j):
                        split_lo(dve, name, i, j)
                        if isinstance(i, int) and i == 0 and j == 0:
                            if acc_at is None:
                                rstd_dve(dve, st, D)
                            dve.wait_ge(rstd_done, st + 1)
                        dve.wait_ge(tile_done, i * 4 + (t0 + j + 1))
                        if evac_dve is not None:
                            evac_dve(dve, i, j, ev0)
                        else:
                            k = i * 4 + j
                            nc.vector.tensor_tensor(dst[:, bass.ds(k, 1), :],
                                                    ps[j][:, :].rearrange("p (o q) -> p o q", o=1),
                                                    rstd[:, :].rearrange("p (o q) -> p o q", o=1), ALU.mult).then_inc(evac, 1)
                    steps(dve, name, body, loop_end)
                    if "dve" in tails:
                        tails["dve"](dve, ev0)

                @block.tensor
                def _(pe):
                    if acc_at is not None:
                        rstd_pe(pe, acc_at)
                    pe_tiles(pe, name, xh, xl, ev0, pro=pro,
                             stat_after=None if acc_at is not None else (1, pro.acc0 + DB))
                    if "pe" in tails:
                        tails["pe"](pe, ev0)
            return ev0

        vec_rows = []
        for nm in ("g_ffn1_pre", "g_ffn1_post", "g_mix_pre", "g_mix_post", "g_ffn2_pre", "g_ffn2_post", "g_ple_post",
                   "g_out_sb", "g_out_ch", "norm_w_2", "final_norm_w_2", "conv_w_conv_2"):
            a = I[nm]
            if len(a.shape) == 1:
                v = a.rearrange("(r c) -> r c", c=P)
            elif len(a.shape) == 2:
                v = a.rearrange("a (r c) -> (a r) c", c=P)
            else:
                v = a.rearrange("a k (r c) -> (a k r) c", c=P)
            vec_rows.append((nm, v))
        col = {}
        at = 0
        for nm, v in vec_rows:
            col[nm] = at
            at += v.shape[0]
        assert at == P
        gdn_conv_rows = I["gdn_w_conv_2"].rearrange("a k (r c) -> (a k r) c", c=P)

        def gains(nm, first_=0, m=DB):
            return vA[:, col[nm] + first_:col[nm] + first_ + m]

        boot = ExitStack()
        with boot:
            xt = sb("xt", [P, TB, D], ctx=boot)
            vrow = sb("vrow", [P, 2, P], ctx=boot)
            vec_in, x_in = sem("vec_in"), sem("x_in")
            const = sem("const_ready")
            tr, tr_out, half_done = sem("boot_transposed"), sem("boot_copied"), sem("half_done")
            n_vec = 16 * (len(vec_rows) + 2)
            with nc.Block() as block:
                @block.sync
                def _(sp):
                    sp.dma_start(xt[:, :, :], I["x"][0].rearrange("(t p) d -> p t d", p=P)).then_inc(x_in, 16)
                    for nm, v in vec_rows:
                        sp.dma_start(vrow[col[nm]:col[nm] + v.shape[0], 0, :], v).then_inc(vec_in, 16)
                    sp.dma_start(vrow[0:96, 1, :], gdn_conv_rows).then_inc(vec_in, 16)
                    sp.dma_start(vrow[96:97, 1, :], I["gdn_norm_w_2"]).then_inc(vec_in, 16)
                    for k in range(RAW):
                        load(sp, "ffn1_up", 0, k)

                @block.gpsimd
                def _(pool):
                    nc.gpsimd.memset(ones[:, :], 1.0).then_inc(const, 1)
                    nc.gpsimd.memset(ident[:, :], 0.0).then_inc(const, 1)
                    pool.wait_ge(const, 2)
                    nc.gpsimd.affine_select(out=ident[:, :], in_=ident[:, :], compare_op=ALU.not_equal, fill=1.0,
                                            base=0, pattern=[[-1, P]], channel_multiplier=1).then_inc(const, 1)

                @block.tensor
                def _(pe):
                    pe.wait_ge(const, 3)
                    pe.wait_ge(x_in, 16)
                    for b in range(DB):
                        if b >= 4:
                            pe.wait_ge(tr_out, b - 3)
                        for t in range(TB):
                            m = pe.transpose(ps[b % 4][:, t * P:t * P + P], xt[:, t, b * P:b * P + P], ident[:, :])
                        m.then_inc(tr, 1)
                    pe.wait_ge(vec_in, n_vec)
                    pe.transpose(ps[4][:, 0:P], vrow[:, 0, :], ident[:, :]).then_inc(tr, 1)
                    pe.transpose(ps[5][:, 0:97], vrow[0:97, 1, :], ident[0:97, 0:97]).then_inc(tr, 1)

                @block.vector
                def _(dve):
                    for b in range(DB):
                        dve.wait_ge(tr, b + 1)
                        nc.vector.tensor_copy(h[:, b, :], ps[b % 4][:, :]).then_inc(tr_out, 1)
                    dve.wait_ge(tr, DB + 1)
                    nc.vector.tensor_copy(vA[:, :], ps[4][:, 0:P]).then_inc(tr_out, 1)
                    dve.wait_ge(tr, DB + 2)
                    nc.vector.tensor_copy(vB[:, :], ps[5][:, 0:97]).then_inc(tr_out, 1)
                    dve.wait_ge(tr_out, DB + 1)
                    nc.vector.tensor_scalar(half[:, 0, :], gains("g_ffn1_post"), 0.5, None, ALU.mult).then_inc(half_done, 1)
                    nc.vector.tensor_scalar(half[:, 1, :], gains("g_ffn2_post"), 0.5, None, ALU.mult).then_inc(half_done, 1)
                    for k in range(2):
                        split_lo(dve, "ffn1_up", 0, k, 0)

                @block.scalar
                def _(act):
                    for k in range(2):
                        split_hi(act, "ffn1_up", 0, k, 0)

        def ffn_up(name, gain, update, act_hi, act_lo, ctx):
            S = F[:, 0:2, :]
            SR = F[:, 2:4, :]
            g_done, silu_done, sr_done, prod, a_hi = (sem(f"{name}_{x}") for x in ("gate", "silu", "silur", "prod", "ahi"))
            pro = Prologue(gain, update)
            st = n["stat"]
            n["stat"] += 1
            ev0 = n["ev"]
            n["ev"] += 2 * FB
            t0 = first[name]
            with nc.Block() as block:
                @block.sync
                def _(sp):
                    load_steps(sp, name)

                @block.gpsimd
                def _(pool):
                    pro.pool(pool)

                    def body(i, j):
                        if j % 2 == 1:
                            p, s = i * 2 + j // 2, (j // 2) % 2
                            pool.wait_ge(silu_done, p + 1)
                            wait(pool, prod, p - 1)
                            nc.gpsimd.tensor_tensor(SR[:, s, :], S[:, s, :], rstd[:, :], ALU.mult).then_inc(sr_done, 1)
                    steps(pool, name, body)

                @block.scalar
                def _(act):
                    pro.act(act)

                    def body(i, j):
                        split_hi(act, name, i, j)
                        if isinstance(i, int) and i == 0 and j == 0:
                            rstd_act(act, st)
                        p, s = i * 2 + j // 2, (j // 2) % 2
                        if j % 2 == 0:
                            act.wait_ge(g_done, p + 1)
                            wait(act, sr_done, p - 1)
                            nc.scalar.activation(S[:, s, :], ps[j][:, :], ACT.Silu).then_inc(silu_done, 1)
                        else:
                            act.wait_ge(prod, p + 1)
                            nc.scalar.activation(act_hi[:, bass.ds(p, 1), :], ps[j][:, :].rearrange("p (o q) -> p o q", o=1),
                                                 ACT.Copy).then_inc(a_hi, 1)
                    steps(act, name, body)

                @block.vector
                def _(dve):
                    pro.dve(dve)

                    def body(i, j):
                        split_lo(dve, name, i, j)
                        if isinstance(i, int) and i == 0 and j == 0:
                            rstd_dve(dve, st, D)
                            dve.wait_ge(rstd_done, st + 1)
                        p, s = i * 2 + j // 2, (j // 2) % 2
                        dve.wait_ge(tile_done, i * 4 + (t0 + j + 1))
                        if j % 2 == 0:
                            nc.vector.tensor_tensor(ps[j][:, :], ps[j][:, :], rstd[:, :], ALU.mult).then_inc(g_done, 1)
                        else:
                            dve.wait_ge(sr_done, p + 1)
                            nc.vector.tensor_tensor(ps[j][:, :], ps[j][:, :], SR[:, s, :], ALU.mult).then_inc(prod, 1)
                            dve.wait_ge(a_hi, p + 1)
                            nc.vector.tensor_tensor(act_lo[:, bass.ds(p, 1), :], ps[j][:, :].rearrange("p (o q) -> p o q", o=1),
                                                    act_hi[:, bass.ds(p, 1), :].bitcast(F32), ALU.subtract).then_inc(evac, 2)
                    steps(dve, name, body)

                @block.tensor
                def _(pe):
                    pe_tiles(pe, name, xh, xl, ev0, pro=pro, stat_after=(1, pro.acc0 + DB))

        def post_out(name, x_hi, x_lo, parts):
            ev0, sq0, acc0, st = n["ev"], n["sq"], n["acc"], n["stat"]
            n["ev"] += DB
            n["sq"] += DB
            n["acc"] += DB
            n["stat"] += 1
            t0 = first[name]
            with nc.Block() as block:
                @block.sync
                def _(sp):
                    load_steps(sp, name)

                @block.gpsimd
                def _(pool):
                    sum_squares(pool, sq0, acc0)

                @block.scalar
                def _(act):
                    def body(i, j):
                        split_hi(act, name, i, j)
                        if j % parts == parts - 1:
                            o, bank = i * (4 // parts) + j // parts, j // parts
                            act.wait_ge(tile_done, i * 4 + (t0 + j + 1))
                            wait(act, acc_done, acc0 + o - 1 if not (isinstance(o, int) and o < 2) else 0)
                            nc.scalar.activation(sq[:, bank % 2, :], ps[bank][:, :], ACT.Square).then_inc(sq_done, 1)
                            nc.scalar.activation(F[:, o:o + 1, :] if isinstance(o, int) else F[:, bass.ds(o, 1), :],
                                                 ps[bank][:, :].rearrange("p (o q) -> p o q", o=1), ACT.Copy).then_inc(evac, 1)
                    steps(act, name, body)
                    rstd_act(act, st)

                @block.vector
                def _(dve):
                    def body(i, j):
                        split_lo(dve, name, i, j)
                    steps(dve, name, body)
                    rstd_dve(dve, st, D)

                @block.tensor
                def _(pe):
                    pe_tiles(pe, name, x_hi, x_lo, ev0, parts=parts)
                    rstd_pe(pe, acc0 + DB)

        def resid_out(name):
            ev0, sq0, acc0 = n["ev"], n["sq"], n["acc"]
            n["ev"] += DB
            n["sq"] += DB
            n["acc"] += DB
            t0 = first[name]
            with nc.Block() as block:
                @block.sync
                def _(sp):
                    load_steps(sp, name)

                @block.gpsimd
                def _(pool):
                    sum_squares(pool, sq0, acc0)

                @block.scalar
                def _(act):
                    def body(i, j):
                        k = 4 * i + j
                        split_hi(act, name, i, j)
                        act.wait_ge(evac, ev0 + k + 1)
                        wait(act, acc_done, acc0 + k - 1 if k >= 2 else 0)
                        nc.scalar.activation(sq[:, k % 2, :], h[:, k, :], ACT.Square).then_inc(sq_done, 1)
                    steps(act, name, body)

                @block.vector
                def _(dve):
                    def body(i, j):
                        k = 4 * i + j
                        split_lo(dve, name, i, j)
                        dve.wait_ge(tile_done, t0 + k + 1)
                        nc.vector.tensor_tensor(h[:, k, :], ps[j][:, :], h[:, k, :], ALU.add).then_inc(evac, 1)
                    steps(dve, name, body)

                @block.tensor
                def _(pe):
                    pe_tiles(pe, name, xh, xl, ev0)
            return acc0 + DB

        def final(acc_at):
            ot = ExitStack()
            with ot:
                fo = sb("final_o", [P, DB, SEQ], ctx=ot)
                res = sb("final_res", [P, TB, D], ctx=ot)
                fr, fs, ft, fe, stored = (sem(f"final_{x}") for x in ("scaled", "gained", "transposed", "copied", "stored"))
                st = n["stat"]
                n["stat"] += 1
                g = gains("final_norm_w_2")
                with nc.Block() as block:
                    @block.tensor
                    def _(pe):
                        rstd_pe(pe, acc_at)
                        for t in range(TB):
                            for b in range(2):
                                q = 2 * t + b
                                if q >= 4:
                                    pe.wait_ge(fe, q - 3)
                                for c in range(4):
                                    if t == 0:
                                        pe.wait_ge(fs, 4 * b + c + 1)
                                    m = pe.transpose(ps[q % 4][:, c * P:c * P + P],
                                                     fo[:, 4 * b + c, t * P:t * P + P], ident[:, :])
                                m.then_inc(ft, 1)

                    @block.vector
                    def _(dve):
                        rstd_dve(dve, st, D)
                        dve.wait_ge(rstd_done, st + 1)
                        for b in range(DB):
                            nc.vector.tensor_tensor(fo[:, b, :], h[:, b, :], rstd[:, :], ALU.mult).then_inc(fr, 1)
                        for q in range(2 * TB):
                            dve.wait_ge(ft, q + 1)
                            nc.vector.tensor_copy(res[:, q // 2, (q % 2) * SEQ:(q % 2) * SEQ + SEQ], ps[q % 4][:, :]).then_inc(fe, 1)

                    @block.scalar
                    def _(act):
                        rstd_act(act, st)
                        for b in range(DB):
                            act.wait_ge(fr, b + 1)
                            nc.scalar.activation(fo[:, b, :], fo[:, b, :], ACT.Copy,
                                                 scale=g[:, b:b + 1]).then_inc(fs, 1)

                    @block.sync
                    def _(sp):
                        for t in range(TB):
                            sp.wait_ge(fe, 2 * t + 2)
                            sp.dma_start(out[0, t * P:t * P + P, :], res[:, t, :]).then_inc(stored, 16)
                        sp.wait_ge(stored, 16 * TB)

        with ExitStack() as c:
            a_hi = sb("a_hi1", [P, FB, SEQ], F32R, ctx=c)
            a_lo = sb("a_lo1", [P, FB, SEQ], F32R, ctx=c)
            with ExitStack() as c2:
                ffn_up("ffn1_up", gains("g_ffn1_pre"), None, a_hi, a_lo, c2)
            post_out("ffn1_down", a_hi, a_lo, 2)

        def token_turn(v_of, blocks, dst, v_ready, name, bank=4):
            turned, taken = sem(f"{name}_turned"), sem(f"{name}_taken")
            lots = [(t, g) for g in range(-(-blocks // 4)) for t in range(TB)]

            def pe_part(pe):
                for q, (t, g) in enumerate(lots):
                    if q == 0 or lots[q - 1][1] != g:
                        pe.wait_ge(*v_ready(min(4 * g + 4, blocks) - 1))
                    if q >= 2:
                        pe.wait_ge(taken, q - 1)
                    for b in range(4 * g, min(4 * g + 4, blocks)):
                        m = pe.transpose(ps[bank + q % 2][:, (b % 4) * P:(b % 4) * P + P],
                                         v_of(b)[:, t * P:t * P + P], ident[:, :])
                    m.then_inc(turned, 1)

            def dve_part(dve):
                for q, (t, g) in enumerate(lots):
                    w = (min(4 * g + 4, blocks) - 4 * g) * P
                    dve.wait_ge(turned, q + 1)
                    nc.vector.tensor_copy(dst[:, t, g * 4 * P:g * 4 * P + w], ps[bank + q % 2][:, 0:w]).then_inc(taken, 1)
            return pe_part, dve_part

        (scored, z_done, nm_done, p_done, ri_done, p_scaled, t_done, pt_done, pv_done, o_taken) = (
            sem(f"att_{x}") for x in ("scored", "z", "negmax", "exp", "inv", "scaled", "turned", "pt", "pv", "otaken"))
        e_sink, den_done = sem("att_expsink"), sem("att_den")

        def softmax_attention(name, units, groups, room, ctx):
            U = len(units)
            Z, PT = room[:, 0:4, :], room[:, 4:6, :]
            cols = sb(f"{name}_cols", [P, 5, U], ctx=ctx)
            MX, NM, RS, RI, ES = range(5)
            B, BG = n["units"], n["groups"]
            n["units"] += U
            n["groups"] += len(groups)
            sinks = units[0].get("sink") is not None
            group_of, start = {}, 0
            for g, (last, _, _) in enumerate(groups):
                for u in range(start, last + 1):
                    group_of[u] = g
                start = last + 1
            last_of = {last: g for g, (last, _, _) in enumerate(groups)}

            def pe_part(pe):
                for s in range(U + 3):
                    if s < U:
                        u, d = s, units[s]
                        if u >= 3:
                            pe.wait_ge(z_done, B + u - 2)
                        o = ps[u % 3][:, 0:d["klen"]]
                        m = pe.matmul(o, d["q"], d["k"], start=True, stop=not d["add"])
                        for x, (a, b) in enumerate(d["add"]):
                            m = pe.matmul(o, a, b, start=False, stop=x == len(d["add"]) - 1)
                        m.then_inc(scored, 1)
                    if 2 <= s < U + 2:
                        u, d = s - 2, units[s - 2]
                        pe.wait_ge(p_scaled, B + u + 1)
                        if u >= 2:
                            pe.wait_ge(pt_done, B + u - 1)
                        for x in range(d["klen"] // P):
                            m = pe.transpose(ps[3 + u % 2][:, x * P:x * P + P], Z[:, u % 4, x * P:x * P + P], ident[:, :])
                        m.then_inc(t_done, 1)
                    if s >= 3:
                        u, d = s - 3, units[s - 3]
                        g = group_of[u]
                        pe.wait_ge(pt_done, B + u + 1)
                        if g >= 2:
                            pe.wait_ge(o_taken, BG + g - 1)
                        o = ps[5 + g % 2][d["po"]:d["po"] + d["m"], d["oc"]:d["oc"] + P]
                        nk = d["klen"] // P
                        for x in range(nk):
                            m = pe.matmul(o, d["v"][x], PT[:, u % 2, x * P:x * P + P], start=x == 0, stop=x == nk - 1)
                        m.then_inc(pv_done, 1)

            def dve_part(dve):
                for s in range(U + 5):
                    if s < U:
                        u, d = s, units[s]
                        dve.wait_ge(scored, B + u + 1)
                        if u >= 4:
                            dve.wait_ge(t_done, B + u - 3)
                        nc.vector.tensor_tensor_reduce(Z[:, u % 4, 0:d["klen"]], ps[u % 3][:, 0:d["klen"]], d["mask"],
                                                       1.0, NEG, ALU.add, ALU.max, cols[:, MX, u:u + 1]).then_inc(z_done, 1)
                        dve.wait_ge(z_done, B + u + 1)
                        if sinks:
                            nc.vector.tensor_scalar(cols[:, NM, u:u + 1], cols[:, MX, u:u + 1], d["sink"], -1.0,
                                                    ALU.max, ALU.mult).then_inc(nm_done, 1)
                        else:
                            nc.vector.tensor_scalar(cols[:, NM, u:u + 1], cols[:, MX, u:u + 1], -1.0, None,
                                                    ALU.mult).then_inc(nm_done, 1)
                    if 1 <= s < U + 1:
                        u, d = s - 1, units[s - 1]
                        dve.wait_ge(p_done, B + u + 1)
                        den = cols[:, RS, u:u + 1]
                        if sinks:
                            dve.wait_ge(e_sink, u + 1)
                            nc.vector.tensor_tensor(den, den, cols[:, ES, u:u + 1], ALU.add).then_inc(den_done, 1)
                            dve.wait_ge(den_done, u + 1)
                        nc.vector.reciprocal(cols[:, RI, u:u + 1], den).then_inc(ri_done, 1)
                        dve.wait_ge(ri_done, B + u + 1)
                        nc.vector.tensor_scalar(Z[:, u % 4, 0:d["klen"]], Z[:, u % 4, 0:d["klen"]], cols[:, RI, u:u + 1],
                                                None, ALU.mult).then_inc(p_scaled, 1)
                    if s - 4 in last_of:
                        g = last_of[s - 4]
                        dve.wait_ge(pv_done, B + s - 3)
                        nc.vector.tensor_copy(groups[g][1], groups[g][2](ps[5 + g % 2])).then_inc(o_taken, 1)

            def act_part(act):
                for s in range(U + 2):
                    if s < U:
                        u, d = s, units[s]
                        act.wait_ge(nm_done, B + u + 1)
                        z = Z[:, u % 4, 0:d["klen"]]
                        nc.scalar.activation(z, z, ACT.Exp, bias=cols[:, NM, u:u + 1],
                                             accum_out=cols[:, RS, u:u + 1]).then_inc(p_done, 1)
                        if sinks:
                            nc.scalar.activation(cols[:, ES, u:u + 1], d["sink"], ACT.Exp,
                                                 bias=cols[:, NM, u:u + 1]).then_inc(e_sink, 1)
                    if s >= 2:
                        u, d = s - 2, units[s - 2]
                        act.wait_ge(t_done, B + u + 1)
                        if u >= 2:
                            act.wait_ge(pv_done, B + u - 1)
                        nc.scalar.activation(PT[:, u % 2, 0:d["klen"]], ps[3 + u % 2][:, 0:d["klen"]],
                                             ACT.Copy).then_inc(pt_done, 1)
            return pe_part, dve_part, act_part

        with ExitStack() as c:
            qkv = sb("qkv", [P, 24, SEQ], ctx=c)
            va = sb("va", [P, TB, 4 * P], ctx=c)
            vb = sb("vb", [P, TB, 4 * P], ctx=c)
            bias = sb("bias", [P, H8, SEQ], ctx=c)
            scratch = nc.dram_tensor("bias_rows", (H8, P, BAND_W), F32, kind="Internal").ap()
            q_scaled = sem("q_scaled")
            b_in, b_rev, b_out, b_back, b_mask = (sem(f"bias_{x}") for x in ("in", "reversed", "out", "back", "masked"))
            ev_mix = n["ev"]
            turn_a = token_turn(lambda b: qkv[:, 8 + b, :], 4, va, lambda b: (evac, ev_mix + 8 + b + 1), "va")
            turn_b = token_turn(lambda b: qkv[:, 20 + b, :], 4, vb, lambda b: (evac, ev_mix + 20 + b + 1), "vb", 6)
            with ExitStack() as c2:
                rb = sb("rb", [H8, 2 * REL + 1], ctx=c2)
                ext = sb("ext", [H8, BAND_W], ctx=c2)
                far = BAND_W - 2 * REL

                def sp_tail(sp):
                    sp.dma_start(rb[:, :], I["rel_bias"][0]).then_inc(b_in, 16)
                    sp.wait_ge(b_rev, 2)
                    sp.dma_start(scratch, ext[:, :].rearrange("h (o n) -> h o n", o=1).broadcast_to([H8, P, BAND_W])).then_inc(b_out, 16)
                    sp.wait_ge(b_out, 16)
                    for hd in range(H8):
                        src = bass.AP(scratch.tensor, hd * P * BAND_W + P - 1, [[BAND_W - 1, P], [1, SEQ]])
                        sp.dma_start(bias[:, hd, :], src).then_inc(b_back, 16)

                def pool_tail(pool):
                    pool.wait_ge(b_in, 16)
                    nc.gpsimd.tensor_copy(ext[:, far:BAND_W], rb[:, 2 * REL - 1::-1]).then_inc(b_rev, 1)
                    nc.gpsimd.tensor_copy(ext[:, 0:far], rb[:, 2 * REL:2 * REL + 1].broadcast_to([H8, far])).then_inc(b_rev, 1)
                    pool.wait_ge(b_back, 16 * H8)
                    nc.gpsimd.memset(bias[0:HD, :, SEQ - HD:SEQ], NEG).then_inc(b_mask, 1)

                def dve_tail(dve, ev0):
                    dve.wait_ge(evac, ev0 + 16)
                    for g in range(2):
                        q = qkv[:, 12 * g:12 * g + 4, :]
                        nc.vector.tensor_scalar(q, q, HD ** -0.5, None, ALU.mult).then_inc(q_scaled, 1)
                    turn_a[1](dve)
                    turn_b[1](dve)

                def pe_tail(pe, ev0):
                    turn_a[0](pe)
                    turn_b[0](pe)

                in_proj("mix_in", gains("g_mix_pre"), qkv, update=half[:, 0, :],
                        tails=dict(sp=sp_tail, pool=pool_tail, dve=dve_tail, pe=pe_tail))

            with ExitStack() as c2:
                off = {3: 0, 2: P, 1: 3 * P, 0: 6 * P}
                wide = 10 * P
                SP_ = sb("softplus", [P, 2, wide], ctx=c2)
                A = sb("weights", [P, 2, wide], ctx=c2)
                tmp = qkv[:, 8:11, :]
                ntri = sb("ntri", [P, P], ctx=c2)
                nones = sb("nones", [P, P], ctx=c2)
                (sbc, z_mm, abs_d, exp_d, ln_d, sp_raw, sp_d, c_mm, a_raw, a_d, av_mm, o_d) = (sem(f"sb_{x}") for x in (
                    "const", "z", "abs", "exp", "ln", "spraw", "sp", "c", "araw", "a", "av", "o"))
                units = [(hd, kb) for hd in range(H8) for kb in (3, 2, 1, 0)]
                U = len(units)
                ZB = 6

                with nc.Block() as block:
                    @block.gpsimd
                    def _(pool):
                        nc.gpsimd.memset(nones[:, :], -1.0).then_inc(sbc, 1)
                        pool.wait_ge(sbc, 1)
                        nc.gpsimd.affine_select(out=ntri[:, :], in_=nones[:, :], compare_op=ALU.is_ge, fill=0.0,
                                                base=0, pattern=[[-1, P]], channel_multiplier=1).then_inc(sbc, 1)
                        for s in range(U + 2):
                            if s < U:
                                hd, kb = units[s]
                                v = SP_[:, hd % 2, off[kb]:off[kb] + P]
                                pool.wait_ge(sp_raw, s + 1)
                                nc.gpsimd.affine_select(out=v, in_=v, compare_op=ALU.is_gt, fill=0.0, base=0,
                                                        pattern=[[1, P]], channel_multiplier=-1).then_inc(sp_d, 1)
                            if s >= 2:
                                hd, kb = units[s - 2]
                                v = A[:, hd % 2, off[kb]:off[kb] + P]
                                pool.wait_ge(a_raw, s - 1)
                                nc.gpsimd.affine_select(out=v, in_=v, compare_op=ALU.is_gt, fill=0.0, base=0,
                                                        pattern=[[1, P]], channel_multiplier=-1).then_inc(a_d, 1)

                    @block.tensor
                    def _(pe):
                        pe.wait_ge(sbc, 2)
                        for s in range(U + 4):
                            if s < U:
                                hd, kb = units[s]
                                po = HD * (hd % 2)
                                if s >= ZB:
                                    pe.wait_ge(a_raw, s - ZB + 1)
                                pe.matmul(ps[s % ZB][:, 0:SEQ - kb * P],
                                          qkv[po:po + HD, 4 + hd // 2, kb * P:kb * P + P],
                                          qkv[po:po + HD, hd // 2, kb * P:SEQ], start=True, stop=True).then_inc(z_mm, 1)
                            if 2 <= s < U + 2:
                                u = s - 2
                                hd, kb = units[u]
                                pe.wait_ge(sp_d, u + 1)
                                for k2 in range(kb, TB):
                                    m = pe.matmul(ps[u % ZB][:, (k2 - kb) * P:SEQ - kb * P], (ntri if k2 == kb else nones)[:, :],
                                                  SP_[:, hd % 2, off[k2]:off[k2] + SEQ - k2 * P],
                                                  start=False, stop=True, skip_group_check=True)
                                m.then_inc(c_mm, 1)
                            if s >= 4:
                                u = s - 4
                                hd, kb = units[u]
                                po, pair = HD * (hd % 2), hd // 2
                                pe.wait_ge(a_d, u + 1)
                                if kb == 3 and pair >= 2:
                                    pe.wait_ge(o_d, pair - 1)
                                pe.matmul(ps[6 + pair % 2][po:po + HD, kb * P:SEQ], va[:, kb, hd * HD:hd * HD + HD],
                                          A[:, hd % 2, off[kb]:off[kb] + SEQ - kb * P],
                                          start=kb == 3, stop=kb == 0, skip_group_check=True).then_inc(av_mm, 1)

                    @block.vector
                    def _(dve):
                        for s in range(U + 7):
                            if 1 <= s < U + 1:
                                u = s - 1
                                hd, kb = units[u]
                                w = SEQ - kb * P
                                dve.wait_ge(ln_d, u + 1)
                                if hd >= 2:
                                    dve.wait_ge(c_mm, 4 * (hd - 1))
                                nc.vector.scalar_tensor_tensor(out=SP_[:, hd % 2, off[kb]:off[kb] + w], in0=ps[u % ZB][:, 0:w],
                                                               scalar=0.0, in1=tmp[:, u % 3, 0:w], op0=ALU.max,
                                                               op1=ALU.add).then_inc(sp_raw, 1)
                            if s >= 7 and (s - 7) % 8 == 7:
                                pair = (s - 7) // 8
                                dve.wait_ge(av_mm, 8 * pair + 8)
                                nc.vector.tensor_copy(F[:, pair, :], ps[6 + pair % 2][:, :]).then_inc(o_d, 1)

                    @block.scalar
                    def _(act):
                        for s in range(U + 3):
                            if s < U:
                                hd, kb = units[s]
                                w = SEQ - kb * P
                                t = tmp[:, s % 3, 0:w]
                                act.wait_ge(z_mm, s + 1)
                                if s >= 3:
                                    act.wait_ge(sp_raw, s - 2)
                                nc.scalar.activation(t, ps[s % ZB][:, 0:w], ACT.Abs).then_inc(abs_d, 1)
                                act.wait_ge(abs_d, s + 1)
                                nc.scalar.activation(t, t, ACT.Exp, scale=-1.0).then_inc(exp_d, 1)
                                act.wait_ge(exp_d, s + 1)
                                nc.scalar.activation(t, t, ACT.Ln, bias=1.0).then_inc(ln_d, 1)
                            if s >= 3:
                                u = s - 3
                                hd, kb = units[u]
                                w = SEQ - kb * P
                                act.wait_ge(c_mm, u + 1)
                                if hd >= 2:
                                    act.wait_ge(av_mm, 4 * (hd - 1))
                                nc.scalar.activation(A[:, hd % 2, off[kb]:off[kb] + w], ps[u % ZB][:, 0:w],
                                                     ACT.Exp).then_inc(a_raw, 1)

            with ExitStack() as c2:
                units = []
                for qb in range(TB):
                    for hd in range(H8):
                        po, klen = HD * (hd % 2), (qb + 1) * P
                        units.append(dict(
                            q=qkv[po:po + HD, 12 + hd // 2, qb * P:qb * P + P], k=qkv[po:po + HD, 16 + hd // 2, 0:klen],
                            klen=klen, add=[], mask=bias[:, hd, SEQ - klen:SEQ], po=po, m=HD, oc=(hd // 2) * P,
                            v=[vb[:, x, hd * HD:hd * HD + HD] for x in range(qb + 1)]))
                groups = [(8 * qb + 7, F[:, 4:8, qb * P:qb * P + P],
                           lambda b: b[:, :].rearrange("p (a q) -> p a q", a=4)) for qb in range(TB)]
                pe_p, dve_p, act_p = softmax_attention("ch", units, groups, qkv[:, 6:12, :], c2)
                with nc.Block() as block:
                    @block.tensor
                    def _(pe):
                        pe_p(pe)

                    @block.vector
                    def _(dve):
                        dve_p(dve)

                    @block.scalar
                    def _(act):
                        act_p(act)

            with ExitStack() as c2:
                rs2 = sb("rs2", [P, 2, SEQ], ctx=c2)
                (n_sq, n_mm, n_ms, n_inv, n_rs, n_f) = (sem(f"mixnorm_{x}") for x in ("sq", "mm", "ms", "inv", "rs", "f"))
                x0 = n["x"]
                n["x"] += DB
                with nc.Block() as block:
                    @block.tensor
                    def _(pe):
                        for b in range(DB):
                            pe.wait_ge(n_sq, b + 1)
                            pe.matmul(ps[6 + b // 4][:, :], ones[:, :], sq[:, b % 2, :], start=b % 4 == 0,
                                      stop=b % 4 == 3).then_inc(n_mm, 1)

                    @block.vector
                    def _(dve):
                        for g in range(2):
                            dve.wait_ge(n_mm, 4 * g + 4)
                            nc.vector.tensor_scalar(rs2[:, g, :], ps[6 + g][:, :], 1.0 / (4 * P), EPS, ALU.mult, ALU.add).then_inc(n_ms, 1)
                            dve.wait_ge(n_ms, g + 1)
                            nc.vector.reciprocal(rs2[:, g, :], rs2[:, g, :]).then_inc(n_inv, 1)
                        for b in range(DB + 1):
                            if b < DB:
                                dve.wait_ge(n_rs, b // 4 + 1)
                                nc.vector.tensor_tensor(F[:, b, :], F[:, b, :], rs2[:, b // 4, :], ALU.mult).then_inc(n_f, 1)
                            if b >= 1:
                                q = b - 1
                                dve.wait_ge(xs_hi, x0 + q + 1)
                                nc.vector.scalar_tensor_tensor(out=xl[:, q, :], in0=F[:, q, :], scalar=vA[:, col["g_out_sb"] + q:col["g_out_sb"] + q + 1],
                                                               in1=xh[:, q, :].bitcast(F32), op0=ALU.mult, op1=ALU.subtract).then_inc(xs_lo, 1)

                    @block.scalar
                    def _(act):
                        for b in range(DB):
                            if b >= 2:
                                act.wait_ge(n_mm, b - 1)
                            nc.scalar.activation(sq[:, b % 2, :], F[:, b, :], ACT.Square).then_inc(n_sq, 1)
                        for g in range(2):
                            act.wait_ge(n_inv, g + 1)
                            nc.scalar.activation(rs2[:, g, :], rs2[:, g, :], ACT.Sqrt).then_inc(n_rs, 1)
                        for b in range(DB):
                            act.wait_ge(n_f, b + 1)
                            nc.scalar.activation(xh[:, b, :], F[:, b, :], ACT.Copy,
                                                 scale=vA[:, col["g_out_sb"] + b:col["g_out_sb"] + b + 1]).then_inc(xs_hi, 1)

        post_out("mix_out", xh, xl, 1)
        with ExitStack() as c:
            a_hi = sb("a_hi2", [P, FB, SEQ], F32R, ctx=c)
            a_lo = sb("a_lo2", [P, FB, SEQ], F32R, ctx=c)
            ffn_up("ffn2_up", gains("g_ffn2_pre"), gains("g_mix_post"), a_hi, a_lo, c)
            post_out("ffn2_down", a_hi, a_lo, 2)
        with ExitStack() as c:
            name = "ple"
            pt = sb("p_tokens", [P, TB, PLE], ctx=c)
            phi = sb("p_hi", [P, 2, SEQ], F32R, ctx=c)
            plo = sb("p_lo", [P, 2, SEQ], F32R, ctx=c)
            sg = sb("sigmoid", [P, 2, SEQ], ctx=c)
            p_in, p_t, p_hi, p_lo, sg_d = (sem(f"ple_{x}") for x in ("in", "turned", "hi", "lo", "sigmoid"))
            pro = Prologue(None, half[:, 1, :], squares=False)
            ev0, sq0, acc0, st, t0 = n["ev"], n["sq"], n["acc"], n["stat"], first[name]
            n["ev"] += 2 * DB
            n["sq"] += DB
            n["acc"] += DB
            n["stat"] += 1
            with nc.Block() as block:
                @block.sync
                def _(sp):
                    sp.dma_start(pt[:, :, :], I["p"][0, 0].rearrange("(t p) d -> p t d", p=P)).then_inc(p_in, 16)
                    load_steps(sp, name)

                @block.gpsimd
                def _(pool):
                    sum_squares(pool, sq0, acc0)

                @block.scalar
                def _(act):
                    pro.act(act)
                    for b in range(2):
                        act.wait_ge(p_t, b + 1)
                        nc.scalar.activation(phi[:, b, :], ps[5 + b][:, :], ACT.Copy).then_inc(p_hi, 1)

                    def body(i, j):
                        split_hi(act, name, i, j)
                        o = i * 2 + j // 2
                        act.wait_ge(tile_done, i * 4 + (t0 + j + 1))
                        if j % 2 == 0:
                            wait(act, evac, ev0 + 2 * (o - 1) if not (isinstance(o, int) and o < 2) else 0)
                            nc.scalar.activation(sg[:, j // 2, :], ps[j][:, :], ACT.Sigmoid).then_inc(sg_d, 1)
                        else:
                            act.wait_ge(evac, i * 4 + (ev0 + j + 1))
                            wait(act, acc_done, acc0 + o - 1 if not (isinstance(o, int) and o < 2) else 0)
                            nc.scalar.activation(sq[:, j // 2, :].rearrange("p (o q) -> p o q", o=1), F[:, bass.ds(o, 1), :],
                                                 ACT.Square).then_inc(sq_done, 1)
                    steps(act, name, body)
                    rstd_act(act, st)

                @block.vector
                def _(dve):
                    pro.dve(dve)
                    for b in range(2):
                        dve.wait_ge(p_hi, b + 1)
                        nc.vector.tensor_tensor(plo[:, b, :], ps[5 + b][:, :], phi[:, b, :].bitcast(F32), ALU.subtract).then_inc(p_lo, 1)

                    def body(i, j):
                        split_lo(dve, name, i, j)
                        if j % 2 == 1:
                            o = i * 2 + j // 2
                            dve.wait_ge(tile_done, i * 4 + (t0 + j + 1))
                            dve.wait_ge(sg_d, o + 1)
                            nc.vector.tensor_tensor(F[:, bass.ds(o, 1), :], ps[j][:, :].rearrange("p (o q) -> p o q", o=1),
                                                    sg[:, j // 2, :].rearrange("p (o q) -> p o q", o=1), ALU.mult).then_inc(evac, 2)
                    steps(dve, name, body)
                    rstd_dve(dve, st, D)

                @block.tensor
                def _(pe):
                    pe.wait_ge(p_in, 16)
                    for b in range(2):
                        for t in range(TB):
                            m = pe.transpose(ps[5 + b][:, t * P:t * P + P], pt[:, t, b * P:b * P + P], ident[:, :])
                        m.then_inc(p_t, 1)

                    def body(i, j):
                        r, s, kb, t, got = tile_at(name, i, j, 0)
                        pe.wait_ge(lo_done, t + 1)
                        wait(pe, evac, i * 4 + (ev0 + j - 3))
                        head = isinstance(i, int) and i == 0
                        if head and j == 1:
                            pe.wait_ge(p_lo, 2)
                        a, b_ = (xh, xl) if j % 2 == 0 else (phi, plo)
                        for b in range(kb):
                            if head and j == 0:
                                pe.wait_ge(xs_lo, pro.x0 + b + 1)
                            last = mm3(pe, ps[j][:, :], s, b, a[:, b, :], b_[:, b, :], b == 0, b == kb - 1)
                        last.then_inc(tile_done, 1)
                    steps(pe, name, body)
                    rstd_pe(pe, acc0 + DB)

        with ExitStack() as c:
            name = "conv_in"
            K = 3
            cv = sb("cv", [P, 2, SEQ + K - 1], ctx=c)
            y = sb("conv_y", [P, 2, SEQ], ctx=c)
            zs = sb("conv_z", [P, 2, SEQ], ctx=c)
            br = sb("conv_b", [P, 2, SEQ], ctx=c)
            yall = sb("conv_yall", [P, DB, SEQ], ctx=c)
            cz, cr, cvd, yd, zd, bd = (sem(f"conv_{x}") for x in ("zeros", "c", "cv", "y", "z", "b"))
            pro = Prologue(gains("norm_w_2"), gains("g_ple_post"))
            ev0, st, t0 = n["ev"], n["stat"], first[name]
            n["ev"] += 4 * DB
            n["stat"] += 1
            wcol = col["conv_w_conv_2"]
            with nc.Block() as block:
                @block.sync
                def _(sp):
                    load_steps(sp, name)

                @block.gpsimd
                def _(pool):
                    for s in range(2):
                        nc.gpsimd.memset(cv[:, s, 0:K - 1], 0.0).then_inc(cz, 1)
                    pro.pool(pool)

                @block.scalar
                def _(act):
                    pro.act(act)

                    def body(i, j):
                        split_hi(act, name, i, j)
                        if isinstance(i, int) and i == 0 and j == 0:
                            rstd_act(act, st)
                        if j == 3:
                            act.wait_ge(zd, i + 1)
                            nc.scalar.activation(zs[:, 0, :], zs[:, 0, :], ACT.Silu).then_inc(bd, 1)
                    steps(act, name, body)

                @block.vector
                def _(dve):
                    pro.dve(dve)
                    dve.wait_ge(cz, 2)

                    def body(i, j):
                        split_lo(dve, name, i, j)
                        if isinstance(i, int) and i == 0 and j == 0:
                            rstd_dve(dve, st, D)
                            dve.wait_ge(rstd_done, st + 1)
                        dve.wait_ge(tile_done, i * 4 + (t0 + j + 1))
                        if j == 0:
                            nc.vector.tensor_tensor(br[:, 0, :], ps[j][:, :], rstd[:, :], ALU.mult).then_inc(evac, 1)
                        elif j == 1:
                            nc.vector.tensor_tensor(br[:, 1, :], ps[j][:, :], rstd[:, :], ALU.mult).then_inc(evac, 1)
                            dve.wait_ge(evac, i * 4 + (ev0 + 2))
                            nc.vector.tensor_tensor(br[:, 1, :], br[:, 1, :], rstd[:, :], ALU.mult).then_inc(cr, 1)
                        elif j == 2:
                            dve.wait_ge(cr, i + 1)
                            nc.vector.tensor_tensor(cv[:, 0, K - 1:SEQ + K - 1], ps[j][:, :], br[:, 1, :], ALU.mult).then_inc(evac, 1)
                            dve.wait_ge(evac, i * 4 + (ev0 + 3))
                            nc.vector.tensor_scalar(y[:, 0, :], cv[:, 0, 0:SEQ], vA[:, bass.ds(i + wcol, 1)], None, ALU.mult).then_inc(yd, 1)
                            dve.wait_ge(yd, i * 4 + 1)
                            nc.vector.scalar_tensor_tensor(out=y[:, 1, :], in0=cv[:, 0, 1:SEQ + 1], scalar=vA[:, bass.ds(i + (wcol + DB), 1)],
                                                           in1=y[:, 0, :], op0=ALU.mult, op1=ALU.add).then_inc(yd, 1)
                            dve.wait_ge(yd, i * 4 + 2)
                            nc.vector.scalar_tensor_tensor(out=y[:, 0, :], in0=cv[:, 0, 2:SEQ + 2], scalar=vA[:, bass.ds(i + (wcol + 2 * DB), 1)],
                                                           in1=y[:, 1, :], op0=ALU.mult, op1=ALU.add).then_inc(yd, 1)
                            dve.wait_ge(yd, i * 4 + 3)
                            nc.vector.tensor_tensor(y[:, 1, :], y[:, 0, :], br[:, 0, :], ALU.mult).then_inc(yd, 1)
                        else:
                            nc.vector.tensor_tensor(zs[:, 0, :], ps[j][:, :], rstd[:, :], ALU.mult).then_inc(zd, 1)
                            dve.wait_ge(bd, i + 1)
                            dve.wait_ge(yd, i * 4 + 4)
                            nc.vector.tensor_tensor(yall[:, bass.ds(i, 1), :], y[:, 1, :].rearrange("p (o q) -> p o q", o=1),
                                                    zs[:, 0, :].rearrange("p (o q) -> p o q", o=1), ALU.mult).then_inc(evac, 1)
                    steps(dve, name, body)

                @block.tensor
                def _(pe):
                    pe_tiles(pe, name, xh, xl, ev0, pro=pro, stat_after=(1, pro.acc0 + DB))

            def split_x(src, gain_of=None):
                x0 = n["x"]
                n["x"] += DB
                with nc.Block() as block:
                    @block.scalar
                    def _(act):
                        for b in range(DB):
                            nc.scalar.activation(xh[:, b, :], src(b), ACT.Copy).then_inc(xs_hi, 1)

                    @block.vector
                    def _(dve):
                        for b in range(DB):
                            dve.wait_ge(xs_hi, x0 + b + 1)
                            nc.vector.tensor_tensor(xl[:, b, :], src(b), xh[:, b, :].bitcast(F32), ALU.subtract).then_inc(xs_lo, 1)

            split_x(lambda b: yall[:, b, :])
        acc_at = resid_out("conv_out")

        with ExitStack() as c:
            qkv = sb("fox_qkvz", [P, 4 * DB, SEQ], ctx=c)
            vt = sb("fox_v", [P, TB, D], ctx=c)
            fl = sb("fox_f", [H8, 4, SEQ], ctx=c)
            bf = sb("fox_bf", [H8, 1], ctx=c)
            nsel = sb("fox_nsel", [H8, H8, P], ctx=c)
            mask = sb("fox_mask", [P, SEQ], ctx=c)
            f_in, fsel, fm, fd, q_sc, z_silu = (sem(f"fox_{x}") for x in ("bf", "sel", "mask", "f", "q", "z"))
            ev0 = n["ev"]
            turn = token_turn(lambda b: qkv[:, 16 + b, :], 8, vt, lambda b: (evac, ev0 + 16 + b + 1), "fox_vt")

            def sp_tail(sp):
                sp.dma_start(bf[:, :], I["fox_b_f_2"].rearrange("a h -> h a")).then_inc(f_in, 16)

            def pool_tail(pool):
                nc.gpsimd.memset(nsel[:, :, :], 0.0).then_inc(fsel, 1)
                nc.gpsimd.memset(fl[:, 3, :], 1.0).then_inc(fsel, 1)
                pool.wait_ge(fsel, 1)
                nc.gpsimd.affine_select(out=nsel[:, :, :], in_=nsel[:, :, :], compare_op=ALU.not_equal, fill=-1.0, base=0,
                                        pattern=[[-1, H8], [0, P]], channel_multiplier=1).then_inc(fsel, 1)
                nc.gpsimd.memset(mask[:, :], 0.0).then_inc(fm, 1)
                pool.wait_ge(fm, 1)
                nc.gpsimd.affine_select(out=mask[:, SEQ - P:SEQ], in_=mask[:, SEQ - P:SEQ], compare_op=ALU.is_ge, fill=NEG,
                                        base=0, pattern=[[-1, P]], channel_multiplier=1).then_inc(fm, 1)

            def f_evac(dve, i, j, ev0_):
                if isinstance(i, int) and i == 8:
                    nc.vector.tensor_tensor(fl[:, 0, :], ps[0][0:H8, :], rstd[0:H8, :], ALU.mult).then_inc(evac, 1)
                else:
                    nc.vector.tensor_tensor(qkv[:, bass.ds(i * 4 + j, 1), :], ps[j][:, :].rearrange("p (o q) -> p o q", o=1),
                                            rstd[:, :].rearrange("p (o q) -> p o q", o=1), ALU.mult).then_inc(evac, 1)

            def dve_tail(dve, ev0_):
                dve.wait_ge(evac, ev0_ + 33)
                nc.vector.tensor_scalar(qkv[:, 0:8, :], qkv[:, 0:8, :], P ** -0.5, None, ALU.mult).then_inc(q_sc, 1)
                turn[1](dve)
                dve.wait_ge(f_in, 16)
                dve.wait_ge(fsel, 3)
                nc.vector.tensor_scalar(fl[:, 0, :], fl[:, 0, :], bf[:, 0:1], None, ALU.add).then_inc(fd, 1)
                dve.wait_ge(fd, 4)
                nc.vector.scalar_tensor_tensor(out=fl[:, 2, :], in0=fl[:, 0, :], scalar=0.0, in1=fl[:, 1, :],
                                               op0=ALU.min, op1=ALU.subtract).then_inc(fd, 1)
                dve.wait_ge(fd, 5)
                nc.vector.tensor_tensor_scan(fl[:, 0, :], fl[:, 3, :], fl[:, 2, :], 0.0, ALU.mult, ALU.add).then_inc(fd, 1)

            def act_tail(act, ev0_):
                act.wait_ge(fd, 1)
                nc.scalar.activation(fl[:, 1, :], fl[:, 0, :], ACT.Abs).then_inc(fd, 1)
                act.wait_ge(fd, 2)
                nc.scalar.activation(fl[:, 1, :], fl[:, 1, :], ACT.Exp, scale=-1.0).then_inc(fd, 1)
                act.wait_ge(fd, 3)
                nc.scalar.activation(fl[:, 1, :], fl[:, 1, :], ACT.Ln, bias=1.0).then_inc(fd, 1)
                act.wait_ge(evac, ev0_ + 33)
                for b in range(2):
                    z = qkv[:, 24 + 4 * b:28 + 4 * b, :]
                    nc.scalar.activation(z, z, ACT.Silu).then_inc(z_silu, 1)

            in_proj("fox_in", vA[:, col["norm_w_2"] + DB:col["norm_w_2"] + 2 * DB], None, acc_at=acc_at,
                    tails=dict(sp=sp_tail, pool=pool_tail, dve=dve_tail, act=act_tail, pe=lambda pe, e: turn[0](pe)),
                    evac_dve=f_evac)
            with ExitStack() as c2:
                units = []
                for qb in range(TB):
                    for hd in range(8):
                        klen = (qb + 1) * P
                        units.append(dict(
                            q=qkv[:, hd, qb * P:qb * P + P], k=qkv[:, 8 + hd, 0:klen], klen=klen,
                            add=[(nsel[:, hd, :], fl[:, 0, 0:klen])], mask=mask[:, SEQ - klen:SEQ], po=0, m=P,
                            oc=(hd % 4) * P, v=[vt[:, x, hd * P:hd * P + P] for x in range(qb + 1)]))
                groups = [(4 * g + 3, F[:, 4 * (g % 2):4 * (g % 2) + 4, (g // 2) * P:(g // 2) * P + P],
                           lambda b: b[:, :].rearrange("p (a q) -> p a q", a=4)) for g in range(2 * TB)]
                pe_p, dve_p, act_p = softmax_attention("fox", units, groups, qkv[:, 16:22, :], c2)
                with nc.Block() as block:
                    @block.tensor
                    def _(pe):
                        pe_p(pe)

                    @block.vector
                    def _(dve):
                        dve_p(dve)

                    @block.scalar
                    def _(act):
                        act_p(act)

            def gate_x(zb):
                x0, f0 = n["x"], n["fs"]
                n["x"] += DB
                n["fs"] += DB
                with nc.Block() as block:
                    @block.scalar
                    def _(act):
                        for b in range(DB):
                            act.wait_ge(f_scaled, f0 + b + 1)
                            nc.scalar.activation(xh[:, b, :], F[:, b, :], ACT.Copy).then_inc(xs_hi, 1)

                    @block.vector
                    def _(dve):
                        for b in range(DB + 1):
                            if b < DB:
                                nc.vector.tensor_tensor(F[:, b, :], F[:, b, :], zb(b), ALU.mult).then_inc(f_scaled, 1)
                            if b >= 1:
                                dve.wait_ge(xs_hi, x0 + b)
                                nc.vector.tensor_tensor(xl[:, b - 1, :], F[:, b - 1, :], xh[:, b - 1, :].bitcast(F32),
                                                        ALU.subtract).then_inc(xs_lo, 1)

            gate_x(lambda b: qkv[:, 24 + b, :])
        acc_at = resid_out("fox_out")
        with ExitStack() as c:
            G = sb("gdn_qkvz", [P, 4 * DB, SEQ], ctx=c)
            X = sb("gdn_slots", [P, 12, SEQ], ctx=c)
            BG = sb("gdn_bg", [40, SEQ], ctx=c)
            K = 4
            ev0 = n["ev"]
            with ExitStack() as c2:
                u = X[:, 0:4, :].rearrange("p a q -> p (a q)")
                W_U = SEQ + K - 1
                ub = [u[:, s * W_U:(s + 1) * W_U] for s in range(2)]
                c_zero, c_tap, c_silu = sem("gdn_zero"), sem("gdn_tap"), sem("gdn_silu")

                def one(ap):
                    return ap.rearrange("p (o q) -> p o q", o=1)

                def g_evac(dve, i, j, ev0_):
                    if isinstance(i, int) and i == 8:
                        nc.vector.tensor_tensor(BG[:, :], ps[0][0:40, :], rstd[0:40, :], ALU.mult).then_inc(evac, 1)
                        return
                    k = i * 4 + j
                    if isinstance(i, int) and i >= 6:
                        nc.vector.tensor_tensor(G[:, k, :], ps[j][:, :], rstd[:, :], ALU.mult).then_inc(evac, 1)
                        return
                    if isinstance(i, int) and k == 0:
                        dve.wait_ge(c_zero, 2)
                    U_, dst = ub[j % 2], G[:, bass.ds(k, 1), :]
                    nc.vector.tensor_tensor(U_[:, K - 1:K - 1 + SEQ], ps[j][:, :], rstd[:, :], ALU.mult).then_inc(evac, 1)
                    dve.wait_ge(evac, i * 4 + (ev0_ + j + 1))
                    nc.vector.tensor_scalar(dst, one(U_[:, 0:SEQ]), vB[:, bass.ds(k, 1)], None, ALU.mult).then_inc(c_tap, 1)
                    for tap in range(1, K):
                        dve.wait_ge(c_tap, i * 16 + (4 * j + tap))
                        nc.vector.scalar_tensor_tensor(out=dst, in0=one(U_[:, tap:tap + SEQ]), scalar=vB[:, bass.ds(i * 4 + (j + 24 * tap), 1)],
                                                       in1=dst, op0=ALU.mult, op1=ALU.add).then_inc(c_tap, 1)

                def g_act(act, i, j, ev0_):
                    if isinstance(i, int) and i >= 6:
                        return
                    act.wait_ge(c_tap, i * 16 + (4 * j + 4))
                    dst = G[:, bass.ds(i * 4 + j, 1), :]
                    nc.scalar.activation(dst, dst, ACT.Silu).then_inc(c_silu, 1)

                def act_tail(act, ev0_):
                    act.wait_ge(evac, ev0_ + 32)
                    for b in range(2):
                        z = G[:, 24 + 4 * b:28 + 4 * b, :]
                        nc.scalar.activation(z, z, ACT.Silu).then_inc(c_silu, 1)

                def pool_tail(pool):
                    for s in range(2):
                        nc.gpsimd.memset(ub[s][:, 0:K - 1], 0.0).then_inc(c_zero, 1)

                in_proj("gdn_in", vA[:, col["norm_w_2"] + 2 * DB:col["norm_w_2"] + 3 * DB], None, acc_at=acc_at,
                        tails=dict(pool=pool_tail, act=act_tail), evac_dve=g_evac, evac_act=g_act, loop_end=6)

            LV = 7
            TH = [P, TB, H8]
            cc = sb("gdn_cc", [P, TB, 40], ctx=c)
            tab = sb("gdn_tab", [P, 16, TB, H8], ctx=c)
            (BETA, AX, AE, GG, GC, GL, EGC, EGL, EKD, CKN, CKB, CKBE, CKD, CQN, CQD, TMP) = range(16)
            nrm = sb("gdn_norm", [P, TB, 16], ctx=c)
            al = sb("gdn_al", [P, 3, H8], ctx=c)
            lev = sb("gdn_levels", [P, LV, P], ctx=c)
            triu = sb("gdn_triu", [P, P], ctx=c)
            state = sb("gdn_state", [P, 2, P], ctx=c)
            vn = sb("gdn_vnew", [P, 2, P], ctx=c)
            a_in, g_const, g_c, g_ct, g_sq, g_ss = (sem(f"gdn_{x}") for x in ("ain", "const", "col", "colturn", "sq", "ss"))
            g_dv = sem("gdn_link")
            with nc.Block() as block:
                @block.sync
                def _(sp):
                    for r, nm in enumerate(("gdn_a_log_2", "gdn_dt_bias_2")):
                        sp.dma_start(al[:, r, :], I[nm].broadcast_to([P, H8])).then_inc(a_in, 16)

                @block.gpsimd
                def _(pool):
                    nc.gpsimd.affine_select(out=triu[:, :], in_=ones[:, :], compare_op=ALU.is_ge, fill=0.0, base=0,
                                            pattern=[[1, P]], channel_multiplier=-1).then_inc(g_const, 1)
                    nc.gpsimd.memset(lev[:, :, :], 0.0).then_inc(g_const, 1)
                    pool.wait_ge(g_const, 2)
                    for l in range(LV):
                        b = 2 ** l
                        m = P // (2 * b)
                        v = lev[:, l, :].rearrange("p (m s r) -> p m s r", m=m, s=2)[:, :, 1, :]
                        src = ones[:, 0:m * b].rearrange("p (m r) -> p m r", m=m)
                        nc.gpsimd.affine_select(out=v, in_=src, compare_op=ALU.is_ge, fill=0.0, base=0,
                                                pattern=[[-2 * b, m], [0, b]], channel_multiplier=1).then_inc(g_const, 1)
                        pool.wait_ge(g_const, 3 + 2 * l)
                        nc.gpsimd.affine_select(out=v, in_=v, compare_op=ALU.is_ge, fill=0.0, base=b - 1,
                                                pattern=[[2 * b, m], [0, b]], channel_multiplier=-1).then_inc(g_const, 1)

                @block.tensor
                def _(pe):
                    for t in range(TB):
                        m = pe.transpose(ps[0][:, t * 40:t * 40 + 40], BG[:, t * P:t * P + P], ident[0:40, 0:40])
                    m.then_inc(g_ct, 1)
                    for b in range(16):
                        pe.wait_ge(g_sq, b + 1)
                        for t in range(TB):
                            m = pe.matmul(ps[1][:, t * 16 + b:t * 16 + b + 1], X[:, b % 4, t * P:t * P + P], ones[:, 0:1],
                                          start=True, stop=True)
                        m.then_inc(g_ss, 1)
                    pe.wait_ge(g_c, 6)
                    pe.wait_ge(g_const, 1)
                    g = tab[:, GG, :, :].rearrange("p t h -> p (t h)")
                    pe.matmul(ps[2][:, 0:32], triu[:, :], g, start=True, stop=True)
                    pe.matmul(ps[2][:, 32:64], ones[:, :], g, start=True, stop=True).then_inc(g_ct, 1)

                @block.scalar
                def _(act):
                    for b in range(16):
                        if b >= 4:
                            act.wait_ge(g_ss, b - 3)
                        nc.scalar.activation(X[:, b % 4, :], G[:, b, :], ACT.Square).then_inc(g_sq, 1)
                    act.wait_ge(g_c, 2)
                    nc.scalar.activation(nrm[:, :, :], nrm[:, :, :], ACT.Sqrt).then_inc(g_c, 1)
                    nc.scalar.activation(tab[:, BETA, :, :], cc[:, :, 0:H8], ACT.Sigmoid).then_inc(g_c, 1)
                    nc.scalar.activation(tab[:, AE, :, :], tab[:, AX, :, :], ACT.Abs).then_inc(g_sq, 1)
                    act.wait_ge(g_sq, 17)
                    nc.scalar.activation(tab[:, AE, :, :], tab[:, AE, :, :], ACT.Exp, scale=-1.0).then_inc(g_sq, 1)
                    act.wait_ge(a_in, 32)
                    nc.scalar.activation(al[:, 2, :], al[:, 0, :], ACT.Exp).then_inc(g_sq, 1)
                    act.wait_ge(g_sq, 18)
                    nc.scalar.activation(tab[:, AE, :, :], tab[:, AE, :, :], ACT.Ln, bias=1.0).then_inc(g_sq, 1)
                    act.wait_ge(g_c, 8)
                    nc.scalar.activation(tab[:, EGC:EGC + 3, :, :], tab[:, EGC:EGC + 3, :, :], ACT.Exp).then_inc(g_c, 1)

                @block.vector
                def _(dve):
                    def bc(ap):
                        return ap.rearrange("p (o h) -> p o h", o=1).broadcast_to(TH)

                    steps_ = [0]

                    def link(ins):
                        steps_[0] += 1
                        ins.then_inc(g_dv, 1)
                        dve.wait_ge(g_dv, steps_[0])

                    dve.wait_ge(g_ct, 1)
                    link(nc.vector.tensor_copy(cc[:, :, :], ps[0][:, 0:160].rearrange("p (t c) -> p t c", t=TB)))
                    dve.wait_ge(a_in, 32)
                    nc.vector.tensor_tensor(tab[:, AX, :, :], cc[:, :, 32:40], bc(al[:, 1, :]), ALU.add).then_inc(g_c, 1)
                    dve.wait_ge(g_ss, 16)
                    nc.vector.tensor_scalar(nrm[:, :, :], ps[1][:, 0:64].rearrange("p (t c) -> p t c", t=TB), EPS, None,
                                            ALU.add).then_inc(g_c, 1)
                    dve.wait_ge(g_c, 4)
                    link(nc.vector.reciprocal(nrm[:, :, :], nrm[:, :, :]))
                    dve.wait_ge(g_sq, 20)
                    link(nc.vector.scalar_tensor_tensor(out=tab[:, TMP, :, :], in0=tab[:, AX, :, :], scalar=0.0, in1=tab[:, AE, :, :],
                                                        op0=ALU.max, op1=ALU.add))
                    nc.vector.tensor_scalar(al[:, 2, :], al[:, 2, :], -1.0, None, ALU.mult).then_inc(g_c, 1)
                    dve.wait_ge(g_c, 5)
                    nc.vector.tensor_tensor(tab[:, GG, :, :], tab[:, TMP, :, :], bc(al[:, 2, :]), ALU.mult).then_inc(g_c, 1)
                    dve.wait_ge(g_ct, 2)
                    link(nc.vector.tensor_copy(tab[:, GC:GC + 2, :, :], ps[2][:, 0:64].rearrange("p (a t h) -> p a t h", a=2, t=TB)))
                    link(nc.vector.tensor_copy(tab[:, EGC:EGC + 2, :, :], tab[:, GC:GC + 2, :, :]))
                    nc.vector.tensor_tensor(tab[:, EKD, :, :], tab[:, GL, :, :], tab[:, GC, :, :], ALU.subtract).then_inc(g_c, 2)
                    dve.wait_ge(g_c, 9)
                    k_, q_ = nrm[:, :, 8:16], nrm[:, :, 0:8]
                    link(nc.vector.tensor_copy(tab[:, CKN, :, :], k_))
                    link(nc.vector.tensor_tensor(tab[:, CKB, :, :], k_, tab[:, BETA, :, :], ALU.mult))
                    link(nc.vector.tensor_tensor(tab[:, CKBE, :, :], tab[:, CKB, :, :], tab[:, EGC, :, :], ALU.mult))
                    link(nc.vector.tensor_tensor(tab[:, CKD, :, :], k_, tab[:, EKD, :, :], ALU.mult))
                    link(nc.vector.tensor_scalar(tab[:, CQN, :, :], q_, P ** -0.5, None, ALU.mult))
                    link(nc.vector.tensor_tensor(tab[:, CQD, :, :], tab[:, CQN, :, :], tab[:, EGC, :, :], ALU.mult))

            KN, KB, QN, QD, KNT, KBT, QNT, KBE, KD, DD = range(10)
            LT, BT0, BT1, US, T_, TT, QKT = KN, KB, QN, QD, KNT, KBT, QNT

            def slot(s, r):
                return F[:, s, :] if r == 0 and s < 8 else X[:, s - 8 if r == 0 else 2 + s, :]

            def blk(ap, t):
                return ap[:, t * P:t * P + P]

            def v4(ap):
                return ap.rearrange("p (t d) -> p t d", t=TB)

            def colb(row, hd):
                return tab[:, row, :, hd:hd + 1].broadcast_to([P, TB, P])

            (t_in, k_copied, tok_d, tok_p, t_back, back_a, back_d, kk_mm, dif, dif_m, dec, qkt_d, strict, lt_d, bt_d, u_mm,
             us_d, p_mm, t_d, w_mm, w_d, v_mm, vn_d, o_mm, s_mm, s_d, o_tok) = (sem(f"gd_{x}") for x in (
                 "tin", "kcopied", "tokd", "tokp", "tback", "backa", "backd", "kk", "dif", "difm", "dec", "qkt", "strict", "lt",
                 "bt", "u", "us", "p", "t", "w", "wd", "v", "vn", "o", "s", "sd", "otok"))
            NP_ = H8 // 2

            def lvl(p, l, r):
                return (p * LV + l) * 2 + r + 1

            with nc.Block() as block:
                @block.tensor
                def _(pe):
                    for p in range(NP_):
                        for r in range(2):
                            m, b = 2 * p + r, 4 * r
                            if p:
                                pe.wait_ge(o_tok, m - 1)
                            for src, bank in ((m, 0), (8 + m, 1), (16 + m, 2)):
                                for t in range(TB):
                                    ins = pe.transpose(blk(ps[b + bank], t), blk(G[:, src, :], t), ident[:, :])
                            ins.then_inc(t_in, 1)
                        for r in range(2):
                            m, b = 2 * p + r, 4 * r
                            pe.wait_ge(tok_d, 5 * m + 5)
                            pe.wait_ge(k_copied, m + 1)
                            for x, s in enumerate((KN, KB, QN, QD)):
                                for t in range(TB):
                                    ins = pe.transpose(blk(ps[b + x], t), blk(slot(s, r), t), ident[:, :])
                            ins.then_inc(t_back, 1)
                        for r in range(2):
                            m, b = 2 * p + r, 4 * r
                            pe.wait_ge(back_a, 2 * m + 2)
                            pe.wait_ge(back_d, 2 * m + 2)
                            for t in range(TB):
                                pe.matmul(blk(ps[b + 2], t), tab[:, GC, t, m:m + 1].broadcast_to([P, P]), ident[:, :],
                                          start=True, stop=True)
                                pe.matmul(blk(ps[b], t), blk(slot(KNT, r), t), blk(slot(KBT, r), t), start=True, stop=True)
                                ins = pe.matmul(blk(ps[b + 1], t), blk(slot(KNT, r), t), blk(slot(QNT, r), t),
                                                start=True, stop=True)
                            ins.then_inc(kk_mm, 1)
                        for l in range(LV):
                            for r in range(2):
                                m, b = 2 * p + r, 4 * r
                                pe.wait_ge(bt_d, lvl(p, l, r))
                                if l:
                                    pe.wait_ge(t_d, 2 * (lvl(p, l - 1, r)))
                                rhs = ident if l == 0 else slot(T_, r)
                                for t in range(TB):
                                    ins = pe.matmul(blk(ps[b], t), blk(slot(BT0 + l % 2, r), t),
                                                    ident[:, :] if l == 0 else blk(slot(T_, r), t), start=True, stop=True)
                                ins.then_inc(u_mm, 1)
                            if l == 0:
                                continue
                            for r in range(2):
                                m, b = 2 * p + r, 4 * r
                                pe.wait_ge(us_d, (p * (LV - 1) + l - 1) * 2 + r + 1)
                                for t in range(TB):
                                    if l < LV - 1:
                                        pe.matmul(blk(ps[b + 1], t), blk(slot(TT, r), t), blk(slot(US, r), t), start=True, stop=True)
                                    ins = pe.matmul(blk(ps[b + 2], t), blk(slot(US, r), t), blk(slot(TT, r), t), start=True, stop=True)
                                ins.then_inc(p_mm, 1)
                        for r in range(2):
                            m, b = 2 * p + r, 4 * r
                            pe.wait_ge(t_d, 2 * lvl(p, LV - 1, r))
                            pe.wait_ge(tok_p, 2 * m + 2)
                            for t in range(TB):
                                ins = pe.matmul(blk(ps[b + 3], t), blk(slot(KBE, r), t), blk(slot(TT, r), t), start=True, stop=True)
                            ins.then_inc(w_mm, 1)
                        for t in range(TB):
                            for r in range(2):
                                m, b = 2 * p + r, 4 * r
                                ins = pe.matmul(blk(ps[b], t), blk(slot(TT, r), t), blk(G[:, 16 + m, :], t), start=True, stop=t == 0)
                                if t:
                                    pe.wait_ge(w_d, m + 1)
                                    pe.wait_ge(s_d, (p * 3 + t - 1) * 2 + r + 1)
                                    ins = pe.matmul(blk(ps[b], t), blk(G[:, 8 + m, :], t), state[:, r, :], start=False, stop=True)
                                ins.then_inc(v_mm, 1)
                            for r in range(2):
                                m, b = 2 * p + r, 4 * r
                                pe.wait_ge(vn_d, (p * TB + t) * 2 + r + 1)
                                if t == 0:
                                    pe.wait_ge(qkt_d, m + 1)
                                ins = pe.matmul(blk(ps[b + 1], t), blk(slot(QKT, r), t), vn[:, r, :], start=True, stop=t == 0)
                                if t:
                                    ins = pe.matmul(blk(ps[b + 1], t), blk(G[:, m, :], t), state[:, r, :], start=False, stop=True)
                                ins.then_inc(o_mm, 1)
                                if t < TB - 1:
                                    pe.matmul(ps[b + 2][:, 0:P], blk(slot(KD, r), t), vn[:, r, :], start=True, stop=True).then_inc(s_mm, 1)

                @block.vector
                def _(dve):
                    for p in range(NP_):
                        for r in range(2):
                            m, b = 2 * p + r, 4 * r
                            dve.wait_ge(t_in, m + 1)
                            for dst, bank, cf in ((slot(KN, r), 1, CKN), (slot(KB, r), 1, CKB), (slot(QN, r), 0, CQN),
                                                  (slot(QD, r), 0, CQD), (G[:, 16 + m, :], 2, BETA)):
                                nc.vector.tensor_tensor(v4(dst), v4(ps[b + bank][:, :]), colb(cf, m), ALU.mult).then_inc(tok_d, 1)
                        for r in range(2):
                            m, b = 2 * p + r, 4 * r
                            dve.wait_ge(t_back, m + 1)
                            nc.vector.tensor_copy(slot(KBT, r), ps[b + 1][:, :]).then_inc(back_d, 1)
                            nc.vector.tensor_copy(G[:, m, :], ps[b + 3][:, :]).then_inc(back_d, 1)
                        for r in range(2):
                            m, b = 2 * p + r, 4 * r
                            dve.wait_ge(kk_mm, m + 1)
                            dve.wait_ge(tok_p, 2 * m + 2)
                            nc.vector.tensor_tensor(v4(slot(DD, r)), v4(ps[b + 2][:, :]), colb(GC, m), ALU.subtract).then_inc(dif, 1)
                        for r in range(2):
                            m, b = 2 * p + r, 4 * r
                            dve.wait_ge(dec, m + 1)
                            nc.vector.tensor_tensor(slot(QKT, r), ps[b + 1][:, :], slot(DD, r), ALU.mult).then_inc(qkt_d, 1)
                        for r in range(2):
                            m, b = 2 * p + r, 4 * r
                            dve.wait_ge(strict, m + 1)
                            nc.vector.tensor_tensor(slot(LT, r), ps[b][:, :], slot(DD, r), ALU.mult).then_inc(lt_d, 1)
                        idb = ident[:, :].rearrange("p (o d) -> p o d", o=1).broadcast_to([P, TB, P])
                        for l in range(LV):
                            for r in range(2):
                                m, b = 2 * p + r, 4 * r
                                if l == 0:
                                    dve.wait_ge(u_mm, lvl(p, l, r))
                                    nc.vector.tensor_tensor(v4(slot(T_, r)), idb, v4(ps[b][:, :]), ALU.subtract).then_inc(t_d, 1)
                                    nc.vector.tensor_tensor(v4(slot(TT, r)), idb, v4(slot(BT0, r)), ALU.subtract).then_inc(t_d, 1)
                                    continue
                                dve.wait_ge(p_mm, (p * (LV - 1) + l - 1) * 2 + r + 1)
                                if l < LV - 1:
                                    nc.vector.tensor_tensor(slot(T_, r), slot(T_, r), ps[b + 1][:, :], ALU.subtract).then_inc(t_d, 1)
                                    nc.vector.tensor_tensor(slot(TT, r), slot(TT, r), ps[b + 2][:, :], ALU.subtract).then_inc(t_d, 1)
                                else:
                                    nc.vector.tensor_tensor(slot(TT, r), slot(TT, r), ps[b + 2][:, :], ALU.subtract).then_inc(t_d, 2)
                        for t in range(TB - 1):
                            for r in range(2):
                                m, b = 2 * p + r, 4 * r
                                dve.wait_ge(s_mm, (p * 3 + t) * 2 + r + 1)
                                dve.wait_ge(o_mm, (p * TB + t) * 2 + r + 1)
                                if t == 0:
                                    nc.vector.tensor_copy(state[:, r, :], ps[b + 2][:, 0:P]).then_inc(s_d, 1)
                                else:
                                    nc.vector.scalar_tensor_tensor(out=state[:, r, :], in0=state[:, r, :], scalar=tab[:, EGL, t, m:m + 1],
                                                                   in1=ps[b + 2][:, 0:P], op0=ALU.mult, op1=ALU.add).then_inc(s_d, 1)
                        for r in range(2):
                            m, b = 2 * p + r, 4 * r
                            dve.wait_ge(o_mm, (p * TB + TB - 1) * 2 + r + 1)
                            nc.vector.tensor_copy(G[:, m, :], ps[b + 1][:, :]).then_inc(o_tok, 1)

                @block.scalar
                def _(act):
                    for p in range(NP_):
                        for r in range(2):
                            m, b = 2 * p + r, 4 * r
                            act.wait_ge(t_in, m + 1)
                            act.wait_ge(tok_d, 5 * m + 5)
                            nc.scalar.activation(slot(DD, r), ps[b + 1][:, :], ACT.Copy).then_inc(k_copied, 1)
                        for r in range(2):
                            m, b = 2 * p + r, 4 * r
                            act.wait_ge(t_back, m + 1)
                            nc.scalar.activation(slot(KNT, r), ps[b][:, :], ACT.Copy).then_inc(back_a, 1)
                            nc.scalar.activation(slot(QNT, r), ps[b + 2][:, :], ACT.Copy).then_inc(back_a, 1)
                        for r in range(2):
                            m = 2 * p + r
                            act.wait_ge(dif_m, m + 1)
                            nc.scalar.activation(slot(DD, r), slot(DD, r), ACT.Exp).then_inc(dec, 1)
                        for l in range(1, LV):
                            for r in range(2):
                                b = 4 * r
                                act.wait_ge(u_mm, lvl(p, l, r))
                                nc.scalar.activation(slot(US, r), ps[b][:, :], ACT.Copy).then_inc(us_d, 1)
                        for r in range(2):
                            m, b = 2 * p + r, 4 * r
                            act.wait_ge(w_mm, m + 1)
                            nc.scalar.activation(G[:, 8 + m, :], ps[b + 3][:, :], ACT.Copy, scale=-1.0).then_inc(w_d, 1)
                        for t in range(TB):
                            for r in range(2):
                                b = 4 * r
                                act.wait_ge(v_mm, (p * TB + t) * 2 + r + 1)
                                nc.scalar.activation(vn[:, r, :], blk(ps[b], t), ACT.Copy).then_inc(vn_d, 1)

                @block.gpsimd
                def _(pool):
                    for p in range(NP_):
                        for r in range(2):
                            m = 2 * p + r
                            pool.wait_ge(k_copied, m + 1)
                            for dst, cf in ((KBE, CKBE), (KD, CKD)):
                                nc.gpsimd.tensor_tensor(v4(slot(dst, r)), v4(slot(DD, r)), colb(cf, m), ALU.mult).then_inc(tok_p, 1)
                        for r in range(2):
                            m = 2 * p + r
                            pool.wait_ge(dif, m + 1)
                            nc.gpsimd.affine_select(out=v4(slot(DD, r)), in_=v4(slot(DD, r)), compare_op=ALU.is_ge, fill=NEG, base=0,
                                                    pattern=[[0, TB], [1, P]], channel_multiplier=-1).then_inc(dif_m, 1)
                        for r in range(2):
                            m = 2 * p + r
                            pool.wait_ge(qkt_d, m + 1)
                            nc.gpsimd.affine_select(out=v4(slot(DD, r)), in_=v4(slot(DD, r)), compare_op=ALU.is_gt, fill=0.0, base=0,
                                                    pattern=[[0, TB], [1, P]], channel_multiplier=-1).then_inc(strict, 1)
                        for l in range(LV):
                            for r in range(2):
                                m = 2 * p + r
                                if l == 0:
                                    pool.wait_ge(lt_d, m + 1)
                                if l >= 2:
                                    pool.wait_ge(u_mm, lvl(p, l - 2, r))
                                    if l == 2:
                                        pool.wait_ge(t_d, 2 * lvl(p, 0, r))
                                nc.gpsimd.tensor_tensor(v4(slot(BT0 + l % 2, r)), v4(slot(LT, r)),
                                                        lev[:, l, :].rearrange("p (o d) -> p o d", o=1).broadcast_to([P, TB, P]),
                                                        ALU.mult).then_inc(bt_d, 1)

            sso = sb("gdn_sso", [P, H8, TB], ctx=c)
            (o_sq, o_ss, o_ms, o_rt, o_in, o_n, o_t, o_y) = (sem(f"gdo_{x}") for x in ("sq", "ss", "ms", "rt", "inv", "n", "t", "y"))
            x0 = n["x"]
            n["x"] += DB
            with nc.Block() as block:
                @block.scalar
                def _(act):
                    for hd in range(H8):
                        if hd >= 2:
                            act.wait_ge(o_ss, hd - 1)
                        nc.scalar.activation(sq[:, hd % 2, :], G[:, hd, :], ACT.Square).then_inc(o_sq, 1)
                    act.wait_ge(o_ms, 1)
                    nc.scalar.activation(sso[:, :, :], sso[:, :, :], ACT.Sqrt).then_inc(o_rt, 1)
                    for hd in range(H8):
                        act.wait_ge(o_y, hd + 1)
                        nc.scalar.activation(xh[:, hd, :], F[:, hd, :], ACT.Copy).then_inc(xs_hi, 1)

                @block.vector
                def _(dve):
                    for hd in range(H8):
                        dve.wait_ge(o_sq, hd + 1)
                        nc.vector.tensor_reduce(sso[:, hd, :], v4(sq[:, hd % 2, :]), AX_X, ALU.add).then_inc(o_ss, 1)
                    dve.wait_ge(o_ss, H8)
                    nc.vector.tensor_scalar(sso[:, :, :], sso[:, :, :], 1.0 / P, EPS, ALU.mult, ALU.add).then_inc(o_ms, 1)
                    dve.wait_ge(o_rt, 1)
                    nc.vector.reciprocal(sso[:, :, :], sso[:, :, :]).then_inc(o_in, 1)
                    dve.wait_ge(o_in, 1)
                    for s in range(H8 + 3):
                        if s < H8:
                            nc.vector.tensor_tensor(v4(G[:, s, :]), v4(G[:, s, :]),
                                                    sso[:, s, :].rearrange("p (t o) -> p t o", o=1).broadcast_to([P, TB, P]),
                                                    ALU.mult).then_inc(o_n, 1)
                        if 2 <= s < H8 + 2:
                            hd = s - 2
                            dve.wait_ge(o_t, hd + 1)
                            nc.vector.scalar_tensor_tensor(out=F[:, hd, :], in0=ps[hd % 4][:, :], scalar=vB[:, 96:97],
                                                           in1=G[:, 24 + hd, :], op0=ALU.mult, op1=ALU.mult).then_inc(o_y, 1)
                        if s >= 3:
                            hd = s - 3
                            dve.wait_ge(xs_hi, x0 + hd + 1)
                            nc.vector.tensor_tensor(xl[:, hd, :], F[:, hd, :], xh[:, hd, :].bitcast(F32), ALU.subtract).then_inc(xs_lo, 1)

                @block.tensor
                def _(pe):
                    for hd in range(H8):
                        pe.wait_ge(o_n, hd + 1)
                        if hd >= 4:
                            pe.wait_ge(o_y, hd - 3)
                        for t in range(TB):
                            ins = pe.transpose(blk(ps[hd % 4], t), blk(G[:, hd, :], t), ident[:, :])
                        ins.then_inc(o_t, 1)
        acc_at = resid_out("gdn_out")

        with ExitStack() as c:
            qkv = sb("swa_qkvz", [P, 20, SEQ], ctx=c)
            vt = sb("swa_v", [P, TB, 2 * P], ctx=c)
            mask = sb("swa_mask", [P, 2 * P], ctx=c)
            snk = sb("swa_sinks", [P, 16], ctx=c)
            zp = sb("swa_zp", [P, 6, SEQ], ctx=c)
            ev0 = n["ev"]
            turn = token_turn(lambda b: qkv[:, 10 + b, :], 2, vt, lambda b: (evac, ev0 + 10 + b + 1), "swa_vt")
            (p_in, w_con, ang_d, trig, rot_mm, rp, rope_d, z_d) = (sem(f"swa_{x}") for x in ("pin", "con", "ang", "trig", "rot", "rp", "rope", "zd"))
            with ExitStack() as c2:
                pos = sb("swa_pos", [P, SEQ], I32, ctx=c2)
                inv = sb("swa_inv", [P, 1], ctx=c2)
                tg = sb("swa_trig", [P, 4, SEQ], ctx=c2)
                rot = sb("swa_rot", [P, P], ctx=c2)
                TWO_PI = 2 * np.pi
                C1 = 6.28125
                C2 = float(np.float32(round((TWO_PI - C1) * 2 ** 20) / 2 ** 20))
                C3 = float(np.float32(TWO_PI - C1 - C2))
                MAGIC = 1.5 * 2 ** 23
                LIM = 3.1415925
                RB = 10

                def sp_tail(sp):
                    sp.dma_start(pos[:, :], I["positions_2"].broadcast_to([P, SEQ])).then_inc(p_in, 16)
                    sp.dma_start(inv[:, :], I["rope_inv_freq"]).then_inc(p_in, 16)
                    sp.dma_start(snk[:, :], I["swa_sinks_2"].broadcast_to([P, 16])).then_inc(p_in, 16)

                def pool_tail(pool):
                    nc.gpsimd.memset(rot[:, :], 0.0).then_inc(w_con, 1)
                    nc.gpsimd.memset(mask[:, :], 0.0).then_inc(w_con, 1)
                    pool.wait_ge(w_con, 2)
                    r4 = rot[:, :].rearrange("p (a b r) -> p a b r", a=2, b=2)
                    nc.gpsimd.affine_select(out=r4[:, :, 0, :], in_=r4[:, :, 0, :], compare_op=ALU.not_equal, fill=-1.0, base=-32,
                                            pattern=[[-64, 2], [-1, 32]], channel_multiplier=1).then_inc(w_con, 1)
                    nc.gpsimd.affine_select(out=r4[:, :, 1, :], in_=r4[:, :, 1, :], compare_op=ALU.not_equal, fill=1.0, base=0,
                                            pattern=[[-64, 2], [-1, 32]], channel_multiplier=1).then_inc(w_con, 1)
                    nc.gpsimd.affine_select(out=mask[:, :], in_=mask[:, :], compare_op=ALU.is_gt, fill=NEG, base=0,
                                            pattern=[[1, 2 * P]], channel_multiplier=-1).then_inc(w_con, 1)
                    pool.wait_ge(w_con, 5)
                    nc.gpsimd.affine_select(out=mask[:, :], in_=mask[:, :], compare_op=ALU.is_ge, fill=NEG, base=P,
                                            pattern=[[-1, 2 * P]], channel_multiplier=1).then_inc(w_con, 1)
                    for b in range(RB):
                        pool.wait_ge(trig, 2)
                        pool.wait_ge(evac, ev0 + b + 1)
                        pool.wait_ge(rot_mm, b + 1)
                        nc.gpsimd.tensor_tensor(qkv[:, b, :], qkv[:, b, :], tg[:, 1, :], ALU.mult).then_inc(rp, 1)

                def pe_tail(pe, e):
                    turn[0](pe)
                    pe.wait_ge(w_con, 4)
                    for b in range(RB):
                        if b >= 2:
                            pe.wait_ge(rope_d, 2 * (b - 2) + 1)
                        pe.wait_ge(evac, ev0 + 20)
                        pe.matmul(ps[6 + b % 2][:, :], rot[:, :], qkv[:, b, :], start=True, stop=True).then_inc(rot_mm, 1)

                def act_tail(act, e):
                    act.wait_ge(ang_d, 7)
                    nc.scalar.activation(tg[:, 0, :], tg[:, 0, :], ACT.Sin).then_inc(trig, 1)
                    nc.scalar.activation(tg[:, 1, :], tg[:, 1, :], ACT.Sin).then_inc(trig, 1)
                    act.wait_ge(evac, ev0 + 20)
                    for b in range(2):
                        z = qkv[:, 12 + 4 * b:16 + 4 * b, :]
                        nc.scalar.activation(z, z, ACT.Silu).then_inc(z_d, 1)

                def dve_tail(dve, e):
                    k_ = [0]

                    def link(ins):
                        k_[0] += 1
                        ins.then_inc(ang_d, 1)
                        dve.wait_ge(ang_d, k_[0])
                    dve.wait_ge(p_in, 48)
                    a, b_, c_, d_ = (tg[:, q, :] for q in range(4))
                    link(nc.vector.tensor_scalar(a, pos[:, :], inv[:, 0:1], None, ALU.mult))
                    link(nc.vector.tensor_scalar(c_, a, float(1 / TWO_PI), MAGIC, ALU.mult, ALU.add))
                    link(nc.vector.tensor_scalar(c_, c_, MAGIC, None, ALU.subtract))
                    for C in (C1, C2, C3):
                        nc.vector.scalar_tensor_tensor(out=a, in0=c_, scalar=-C, in1=a, op0=ALU.mult, op1=ALU.add).then_inc(rr, 1)
                        rr_n[0] += 1
                        dve.wait_ge(rr, rr_n[0])
                    link(nc.vector.tensor_scalar(b_, a, float(np.pi / 2), None, ALU.add))
                    link(nc.vector.tensor_scalar(d_, b_, float(np.pi), TWO_PI, ALU.is_gt, ALU.mult))
                    link(nc.vector.tensor_tensor(b_, b_, d_, ALU.subtract))
                    link(nc.vector.tensor_scalar(tg[:, 0:2, :], tg[:, 0:2, :], LIM, -LIM, ALU.min, ALU.max))
                    turn[1](dve)
                    dve.wait_ge(trig, 2)
                    for b in range(RB):
                        dve.wait_ge(rot_mm, b + 1)
                        t = tg[:, 2 + b % 2, :]
                        nc.vector.tensor_tensor(t, ps[6 + b % 2][:, :], tg[:, 0, :], ALU.mult).then_inc(rope_d, 1)
                        dve.wait_ge(rope_d, 2 * b + 1)
                        dve.wait_ge(rp, b + 1)
                        nc.vector.tensor_tensor(qkv[:, b, :], qkv[:, b, :], t, ALU.add).then_inc(rope_d, 1)
                    dve.wait_ge(rope_d, 2 * RB)
                    nc.vector.tensor_scalar(qkv[:, 0:8, :], qkv[:, 0:8, :], HD ** -0.5, None, ALU.mult).then_inc(rope_d, 1)

                rr = sem("swa_rr")
                rr_n = [0]
                in_proj("swa_in", vA[:, col["norm_w_2"] + 3 * DB:col["norm_w_2"] + 4 * DB], qkv, acc_at=acc_at,
                        tails=dict(sp=sp_tail, pool=pool_tail, pe=pe_tail, act=act_tail, dve=dve_tail))
            with ExitStack() as c2:
                units = []
                for qb in range(TB):
                    for b in range(DB):
                        for s in range(2):
                            k0, k1 = max(qb - 1, 0), qb + 1
                            klen = (k1 - k0) * P
                            kv, hd = 2 * (b // 4) + s, 8 * (b // 4) + 4 * s + b % 4
                            units.append(dict(
                                q=qkv[HD * s:HD * s + HD, b, qb * P:qb * P + P], k=qkv[HD * s:HD * s + HD, 8 + b // 4, k0 * P:k1 * P],
                                klen=klen, add=[], mask=mask[:, 2 * P - klen:2 * P], po=HD * s, m=HD, oc=(b % 4) * P,
                                v=[vt[:, x, kv * HD:kv * HD + HD] for x in range(k0, k1)], sink=snk[:, hd:hd + 1]))
                groups = [(8 * g + 7, F[:, 4 * (g % 2):4 * (g % 2) + 4, (g // 2) * P:(g // 2) * P + P],
                           lambda b: b[:, :].rearrange("p (a q) -> p a q", a=4)) for g in range(2 * TB)]
                pe_p, dve_p, act_p = softmax_attention("swa", units, groups, zp, c2)
                with nc.Block() as block:
                    @block.tensor
                    def _(pe):
                        pe_p(pe)

                    @block.vector
                    def _(dve):
                        dve_p(dve)

                    @block.scalar
                    def _(act):
                        act_p(act)
            gate_x(lambda b: qkv[:, 12 + b, :])
        acc_at = resid_out("swa_out")
        final(acc_at)


_NAMES = ["x", "p", "g_ffn1_pre", "g_ffn1_post", "w_ffn1_gate", "w_ffn1_up", "w_ffn1_down", "g_mix_pre", "g_mix_post",
          "w_in", "g_out_sb", "g_out_ch", "rel_bias", "w_out", "g_ffn2_pre", "g_ffn2_post", "w_ffn2_gate", "w_ffn2_up",
          "w_ffn2_down", "w_ple_proj", "w_ple_gate", "g_ple_post", "positions_2", "norm_w_2", "final_norm_w_2",
          "conv_w_in_2", "conv_w_conv_2", "conv_w_out_2", "fox_w_in_2", "fox_b_f_2", "fox_w_out_2", "gdn_w_in_2",
          "gdn_w_conv_2", "gdn_a_log_2", "gdn_dt_bias_2", "gdn_norm_w_2", "gdn_w_out_2", "swa_w_in_2", "swa_sinks_2",
          "swa_w_out_2"]


def kernel(**inputs):
    import concourse.bacc as bacc
    from concourse.bass_utils import run_bass_kernel_spmd

    nc = bacc.Bacc("TRN2", target_bir_lowering=False, num_devices=1, dynamic_dma_scratch_size=1024)
    arrays, I = {}, {}
    for name in _NAMES:
        a = np.ascontiguousarray(inputs[name])
        arrays[f"in_{name}"] = a
        I[name] = nc.dram_tensor(f"in_{name}", a.shape, mybir.dt.from_np(a.dtype), kind="ExternalInput").ap()
    out = nc.dram_tensor("out", (1, SEQ, D), F32, kind="ExternalOutput").ap()
    half = HD // 2
    freq = (10000.0 ** (-(np.arange(P) % half) / half)).astype(np.float32).reshape(P, 1)
    arrays["in_rope_inv_freq"] = freq
    I["rope_inv_freq"] = nc.dram_tensor("in_rope_inv_freq", freq.shape, F32, kind="ExternalInput").ap()
    kernel_program(nc, I, out)
    r = run_bass_kernel_spmd(nc, [arrays], core_ids=[0])
    return r.results[0]["out"]
```

```python
from contextlib import ExitStack

import numpy as np
import concourse.bass as bass
from concourse import mybir

F32 = mybir.dt.float32
F32R = mybir.dt.float32r
I32 = mybir.dt.int32
ALU = mybir.AluOpType
ACT = mybir.ActivationFunctionType
AX_X = mybir.AxisListType.X

P = 128
SEQ = 512
D = 1024
DB = D // P
TB = SEQ // P
D_FF = 2816
FB = D_FF // P
WB = 8
DOWN = -(-FB // WB)
PLE = 256
EPS = 1e-6
NEG = -1e30
REL = 128
HD = 64
H8 = 8
RAW = 4
SPLIT = 4
HEAD = 3
BAND_W = SEQ + P


def kernel_program(nc, I, out):
    top = ExitStack()
    with top:
        def sem(name):
            return top.enter_context(nc.semaphore(name))

        def sb(name, shape, dt=F32, ctx=top):
            return ctx.enter_context(nc.sbuf_tensor(name, shape, dt))

        def rows(w, kb0=0, kbn=None):
            v = w.rearrange("(k p) n -> p k n", p=P)
            return v if kbn is None else v[:, kb0:kb0 + kbn, :]

        w1g, w1u, w1d = (I[n][0] for n in ("w_ffn1_gate", "w_ffn1_up", "w_ffn1_down"))
        w2g, w2u, w2d = (I[n][0] for n in ("w_ffn2_gate", "w_ffn2_up", "w_ffn2_down"))
        conv_in, conv_out = I["conv_w_in_2"][0], I["conv_w_out_2"][0]
        fox_in, fox_out = I["fox_w_in_2"][0], I["fox_w_out_2"][0]
        gdn_in, gdn_out = I["gdn_w_in_2"][0], I["gdn_w_out_2"][0]
        swa_in, swa_out = I["swa_w_in_2"][0], I["swa_w_out_2"][0]

        def ffn_up_src(wg, wu):
            g, u = rows(wg), rows(wu)
            return lambda i, j: [(0, P, (g, u)[j % 2], i * (2 * P) + (j // 2) * P)]

        def ffn_down_src(wd):
            v = [rows(wd, WB * q, min(WB, FB - WB * q)) for q in range(DOWN)]
            return lambda i, j: [(0, P, v[(4 * i + j) % DOWN], (4 * i + j) // DOWN * P)]

        def plain_src(w):
            v = rows(w)
            return lambda i, j: [(0, P, v, i * (4 * P) + j * P)]

        def mix_block(i, j):
            return 4 * {4: 5, 5: 4}.get(i, i) + j if isinstance(i, int) else i * 4 + j

        def mix_src():
            v = rows(I["w_in"][0])
            return lambda i, j: [(0, P, v, mix_block(i, j) * P)]

        def ple_src():
            g, q = rows(I["w_ple_gate"][0]), rows(I["w_ple_proj"][0])
            return lambda i, j: [(0, P, (g, q)[j % 2], i * (2 * P) + (j // 2) * P)]

        def conv_src():
            v = rows(conv_in)
            return lambda i, j: [(0, P, v, i * P + j * D)]

        def fox_src():
            v = rows(fox_in)

            def src(i, j):
                if isinstance(i, int) and 4 * i + j >= 28:
                    if j == 0 and i == 7:
                        return [(0, H8, v, 4 * D)]
                    return [(0, P, v, (4 * i + j - 1) * P)]
                return [(0, P, v, i * (4 * P) + j * P)]
            return src

        def gdn_src():
            v = rows(gdn_in)

            def src(i, j):
                if isinstance(i, int) and i >= 6:
                    if i == 6 and j == 0:
                        return [(0, 2 * H8, v, 4 * D)]
                    return [(0, P, v, (4 * i + j - 1) * P)]
                return [(0, P, v, i * (4 * P) + j * P)]
            return src

        def swa_cols(b):
            kvp, m = b // 4, b % 4
            return (8 * kvp + m) * HD, (8 * kvp + 4 + m) * HD

        def swa_src():
            v = rows(swa_in)

            def src(i, j):
                k = 4 * i + j
                if k < 8:
                    a, b = swa_cols(k)
                    return [(0, HD, v, a), (HD, HD, v, b)]
                if k < 12:
                    return [(0, P, v, D + (k - 8) * P)]
                a, b = swa_cols(k - 12)
                return [(0, HD, v, D + 512 + a), (HD, HD, v, D + 512 + b)]
            return src

        stages = [
            ("ffn1_up", 2 * FB, ffn_up_src(w1g, w1u)),
            ("ffn1_down", DOWN * DB, ffn_down_src(w1d)),
            ("mix_in", 24, mix_src()),
            ("mix_out", DB, plain_src(I["w_out"][0])),
            ("ffn2_up", 2 * FB, ffn_up_src(w2g, w2u)),
            ("ffn2_down", DOWN * DB, ffn_down_src(w2d)),
            ("ple", 2 * DB, ple_src()),
            ("conv_in", 4 * DB, conv_src()),
            ("conv_out", DB, plain_src(conv_out)),
            ("fox_in", 4 * DB + 1, fox_src()),
            ("fox_out", DB, plain_src(fox_out)),
            ("gdn_in", 4 * DB + 1, gdn_src()),
            ("gdn_out", DB, plain_src(gdn_out)),
            ("swa_in", 20, swa_src()),
            ("swa_out", DB, plain_src(swa_out)),
        ]
        swa_out_halves = swa_out.rearrange("(h d) n -> d h n", d=HD)

        sources = {s[0]: s[2] for s in stages}
        tile_stage, first = [], {}
        loaded_at, slot_count = [], [0] * RAW
        for name, n, src in stages:
            first[name] = len(tile_stage)
            for k in range(n):
                slot = len(tile_stage) % RAW
                n_dma = 4 if name == "swa_out" else len(src(k // 4, k % 4))
                slot_count[slot] += 16 * n_dma
                loaded_at.append(slot_count[slot])
                if name == "ple" and k % 2:
                    kb = PLE // P
                elif name.endswith("_down"):
                    kb = min(WB, FB - WB * (k % DOWN))
                else:
                    kb = DB
                tile_stage.append((name, k, kb))
        n_tiles = len(tile_stage)
        tiles_of = {s[0]: s[1] for s in stages}

        h = sb("h", [P, DB, SEQ])
        xh = sb("xh", [P, DB, SEQ], F32R)
        xl = sb("xl", [P, DB, SEQ], F32R)
        F = sb("F", [P, DB, SEQ])
        raw = [sb(f"raw{s}", [P, WB, P]) for s in range(RAW)]
        wh = [sb(f"wh{s}", [P, WB, P], F32R) for s in range(SPLIT)]
        wl = [sb(f"wl{s}", [P, WB, P], F32R) for s in range(SPLIT)]
        acc = sb("acc", [P, SEQ])
        sq = sb("sq", [P, 2, SEQ])
        rcol = sb("rms_col", [P, TB])
        rstd = sb("rstd", [P, SEQ])
        ident = sb("ident", [P, P])
        ones = sb("ones", [P, P])
        vA = sb("vA", [P, P])
        vB = sb("vB", [P, 97])
        half = sb("half", [P, 2, DB])
        ps = [top.enter_context(nc.psum_tensor(f"ps{b}", [P, SEQ], F32)) for b in range(8)]
        STAT = 7

        loaded = [sem(f"loaded{s}") for s in range(RAW)]
        hi_done, lo_done, tile_done = sem("hi_done"), sem("lo_done"), sem("tile_done")

        def wait(eng, s, v):
            if not isinstance(v, int) or v > 0:
                eng.wait_ge(s, v)

        def load(sp, name, i, j, k_ahead=0, split_at=None):
            t0 = first[name]
            if isinstance(i, int):
                t = t0 + 4 * i + j + k_ahead
                if t >= n_tiles:
                    return
                name, k, kb = tile_stage[t]
                i, j = k // 4, k % 4
                slot = t % RAW
            else:
                j += k_ahead
                slot, kb = (t0 + j) % RAW, tile_stage[t0 + j][2]
                i, j = i + j // 4, j % 4
            if name == "swa_out":
                if split_at is not None:
                    sp.wait_ge(lo_done, split_at)
                n0 = (4 * i + j) * P
                for kvp in range(2):
                    for upper in range(2):
                        h0 = 8 * kvp + 4 * upper
                        sp.dma_start(raw[slot][upper * HD:upper * HD + HD, 4 * kvp:4 * kvp + 4, :],
                                     swa_out_halves[:, h0:h0 + 4, n0:n0 + P]).then_inc(loaded[slot], 16)
                return
            parts = [(c0, w, view, c if isinstance(c, int) else sp.snap(c)) for c0, w, view, c in sources[name](i, j)]
            if split_at is not None:
                sp.wait_ge(lo_done, split_at)
            for c0, w, view, c in parts:
                sp.dma_start(raw[slot][:, 0:kb, c0:c0 + w], view[:, :, bass.ds(c, w)]).then_inc(loaded[slot], 16)

        def tile_at(name, i, j, ahead):
            t0 = first[name]
            if isinstance(i, int):
                t = t0 + 4 * i + j + ahead
                if t >= n_tiles:
                    return None
                return t % RAW, t % SPLIT, tile_stage[t][2], t, loaded_at[t]
            s = t0 + j + ahead
            return s % RAW, s % SPLIT, tile_stage[s][2], i * 4 + s, i * 16 + loaded_at[s]

        def split_hi(act, name, i, j, ahead=HEAD):
            at = tile_at(name, i, j, ahead)
            if at is None:
                return
            r, s, kb, t, got = at
            act.wait_ge(loaded[r], got)
            wait(act, tile_done, t - SPLIT + 1)
            nc.scalar.activation(wh[s][:, 0:kb, :], raw[r][:, 0:kb, :], ACT.Copy).then_inc(hi_done, 1)

        def split_lo(dve, name, i, j, ahead=HEAD):
            at = tile_at(name, i, j, ahead)
            if at is None:
                return
            r, s, kb, t, got = at
            dve.wait_ge(loaded[r], got)
            dve.wait_ge(hi_done, t + 1)
            nc.vector.tensor_tensor(wl[s][:, 0:kb, :], raw[r][:, 0:kb, :], wh[s][:, 0:kb, :].bitcast(F32),
                                    ALU.subtract).then_inc(lo_done, 1)

        def load_steps(sp, name, loop_end=None, beside=None):
            def body(i, j):
                load(sp, name, i, j, RAW, i * 4 + (first[name] + j + 1))
                if beside is not None and isinstance(i, int):
                    beside(sp, 4 * i + j)
            steps(sp, name, body, None if loop_end is None else loop_end - 1)

        def steps(eng, name, body, loop_end=None):
            n = tiles_of[name]
            full = n // 4
            if full < 4 or name == "swa_in" or name.endswith("_down"):
                for k in range(n):
                    body(k // 4, k % 4)
                return
            for j in range(4):
                body(0, j)
            end = full - 1 if loop_end is None else loop_end
            with eng.Fori(1, end) as i:
                for j in range(4):
                    body(i, j)
            for k in range(4 * end, n):
                body(k // 4, k % 4)

        def mm3(pe, o, s, kb, x_hi, x_lo, start, stop):
            pe.matmul(o, wh[s][:, kb, :], x_hi, start=start, stop=False)
            pe.matmul(o, wh[s][:, kb, :], x_lo, start=False, stop=False)
            return pe.matmul(o, wl[s][:, kb, :], x_hi, start=False, stop=stop)

        xs_hi, xs_lo = sem("x_hi_done"), sem("x_lo_done")
        h_new = sem("h_new")
        f_scaled = sem("f_scaled")
        sq_done, acc_done = sem("sq_done"), sem("acc_done")
        stat_mm, ms_done, inv_done, root_done = sem("stat_mm"), sem("ms_done"), sem("inv_done"), sem("root_done")
        spread, rstd_done = sem("rstd_spread"), sem("rstd_done")
        evac = sem("psum_evacuated")
        n = dict(x=0, h=0, fs=0, sq=0, acc=0, stat=0, ev=0, units=0, groups=0, lots=0, ffn=0)

        def sums_pe(pe, acc_at, sq_at):
            pe.wait_ge(acc_done, acc_at)
            pe.wait_ge(sq_done, sq_at)
            for t in range(TB):
                pe.matmul(ps[STAT][:, t:t + 1], acc[:, t * P:t * P + P], ones[:, 0:1], start=True, stop=False)
                m = pe.matmul(ps[STAT][:, t:t + 1], sq[:, 1, t * P:t * P + P], ones[:, 0:1], start=False, stop=True)
            m.then_inc(stat_mm, 1)

        def inverse_dve(dve, at, width):
            dve.wait_ge(stat_mm, at + 1)
            nc.vector.tensor_scalar(rcol[:, :], ps[STAT][:, 0:TB], 1.0 / width, EPS, ALU.mult, ALU.add).then_inc(ms_done, 1)
            dve.wait_ge(ms_done, at + 1)
            nc.vector.reciprocal(rcol[:, :], rcol[:, :]).then_inc(inv_done, 1)

        def root_act(act, at):
            act.wait_ge(inv_done, at + 1)
            nc.scalar.activation(rcol[:, :], rcol[:, :], ACT.Sqrt).then_inc(root_done, 1)

        def spread_pe(pe, at):
            pe.wait_ge(root_done, at + 1)
            for t in range(TB):
                m = pe.matmul(ps[STAT][:, t * P:t * P + P], rcol[:, t:t + 1].broadcast_to([P, P]), ident[:, :],
                              start=True, stop=True)
            m.then_inc(spread, 1)

        def rstd_dve(dve, at):
            dve.wait_ge(spread, at + 1)
            nc.vector.tensor_copy(rstd[:, :], ps[STAT][:, :]).then_inc(rstd_done, 1)

        class Prologue:

            def __init__(self, gain=None, update=None, squares=True):
                self.gain, self.update, self.squares = gain, update, squares
                self.x0, self.h0, self.fs0 = n["x"], n["h"], n["fs"]
                self.sq0, self.acc0, self.stat0 = n["sq"], n["acc"], n["stat"]
                n["x"] += DB
                if update is not None:
                    n["h"] += DB
                    n["fs"] += DB
                if squares:
                    n["sq"] += DB
                    n["acc"] += DB - 1
                self.sums = (n["acc"], n["sq"])

            def act(self, act, at_2=None):
                for b in range(DB):
                    if b == 2 and at_2 is not None:
                        at_2(act)
                    if self.update is not None:
                        act.wait_ge(h_new, self.h0 + b + 1)
                    g = 1.0 if self.gain is None else self.gain[:, b:b + 1]
                    nc.scalar.activation(xh[:, b, :], h[:, b, :], ACT.Copy, scale=g).then_inc(xs_hi, 1)
                    if self.squares:
                        if b >= 2:
                            act.wait_ge(acc_done, self.acc0 + b - 1)
                        nc.scalar.activation(sq[:, b % 2, :], h[:, b, :], ACT.Square).then_inc(sq_done, 1)

            def dve(self, dve, at_2=None):
                for b in range(DB):
                    if b == 2 and at_2 is not None:
                        at_2(dve)
                    if self.update is not None:
                        nc.vector.tensor_tensor(F[:, b, :], F[:, b, :], rstd[:, :], ALU.mult).then_inc(f_scaled, 1)
                        dve.wait_ge(f_scaled, self.fs0 + b + 1)
                        nc.vector.scalar_tensor_tensor(out=h[:, b, :], in0=F[:, b, :], scalar=self.update[:, b:b + 1],
                                                       in1=h[:, b, :], op0=ALU.mult, op1=ALU.add).then_inc(h_new, 1)
                        if b == 0:
                            continue
                        self.low(dve, b - 1)
                    else:
                        self.low(dve, b)
                if self.update is not None:
                    self.low(dve, DB - 1)

            def low(self, dve, b):
                dve.wait_ge(xs_hi, self.x0 + b + 1)
                if self.gain is None:
                    nc.vector.tensor_tensor(xl[:, b, :], h[:, b, :], xh[:, b, :].bitcast(F32),
                                            ALU.subtract).then_inc(xs_lo, 1)
                else:
                    nc.vector.scalar_tensor_tensor(out=xl[:, b, :], in0=h[:, b, :], scalar=self.gain[:, b:b + 1],
                                                   in1=xh[:, b, :].bitcast(F32), op0=ALU.mult,
                                                   op1=ALU.subtract).then_inc(xs_lo, 1)

            def pool(self, pool):
                if self.squares:
                    sum_squares(pool, self.sq0, self.acc0)

        def sum_squares(pool, sq0, acc0):
            for b in range(DB - 1):
                pool.wait_ge(sq_done, sq0 + b + 1)
                if b == 0:
                    nc.gpsimd.tensor_copy(acc[:, :], sq[:, 0, :]).then_inc(acc_done, 1)
                else:
                    pool.wait_ge(acc_done, acc0 + b)
                    nc.gpsimd.tensor_tensor(acc[:, :], acc[:, :], sq[:, b % 2, :], ALU.add).then_inc(acc_done, 1)

        def output_of(i, j, parts):
            if parts == 1:
                return i * 4 + j, j, 0
            k = 4 * i + j
            return k // parts, k // parts % 4, k % parts

        def pe_tiles(pe, name, x_hi, x_lo, ev0, x_ready=None, parts=1, sums=None, at=None,
                     beside=None, loop_end=None, x_pe=None):
            def body(i, j):
                r, s, kb, t, got = tile_at(name, i, j, 0)
                o, bank, part = output_of(i, j, parts)
                first_i = isinstance(i, int) and i == 0
                if first_i and x_ready is not None and j < HEAD:
                    if j:
                        return
                    pe.wait_ge(lo_done, t + HEAD)
                    for b in range(kb):
                        if at is not None and sums is None and b == 2:
                            spread_pe(pe, at)
                        if x_pe is not None:
                            x_pe(pe, b)
                        pe.wait_ge(xs_lo, x_ready + b + 1)
                        for g in range(HEAD):
                            last = mm3(pe, ps[g][:, :], (t + g) % SPLIT, b, x_hi[:, b, :], x_lo[:, b, :],
                                       b == 0, b == kb - 1)
                            if b == kb - 1:
                                last.then_inc(tile_done, 1)
                    if sums is not None:
                        sums_pe(pe, *sums)
                    return
                pe.wait_ge(lo_done, t + 1)
                if part == 0:
                    wait(pe, evac, ev0 + o - 3)
                for b in range(kb):
                    if first_i and j == HEAD and b == 2 and sums is not None:
                        spread_pe(pe, at)
                    xb = part * WB + b
                    last = mm3(pe, ps[bank][:, :], s, b, x_hi[:, xb, :], x_lo[:, xb, :],
                               xb == 0, part == parts - 1 and b == kb - 1)
                last.then_inc(tile_done, 1)
                if beside is not None and isinstance(i, int):
                    beside(pe, 4 * i + j)
            steps(pe, name, body, loop_end)

        def in_proj(name, gain, dst, update=None, sums=None, tails=(), evac_dve=None, evac_act=None, loop_end=None,
                    beside=(), between_dve=None):
            pro = Prologue(gain, update, squares=sums is None)
            st = n["stat"]
            n["stat"] += 1
            ev0 = n["ev"]
            n["ev"] += tiles_of[name]
            t0 = first[name]
            tails, beside = dict(tails), dict(beside)
            with nc.Block() as block:
                @block.sync
                def _(sp):
                    if "sp" in tails:
                        tails["sp"](sp)
                    load_steps(sp, name, loop_end, beside.get("sp"))

                @block.gpsimd
                def _(pool):
                    pro.pool(pool)
                    if "pool" in tails:
                        tails["pool"](pool)

                @block.scalar
                def _(act):
                    if sums is not None:
                        root_act(act, st)
                    pro.act(act)
                    if "act_start" in beside:
                        beside["act_start"](act)

                    def body(i, j):
                        split_hi(act, name, i, j)
                        if sums is None and isinstance(i, int) and i == 0 and j == 0:
                            root_act(act, st)
                        if evac_act is not None:
                            evac_act(act, i, j, ev0)
                        if "act" in beside and isinstance(i, int):
                            beside["act"](act, 4 * i + j)
                    steps(act, name, body, loop_end)
                    if "act" in tails:
                        tails["act"](act, ev0)

                @block.vector
                def _(dve):
                    if sums is not None:
                        inverse_dve(dve, st, D)
                    pro.dve(dve, (lambda e: rstd_dve(e, st)) if sums is not None else None)
                    if "dve_start" in beside:
                        beside["dve_start"](dve)

                    def body(i, j):
                        if between_dve is not None:
                            between_dve(dve, i, j, 1)
                        split_lo(dve, name, i, j)
                        if between_dve is not None:
                            between_dve(dve, i, j, 2)
                        if isinstance(i, int) and i == 0 and j == 0:
                            if sums is None:
                                inverse_dve(dve, st, D)
                                rstd_dve(dve, st)
                            dve.wait_ge(rstd_done, st + 1)
                        dve.wait_ge(tile_done, i * 4 + (t0 + j + 1))
                        if evac_dve is not None:
                            evac_dve(dve, i, j, ev0)
                        else:
                            k = i * 4 + j
                            nc.vector.tensor_tensor(dst[:, bass.ds(k, 1), :],
                                                    ps[j][:, :].rearrange("p (o q) -> p o q", o=1),
                                                    rstd[:, :].rearrange("p (o q) -> p o q", o=1), ALU.mult).then_inc(evac, 1)
                        if "dve" in beside and isinstance(i, int):
                            beside["dve"](dve, 4 * i + j)
                    steps(dve, name, body, loop_end)
                    if "dve" in tails:
                        tails["dve"](dve, ev0)

                @block.tensor
                def _(pe):
                    if sums is not None:
                        sums_pe(pe, *sums)
                    pe_tiles(pe, name, xh, xl, ev0, x_ready=pro.x0, sums=None if sums is not None else pro.sums, at=st,
                             beside=beside.get("pe"), loop_end=loop_end)
                    if "pe" in tails:
                        tails["pe"](pe, ev0)
            return ev0

        vec_rows = []
        for nm in ("g_ffn1_pre", "g_ffn1_post", "g_mix_pre", "g_mix_post", "g_ffn2_pre", "g_ffn2_post", "g_ple_post",
                   "g_out_sb", "g_out_ch", "norm_w_2", "final_norm_w_2", "conv_w_conv_2"):
            a = I[nm]
            if len(a.shape) == 1:
                v = a.rearrange("(r c) -> r c", c=P)
            elif len(a.shape) == 2:
                v = a.rearrange("a (r c) -> (a r) c", c=P)
            else:
                v = a.rearrange("a k (r c) -> (a k r) c", c=P)
            vec_rows.append((nm, v))
        col = {}
        at = 0
        for nm, v in vec_rows:
            col[nm] = at
            at += v.shape[0]
        assert at == P
        gdn_conv_rows = I["gdn_w_conv_2"].rearrange("a k (r c) -> (a k r) c", c=P)

        def gains(nm, first_=0, m=DB):
            return vA[:, col[nm] + first_:col[nm] + first_ + m]

        boot = ExitStack()
        with boot:
            xt = sb("xt", [P, TB, D], ctx=boot)
            vrow = sb("vrow", [P, 2, P], ctx=boot)
            vec_in, x_in = sem("vec_in"), sem("x_in")
            const = sem("const_ready")
            tr, tr_out, half_done = sem("boot_transposed"), sem("boot_copied"), sem("half_done")
            n_vec = 16 * (len(vec_rows) + 2)
            with nc.Block() as block:
                @block.sync
                def _(sp):
                    sp.dma_start(xt[:, :, :], I["x"][0].rearrange("(t p) d -> p t d", p=P)).then_inc(x_in, 16)
                    for nm, v in vec_rows:
                        sp.dma_start(vrow[col[nm]:col[nm] + v.shape[0], 0, :], v).then_inc(vec_in, 16)
                    sp.dma_start(vrow[0:96, 1, :], gdn_conv_rows).then_inc(vec_in, 16)
                    sp.dma_start(vrow[96:97, 1, :], I["gdn_norm_w_2"]).then_inc(vec_in, 16)
                    for k in range(RAW):
                        load(sp, "ffn1_up", 0, k)

                @block.gpsimd
                def _(pool):
                    nc.gpsimd.memset(ones[:, :], 1.0).then_inc(const, 1)
                    nc.gpsimd.memset(ident[:, :], 0.0).then_inc(const, 1)
                    pool.wait_ge(const, 2)
                    nc.gpsimd.affine_select(out=ident[:, :], in_=ident[:, :], compare_op=ALU.not_equal, fill=1.0,
                                            base=0, pattern=[[-1, P]], channel_multiplier=1).then_inc(const, 1)

                @block.tensor
                def _(pe):
                    pe.wait_ge(const, 3)
                    pe.wait_ge(x_in, 16)
                    for b in range(DB):
                        if b >= 4:
                            pe.wait_ge(tr_out, b - 3)
                        for t in range(TB):
                            m = pe.transpose(ps[b % 4][:, t * P:t * P + P], xt[:, t, b * P:b * P + P], ident[:, :])
                        m.then_inc(tr, 1)
                    pe.wait_ge(vec_in, n_vec)
                    pe.transpose(ps[4][:, 0:P], vrow[:, 0, :], ident[:, :]).then_inc(tr, 1)
                    pe.transpose(ps[5][:, 0:97], vrow[0:97, 1, :], ident[0:97, 0:97]).then_inc(tr, 1)

                @block.vector
                def _(dve):
                    for b in range(DB):
                        dve.wait_ge(tr, b + 1)
                        nc.vector.tensor_copy(h[:, b, :], ps[b % 4][:, :]).then_inc(tr_out, 1)
                    dve.wait_ge(tr, DB + 1)
                    nc.vector.tensor_copy(vA[:, :], ps[4][:, 0:P]).then_inc(tr_out, 1)
                    dve.wait_ge(tr, DB + 2)
                    nc.vector.tensor_copy(vB[:, :], ps[5][:, 0:97]).then_inc(tr_out, 1)
                    dve.wait_ge(tr_out, DB + 1)
                    nc.vector.tensor_scalar(half[:, 0, :], gains("g_ffn1_post"), 0.5, None, ALU.mult).then_inc(half_done, 1)
                    nc.vector.tensor_scalar(half[:, 1, :], gains("g_ffn2_post"), 0.5, None, ALU.mult).then_inc(half_done, 1)
                    for k in range(HEAD):
                        split_lo(dve, "ffn1_up", 0, k, 0)

                @block.scalar
                def _(act):
                    for k in range(HEAD):
                        split_hi(act, "ffn1_up", 0, k, 0)

        g_done, silu_done, sr_done, prod, up_hi = (sem(f"ffn_{x}") for x in ("gate", "silu", "silur", "prod", "ahi"))

        def ffn_up(name, gain, update, act_hi, act_lo, ctx):
            S = F[:, 0:2, :]
            SR = F[:, 2:4, :]
            p0 = n["ffn"]
            n["ffn"] += FB
            pro = Prologue(gain, update)
            st = n["stat"]
            n["stat"] += 1
            ev0 = n["ev"]
            n["ev"] += 2 * FB
            t0 = first[name]
            with nc.Block() as block:
                @block.sync
                def _(sp):
                    load_steps(sp, name)

                @block.gpsimd
                def _(pool):
                    pro.pool(pool)

                    def body(i, j):
                        if j % 2 == 1:
                            p, s = i * 2 + j // 2, (j // 2) % 2
                            pool.wait_ge(silu_done, p + (p0 + 1))
                            wait(pool, prod, p + (p0 - 1))
                            nc.gpsimd.tensor_tensor(SR[:, s, :], S[:, s, :], rstd[:, :], ALU.mult).then_inc(sr_done, 1)
                    steps(pool, name, body)

                @block.scalar
                def _(act):
                    pro.act(act)

                    def body(i, j):
                        split_hi(act, name, i, j)
                        if isinstance(i, int) and i == 0 and j == 0:
                            root_act(act, st)
                        p, s = i * 2 + j // 2, (j // 2) % 2
                        if j % 2 == 0:
                            act.wait_ge(g_done, p + (p0 + 1))
                            wait(act, sr_done, p + (p0 - 1))
                            nc.scalar.activation(S[:, s, :], ps[j][:, :], ACT.Silu).then_inc(silu_done, 1)
                        else:
                            act.wait_ge(prod, p + (p0 + 1))
                            nc.scalar.activation(act_hi[:, bass.ds(p, 1), :], ps[j][:, :].rearrange("p (o q) -> p o q", o=1),
                                                 ACT.Copy).then_inc(up_hi, 1)
                    steps(act, name, body)

                @block.vector
                def _(dve):
                    pro.dve(dve)

                    def body(i, j):
                        split_lo(dve, name, i, j)
                        if isinstance(i, int) and i == 0 and j == 0:
                            inverse_dve(dve, st, D)
                            rstd_dve(dve, st)
                            dve.wait_ge(rstd_done, st + 1)
                        p, s = i * 2 + j // 2, (j // 2) % 2
                        dve.wait_ge(tile_done, i * 4 + (t0 + j + 1))
                        if j % 2 == 0:
                            nc.vector.tensor_tensor(ps[j][:, :], ps[j][:, :], rstd[:, :], ALU.mult).then_inc(g_done, 1)
                        else:
                            dve.wait_ge(sr_done, p + (p0 + 1))
                            nc.vector.tensor_tensor(ps[j][:, :], ps[j][:, :], SR[:, s, :], ALU.mult).then_inc(prod, 1)
                            dve.wait_ge(up_hi, p + (p0 + 1))
                            nc.vector.tensor_tensor(act_lo[:, bass.ds(p, 1), :], ps[j][:, :].rearrange("p (o q) -> p o q", o=1),
                                                    act_hi[:, bass.ds(p, 1), :].bitcast(F32), ALU.subtract).then_inc(evac, 2)
                    steps(dve, name, body)

                @block.tensor
                def _(pe):
                    pe_tiles(pe, name, xh, xl, ev0, x_ready=pro.x0, sums=pro.sums, at=st)

        def post_out(name, x_hi, x_lo, parts=1, x=None):
            x_act, x_dve, x_pe = (None, None, None) if x is None else x
            x_ready = None if x is None else n["x"] - DB
            ev0, sq0, acc0, st = n["ev"], n["sq"], n["acc"], n["stat"]
            n["ev"] += DB
            n["sq"] += DB
            n["acc"] += DB - 1
            n["stat"] += 1
            t0 = first[name]
            with nc.Block() as block:
                @block.sync
                def _(sp):
                    load_steps(sp, name)

                @block.gpsimd
                def _(pool):
                    sum_squares(pool, sq0, acc0)

                @block.scalar
                def _(act):
                    if x_act is not None:
                        x_act(act)

                    def body(i, j):
                        split_hi(act, name, i, j)
                        o, bank, part = output_of(i, j, parts)
                        if part == parts - 1:
                            act.wait_ge(tile_done, i * 4 + (t0 + j + 1))
                            wait(act, acc_done, acc0 + o - 1 if not (isinstance(o, int) and o < 2) else 0)
                            nc.scalar.activation(sq[:, bank % 2, :], ps[bank][:, :], ACT.Square).then_inc(sq_done, 1)
                            nc.scalar.activation(F[:, o:o + 1, :] if isinstance(o, int) else F[:, bass.ds(o, 1), :],
                                                 ps[bank][:, :].rearrange("p (o q) -> p o q", o=1), ACT.Copy).then_inc(evac, 1)
                    steps(act, name, body)
                    root_act(act, st)

                @block.vector
                def _(dve):
                    if x_dve is not None:
                        x_dve(dve)

                    def body(i, j):
                        split_lo(dve, name, i, j)
                    steps(dve, name, body)
                    inverse_dve(dve, st, D)
                    rstd_dve(dve, st)

                @block.tensor
                def _(pe):
                    pe_tiles(pe, name, x_hi, x_lo, ev0, x_ready=x_ready, parts=parts, x_pe=x_pe)
                    sums_pe(pe, acc0 + DB - 1, sq0 + DB)
                    spread_pe(pe, st)

        def resid_out(name, x_act, x_dve, x_pe=None):
            ev0, sq0, acc0 = n["ev"], n["sq"], n["acc"]
            n["ev"] += DB
            n["sq"] += DB
            n["acc"] += DB - 1
            t0 = first[name]
            x_ready = n["x"] - DB
            with nc.Block() as block:
                @block.sync
                def _(sp):
                    load_steps(sp, name)

                @block.gpsimd
                def _(pool):
                    sum_squares(pool, sq0, acc0)

                @block.scalar
                def _(act):
                    x_act(act)

                    def body(i, j):
                        k = 4 * i + j
                        split_hi(act, name, i, j)
                        act.wait_ge(evac, ev0 + k + 1)
                        wait(act, acc_done, acc0 + k - 1 if k >= 2 else 0)
                        nc.scalar.activation(sq[:, k % 2, :], h[:, k, :], ACT.Square).then_inc(sq_done, 1)
                    steps(act, name, body)

                @block.vector
                def _(dve):
                    x_dve(dve)

                    def body(i, j):
                        k = 4 * i + j
                        split_lo(dve, name, i, j)
                        dve.wait_ge(tile_done, t0 + k + 1)
                        nc.vector.tensor_tensor(h[:, k, :], ps[j][:, :], h[:, k, :], ALU.add).then_inc(evac, 1)
                    steps(dve, name, body)

                @block.tensor
                def _(pe):
                    pe_tiles(pe, name, xh, xl, ev0, x_ready=x_ready, x_pe=x_pe)
            return acc0 + DB - 1, sq0 + DB

        def split_x(src):
            x0 = n["x"]
            n["x"] += DB

            def x_act(act):
                for b in range(DB):
                    nc.scalar.activation(xh[:, b, :], src(b), ACT.Copy).then_inc(xs_hi, 1)

            def x_dve(dve):
                for b in range(DB):
                    dve.wait_ge(xs_hi, x0 + b + 1)
                    nc.vector.tensor_tensor(xl[:, b, :], src(b), xh[:, b, :].bitcast(F32), ALU.subtract).then_inc(xs_lo, 1)
            return x_act, x_dve

        def gate_x(zb):
            x0, f0 = n["x"], n["fs"]
            n["x"] += DB
            n["fs"] += DB

            def x_act(act):
                for b in range(DB):
                    act.wait_ge(f_scaled, f0 + b + 1)
                    nc.scalar.activation(xh[:, b, :], F[:, b, :], ACT.Copy).then_inc(xs_hi, 1)

            def x_dve(dve):
                for b in range(DB + 1):
                    if b < DB:
                        nc.vector.tensor_tensor(F[:, b, :], F[:, b, :], zb(b), ALU.mult).then_inc(f_scaled, 1)
                    if b >= 1:
                        dve.wait_ge(xs_hi, x0 + b)
                        nc.vector.tensor_tensor(xl[:, b - 1, :], F[:, b - 1, :], xh[:, b - 1, :].bitcast(F32),
                                                ALU.subtract).then_inc(xs_lo, 1)
            return x_act, x_dve

        def final(sums):
            ot = ExitStack()
            with ot:
                fo = sb("final_o", [P, DB, SEQ], ctx=ot)
                res = sb("final_res", [P, TB, D], ctx=ot)
                fr, fs, ft, fe, stored = (sem(f"final_{x}") for x in ("scaled", "gained", "transposed", "copied", "stored"))
                st = n["stat"]
                n["stat"] += 1
                g = gains("final_norm_w_2")
                with nc.Block() as block:
                    @block.tensor
                    def _(pe):
                        sums_pe(pe, *sums)
                        spread_pe(pe, st)
                        for t in range(TB):
                            for b in range(2):
                                q = 2 * t + b
                                if q >= 4:
                                    pe.wait_ge(fe, q - 3)
                                for c in range(4):
                                    if t == 0:
                                        pe.wait_ge(fs, 4 * b + c + 1)
                                    m = pe.transpose(ps[q % 4][:, c * P:c * P + P],
                                                     fo[:, 4 * b + c, t * P:t * P + P], ident[:, :])
                                m.then_inc(ft, 1)

                    @block.vector
                    def _(dve):
                        inverse_dve(dve, st, D)
                        rstd_dve(dve, st)
                        dve.wait_ge(rstd_done, st + 1)
                        for b in range(DB):
                            nc.vector.tensor_tensor(fo[:, b, :], h[:, b, :], rstd[:, :], ALU.mult).then_inc(fr, 1)
                        for q in range(2 * TB):
                            dve.wait_ge(ft, q + 1)
                            nc.vector.tensor_copy(res[:, q // 2, (q % 2) * SEQ:(q % 2) * SEQ + SEQ], ps[q % 4][:, :]).then_inc(fe, 1)

                    @block.scalar
                    def _(act):
                        root_act(act, st)
                        for b in range(DB):
                            act.wait_ge(fr, b + 1)
                            nc.scalar.activation(fo[:, b, :], fo[:, b, :], ACT.Copy,
                                                 scale=g[:, b:b + 1]).then_inc(fs, 1)

                    @block.sync
                    def _(sp):
                        for t in range(TB):
                            sp.wait_ge(fe, 2 * t + 2)
                            sp.dma_start(out[0, t * P:t * P + P, :], res[:, t, :]).then_inc(stored, 16)
                        sp.wait_ge(stored, 16 * TB)

        with ExitStack() as c:
            a_hi = sb("a_hi1", [P, FB, SEQ], F32R, ctx=c)
            a_lo = sb("a_lo1", [P, FB, SEQ], F32R, ctx=c)
            with ExitStack() as c2:
                ffn_up("ffn1_up", gains("g_ffn1_pre"), None, a_hi, a_lo, c2)
            post_out("ffn1_down", a_hi, a_lo, DOWN)

        turned, taken = sem("values_turned"), sem("values_taken")

        def token_turn(v_of, blocks, dst, v_ready, bank=4):
            lots = [(t, g) for g in range(-(-blocks // 4)) for t in range(TB)]
            q00 = n["lots"]
            n["lots"] += len(lots)

            def pe_part(pe, q0=0, q1=len(lots)):
                for q in range(q0, q1):
                    t, g = lots[q]
                    if q == 0 or lots[q - 1][1] != g:
                        pe.wait_ge(*v_ready(min(4 * g + 4, blocks) - 1))
                    if q >= 2:
                        pe.wait_ge(taken, q00 + q - 1)
                    for b in range(4 * g, min(4 * g + 4, blocks)):
                        m = pe.transpose(ps[bank + q % 2][:, (b % 4) * P:(b % 4) * P + P],
                                         v_of(b)[:, t * P:t * P + P], ident[:, :])
                    m.then_inc(turned, 1)

            def dve_part(dve, q0=0, q1=len(lots)):
                for q in range(q0, q1):
                    t, g = lots[q]
                    w = (min(4 * g + 4, blocks) - 4 * g) * P
                    dve.wait_ge(turned, q00 + q + 1)
                    nc.vector.tensor_copy(dst[:, t, g * 4 * P:g * 4 * P + w], ps[bank + q % 2][:, 0:w]).then_inc(taken, 1)
            return pe_part, dve_part

        (scored, z_done, nm_done, p_done, ri_done, p_scaled, t_done, pt_done, pv_done, o_taken) = (
            sem(f"att_{x}") for x in ("scored", "z", "negmax", "exp", "inv", "scaled", "turned", "pt", "pv", "otaken"))
        e_sink, den_done = sem("att_expsink"), sem("att_den")

        def softmax_attention(name, units, groups, room, ctx):
            U = len(units)
            Z, PT = room[:, 0:4, :], room[:, 4:6, :]
            cols = sb(f"{name}_cols", [P, 5, U], ctx=ctx)
            MX, NM, RS, RI, ES = range(5)
            B, BG = n["units"], n["groups"]
            n["units"] += U
            n["groups"] += len(groups)
            sinks = units[0].get("sink") is not None
            group_of, start = {}, 0
            for g, (last, _, _) in enumerate(groups):
                for u in range(start, last + 1):
                    group_of[u] = g
                start = last + 1
            last_of = {last: g for g, (last, _, _) in enumerate(groups)}

            def pe_part(pe):
                for s in range(U + 3):
                    if s < U:
                        u, d = s, units[s]
                        if u >= 3:
                            pe.wait_ge(z_done, B + u - 2)
                        o = ps[u % 3][:, 0:d["klen"]]
                        m = pe.matmul(o, d["q"], d["k"], start=True, stop=not d["add"])
                        for x, (a, b) in enumerate(d["add"]):
                            m = pe.matmul(o, a, b, start=False, stop=x == len(d["add"]) - 1)
                        m.then_inc(scored, 1)
                    if 2 <= s < U + 2:
                        u, d = s - 2, units[s - 2]
                        pe.wait_ge(p_scaled, B + u + 1)
                        if u >= 2:
                            pe.wait_ge(pt_done, B + u - 1)
                        for x in range(d["klen"] // P):
                            m = pe.transpose(ps[3 + u % 2][:, x * P:x * P + P], Z[:, u % 4, x * P:x * P + P], ident[:, :])
                        m.then_inc(t_done, 1)
                    if s >= 3:
                        u, d = s - 3, units[s - 3]
                        g = group_of[u]
                        pe.wait_ge(pt_done, B + u + 1)
                        if g >= 2:
                            pe.wait_ge(o_taken, BG + g - 1)
                        o = ps[5 + g % 2][d["po"]:d["po"] + d["m"], d["oc"]:d["oc"] + P]
                        nk = d["klen"] // P
                        for x in range(nk):
                            m = pe.matmul(o, d["v"][x], PT[:, u % 2, x * P:x * P + P], start=x == 0, stop=x == nk - 1)
                        m.then_inc(pv_done, 1)

            def dve_part(dve):
                for s in range(U + 5):
                    if s < U:
                        u, d = s, units[s]
                        dve.wait_ge(scored, B + u + 1)
                        if u >= 4:
                            dve.wait_ge(t_done, B + u - 3)
                        nc.vector.tensor_tensor_reduce(Z[:, u % 4, 0:d["klen"]], ps[u % 3][:, 0:d["klen"]], d["mask"],
                                                       1.0, NEG, ALU.add, ALU.max, cols[:, MX, u:u + 1]).then_inc(z_done, 1)
                        dve.wait_ge(z_done, B + u + 1)
                        if sinks:
                            nc.vector.tensor_scalar(cols[:, NM, u:u + 1], cols[:, MX, u:u + 1], d["sink"], -1.0,
                                                    ALU.max, ALU.mult).then_inc(nm_done, 1)
                        else:
                            nc.vector.tensor_scalar(cols[:, NM, u:u + 1], cols[:, MX, u:u + 1], -1.0, None,
                                                    ALU.mult).then_inc(nm_done, 1)
                    if 1 <= s < U + 1:
                        u, d = s - 1, units[s - 1]
                        dve.wait_ge(p_done, B + u + 1)
                        den = cols[:, RS, u:u + 1]
                        if sinks:
                            dve.wait_ge(e_sink, u + 1)
                            nc.vector.tensor_tensor(den, den, cols[:, ES, u:u + 1], ALU.add).then_inc(den_done, 1)
                            dve.wait_ge(den_done, u + 1)
                        nc.vector.reciprocal(cols[:, RI, u:u + 1], den).then_inc(ri_done, 1)
                        dve.wait_ge(ri_done, B + u + 1)
                        nc.vector.tensor_scalar(Z[:, u % 4, 0:d["klen"]], Z[:, u % 4, 0:d["klen"]], cols[:, RI, u:u + 1],
                                                None, ALU.mult).then_inc(p_scaled, 1)
                    if s - 4 in last_of:
                        g = last_of[s - 4]
                        dve.wait_ge(pv_done, B + s - 3)
                        nc.vector.tensor_copy(groups[g][1], groups[g][2](ps[5 + g % 2])).then_inc(o_taken, 1)

            def act_part(act):
                for s in range(U + 2):
                    if s < U:
                        u, d = s, units[s]
                        act.wait_ge(nm_done, B + u + 1)
                        z = Z[:, u % 4, 0:d["klen"]]
                        nc.scalar.activation(z, z, ACT.Exp, bias=cols[:, NM, u:u + 1],
                                             accum_out=cols[:, RS, u:u + 1]).then_inc(p_done, 1)
                        if sinks:
                            nc.scalar.activation(cols[:, ES, u:u + 1], d["sink"], ACT.Exp,
                                                 bias=cols[:, NM, u:u + 1]).then_inc(e_sink, 1)
                    if s >= 2:
                        u, d = s - 2, units[s - 2]
                        act.wait_ge(t_done, B + u + 1)
                        if u >= 2:
                            act.wait_ge(pv_done, B + u - 1)
                        nc.scalar.activation(PT[:, u % 2, 0:d["klen"]], ps[3 + u % 2][:, 0:d["klen"]],
                                             ACT.Copy).then_inc(pt_done, 1)
            return pe_part, dve_part, act_part

        with ExitStack() as c:
            qkv = sb("qkv", [P, 24, SEQ], ctx=c)
            va = sb("va", [P, TB, 4 * P], ctx=c)
            vb = sb("vb", [P, TB, 4 * P], ctx=c)
            bias = sb("bias", [P, H8, SEQ], ctx=c)
            scratch = nc.dram_tensor("bias_rows", (H8, P, BAND_W), F32, kind="Internal").ap()
            q_scaled = sem("q_scaled")
            b_in, b_rev, b_out, b_back, b_mask = (sem(f"bias_{x}") for x in ("in", "reversed", "out", "back", "masked"))
            ev_mix = n["ev"]
            turn_a = token_turn(lambda b: qkv[:, 8 + b, :], 4, va, lambda b: (evac, ev_mix + 8 + b + 1))
            turn_b = token_turn(lambda b: qkv[:, 20 + b, :], 4, vb, lambda b: (evac, ev_mix + 16 + b + 1), 6)
            with ExitStack() as c2:
                rb = sb("rb", [H8, 2 * REL + 1], ctx=c2)
                ext = sb("ext", [H8, BAND_W], ctx=c2)
                far = BAND_W - 2 * REL

                def sp_beside(sp, k):
                    if k == 0:
                        sp.dma_start(rb[:, :], I["rel_bias"][0]).then_inc(b_in, 16)
                    if k != 3:
                        return
                    sp.wait_ge(b_rev, 2)
                    sp.dma_start(scratch, ext[:, :].rearrange("h (o n) -> h o n", o=1).broadcast_to([H8, P, BAND_W])).then_inc(b_out, 16)
                    sp.wait_ge(b_out, 16)
                    for hd in range(H8):
                        src = bass.AP(scratch.tensor, hd * P * BAND_W + P - 1, [[BAND_W - 1, P], [1, SEQ]])
                        sp.dma_start(bias[:, hd, :], src).then_inc(b_back, 16)

                def pool_tail(pool):
                    pool.wait_ge(b_in, 16)
                    nc.gpsimd.tensor_copy(ext[:, far:BAND_W], rb[:, 2 * REL - 1::-1]).then_inc(b_rev, 1)
                    nc.gpsimd.tensor_copy(ext[:, 0:far], rb[:, 2 * REL:2 * REL + 1].broadcast_to([H8, far])).then_inc(b_rev, 1)
                    pool.wait_ge(b_back, 16 * H8)
                    nc.gpsimd.memset(bias[0:HD, :, SEQ - HD:SEQ], NEG).then_inc(b_mask, 1)

                def mix_evac(dve, i, j, ev0):
                    k = mix_block(i, j)
                    nc.vector.tensor_tensor(qkv[:, bass.ds(k, 1), :], ps[j][:, :].rearrange("p (o q) -> p o q", o=1),
                                            rstd[:, :].rearrange("p (o q) -> p o q", o=1), ALU.mult).then_inc(evac, 1)

                def pe_beside(pe, k):
                    if k >= 16:
                        (turn_a if k < 20 else turn_b)[0](pe, k % 4, k % 4 + 1)

                def dve_beside(dve, k):
                    if k >= 16:
                        (turn_a if k < 20 else turn_b)[1](dve, k % 4, k % 4 + 1)
                    if k in (17, 18):
                        g = k - 17
                        dve.wait_ge(evac, ev_mix + 12 * g + 4)
                        q = qkv[:, 12 * g:12 * g + 4, :]
                        nc.vector.tensor_scalar(q, q, HD ** -0.5, None, ALU.mult).then_inc(q_scaled, 1)

                in_proj("mix_in", gains("g_mix_pre"), qkv, update=half[:, 0, :], evac_dve=mix_evac, loop_end=4,
                        tails=dict(pool=pool_tail), beside=dict(sp=sp_beside, pe=pe_beside, dve=dve_beside))
            with ExitStack() as c2:
                off = {3: 0, 2: P, 1: 3 * P, 0: 6 * P}
                wide = 10 * P
                SP_ = sb("softplus", [P, 2, wide], ctx=c2)
                A = sb("weights", [P, 2, wide], ctx=c2)
                tmp = qkv[:, 8:11, :]
                ntri, nones = sq[:, 0, 0:P], sq[:, 1, 0:P]
                (sbc, z_mm, abs_d, exp_d, ln_d, sp_raw, sp_d, c_mm, a_raw, a_d, av_mm, o_d) = (sem(f"sb_{x}") for x in (
                    "const", "z", "abs", "exp", "ln", "spraw", "sp", "c", "araw", "a", "av", "o"))
                units = [(hd, kb) for hd in range(H8) for kb in (3, 2, 1, 0)]
                U = len(units)
                ZB = 6

                with nc.Block() as block:
                    @block.gpsimd
                    def _(pool):
                        nc.gpsimd.memset(nones[:, :], -1.0).then_inc(sbc, 1)
                        pool.wait_ge(sbc, 1)
                        nc.gpsimd.affine_select(out=ntri[:, :], in_=nones[:, :], compare_op=ALU.is_ge, fill=0.0,
                                                base=0, pattern=[[-1, P]], channel_multiplier=1).then_inc(sbc, 1)
                        for s in range(U + 2):
                            if s < U:
                                hd, kb = units[s]
                                v = SP_[:, hd % 2, off[kb]:off[kb] + P]
                                pool.wait_ge(sp_raw, s + 1)
                                nc.gpsimd.affine_select(out=v, in_=v, compare_op=ALU.is_gt, fill=0.0, base=0,
                                                        pattern=[[1, P]], channel_multiplier=-1).then_inc(sp_d, 1)
                            if s >= 2:
                                hd, kb = units[s - 2]
                                v = A[:, hd % 2, off[kb]:off[kb] + P]
                                pool.wait_ge(a_raw, s - 1)
                                nc.gpsimd.affine_select(out=v, in_=v, compare_op=ALU.is_gt, fill=0.0, base=0,
                                                        pattern=[[1, P]], channel_multiplier=-1).then_inc(a_d, 1)

                    @block.tensor
                    def _(pe):
                        pe.wait_ge(sbc, 2)
                        for s in range(U + 4):
                            if s < U:
                                hd, kb = units[s]
                                po = HD * (hd % 2)
                                if s >= ZB:
                                    pe.wait_ge(a_raw, s - ZB + 1)
                                pe.matmul(ps[s % ZB][:, 0:SEQ - kb * P],
                                          qkv[po:po + HD, 4 + hd // 2, kb * P:kb * P + P],
                                          qkv[po:po + HD, hd // 2, kb * P:SEQ], start=True, stop=True).then_inc(z_mm, 1)
                            if 2 <= s < U + 2:
                                u = s - 2
                                hd, kb = units[u]
                                pe.wait_ge(sp_d, u + 1)
                                for k2 in range(kb, TB):
                                    m = pe.matmul(ps[u % ZB][:, (k2 - kb) * P:SEQ - kb * P], (ntri if k2 == kb else nones)[:, :],
                                                  SP_[:, hd % 2, off[k2]:off[k2] + SEQ - k2 * P],
                                                  start=False, stop=True, skip_group_check=True)
                                m.then_inc(c_mm, 1)
                            if s >= 4:
                                u = s - 4
                                hd, kb = units[u]
                                po, pair = HD * (hd % 2), hd // 2
                                pe.wait_ge(a_d, u + 1)
                                if kb == 3 and pair >= 2:
                                    pe.wait_ge(o_d, pair - 1)
                                pe.matmul(ps[6 + pair % 2][po:po + HD, kb * P:SEQ], va[:, kb, hd * HD:hd * HD + HD],
                                          A[:, hd % 2, off[kb]:off[kb] + SEQ - kb * P],
                                          start=kb == 3, stop=kb == 0, skip_group_check=True).then_inc(av_mm, 1)

                    @block.vector
                    def _(dve):
                        for s in range(U + 7):
                            if 1 <= s < U + 1:
                                u = s - 1
                                hd, kb = units[u]
                                w = SEQ - kb * P
                                dve.wait_ge(ln_d, u + 1)
                                if hd >= 2:
                                    dve.wait_ge(c_mm, 4 * (hd - 1))
                                nc.vector.scalar_tensor_tensor(out=SP_[:, hd % 2, off[kb]:off[kb] + w], in0=ps[u % ZB][:, 0:w],
                                                               scalar=0.0, in1=tmp[:, u % 3, 0:w], op0=ALU.max,
                                                               op1=ALU.add).then_inc(sp_raw, 1)
                            if s >= 7 and (s - 7) % 8 == 7:
                                pair = (s - 7) // 8
                                dve.wait_ge(av_mm, 8 * pair + 8)
                                nc.vector.tensor_copy(F[:, pair, :], ps[6 + pair % 2][:, :]).then_inc(o_d, 1)

                    @block.scalar
                    def _(act):
                        act.preload_act_table_set("natural_log_exp_and_others")
                        for s in range(U + 3):
                            if s < U:
                                hd, kb = units[s]
                                w = SEQ - kb * P
                                t = tmp[:, s % 3, 0:w]
                                act.wait_ge(z_mm, s + 1)
                                if s >= 3:
                                    act.wait_ge(sp_raw, s - 2)
                                nc.scalar.activation(t, ps[s % ZB][:, 0:w], ACT.Abs).then_inc(abs_d, 1)
                                act.wait_ge(abs_d, s + 1)
                                nc.scalar.activation(t, t, ACT.Exp, scale=-1.0).then_inc(exp_d, 1)
                                act.wait_ge(exp_d, s + 1)
                                nc.scalar.activation(t, t, ACT.Ln, bias=1.0).then_inc(ln_d, 1)
                            if s >= 3:
                                u = s - 3
                                hd, kb = units[u]
                                w = SEQ - kb * P
                                act.wait_ge(c_mm, u + 1)
                                if hd >= 2:
                                    act.wait_ge(av_mm, 4 * (hd - 1))
                                nc.scalar.activation(A[:, hd % 2, off[kb]:off[kb] + w], ps[u % ZB][:, 0:w],
                                                     ACT.Exp).then_inc(a_raw, 1)

            with ExitStack() as c2:
                units = []
                for qb in range(TB):
                    for hd in range(H8):
                        po, klen = HD * (hd % 2), (qb + 1) * P
                        units.append(dict(
                            q=qkv[po:po + HD, 12 + hd // 2, qb * P:qb * P + P], k=qkv[po:po + HD, 16 + hd // 2, 0:klen],
                            klen=klen, add=[], mask=bias[:, hd, SEQ - klen:SEQ], po=po, m=HD, oc=(hd // 2) * P,
                            v=[vb[:, x, hd * HD:hd * HD + HD] for x in range(qb + 1)]))
                groups = [(8 * qb + 7, F[:, 4:8, qb * P:qb * P + P],
                           lambda b: b[:, :].rearrange("p (a q) -> p a q", a=4)) for qb in range(TB)]
                pe_p, dve_p, act_p = softmax_attention("ch", units, groups, qkv[:, 6:12, :], c2)
                with nc.Block() as block:
                    @block.tensor
                    def _(pe):
                        pe_p(pe)

                    @block.vector
                    def _(dve):
                        dve_p(dve)

                    @block.scalar
                    def _(act):
                        act_p(act)

            rs2, rc2 = bias[:, 0:2, :], bias[:, 2, 0:2 * TB]
            squares = qkv[:, 0:DB, :]
            (n_sq, n_mm, n_ms, n_inv, n_rt, n_sp, n_rs, n_f) = (sem(f"mixnorm_{x}") for x in (
                "sq", "mm", "ms", "inv", "root", "spread", "rstd", "f"))
            x0 = n["x"]
            n["x"] += DB

            def x_pe(pe, b):
                if b:
                    return
                pe.wait_ge(n_sq, DB)
                for g in range(2):
                    for t in range(TB):
                        for q in range(4):
                            m = pe.matmul(ps[6][:, g * TB + t:g * TB + t + 1], squares[:, 4 * g + q, t * P:t * P + P], ones[:, 0:1],
                                          start=q == 0, stop=q == 3)
                m.then_inc(n_mm, 1)
                pe.wait_ge(n_rt, 1)
                for g in range(2):
                    for t in range(TB):
                        m = pe.matmul(ps[4 + g][:, t * P:t * P + P], rc2[:, g * TB + t:g * TB + t + 1].broadcast_to([P, P]),
                                      ident[:, :], start=True, stop=True)
                    m.then_inc(n_sp, 1)

            def x_dve(dve):
                for b in range(4, DB):
                    nc.vector.tensor_tensor(squares[:, b, :], F[:, b, :], F[:, b, :], ALU.mult).then_inc(n_sq, 1)
                dve.wait_ge(n_mm, 1)
                nc.vector.tensor_scalar(rc2, ps[6][:, 0:2 * TB], 1.0 / (4 * P), EPS, ALU.mult, ALU.add).then_inc(n_ms, 1)
                dve.wait_ge(n_ms, 1)
                nc.vector.reciprocal(rc2, rc2).then_inc(n_inv, 1)
                for b in range(DB + 1):
                    if b < DB:
                        if b % 4 == 0:
                            dve.wait_ge(n_sp, b // 4 + 1)
                            nc.vector.tensor_copy(rs2[:, b // 4, :], ps[4 + b // 4][:, :]).then_inc(n_rs, 1)
                            dve.wait_ge(n_rs, b // 4 + 1)
                        nc.vector.tensor_tensor(F[:, b, :], F[:, b, :], rs2[:, b // 4, :], ALU.mult).then_inc(n_f, 1)
                    if b >= 1:
                        q = b - 1
                        dve.wait_ge(xs_hi, x0 + q + 1)
                        nc.vector.scalar_tensor_tensor(out=xl[:, q, :], in0=F[:, q, :], scalar=vA[:, col["g_out_sb"] + q:col["g_out_sb"] + q + 1],
                                                       in1=xh[:, q, :].bitcast(F32), op0=ALU.mult, op1=ALU.subtract).then_inc(xs_lo, 1)

            def x_act(act):
                for b in range(4):
                    nc.scalar.activation(squares[:, b, :], F[:, b, :], ACT.Square).then_inc(n_sq, 1)
                act.wait_ge(n_inv, 1)
                nc.scalar.activation(rc2, rc2, ACT.Sqrt).then_inc(n_rt, 1)
                for b in range(DB):
                    act.wait_ge(n_f, b + 1)
                    nc.scalar.activation(xh[:, b, :], F[:, b, :], ACT.Copy,
                                         scale=vA[:, col["g_out_sb"] + b:col["g_out_sb"] + b + 1]).then_inc(xs_hi, 1)

            post_out("mix_out", xh, xl, x=(x_act, x_dve, x_pe))

        with ExitStack() as c:
            a_hi = sb("a_hi2", [P, FB, SEQ], F32R, ctx=c)
            a_lo = sb("a_lo2", [P, FB, SEQ], F32R, ctx=c)
            ffn_up("ffn2_up", gains("g_ffn2_pre"), gains("g_mix_post"), a_hi, a_lo, c)
            post_out("ffn2_down", a_hi, a_lo, DOWN)
        with ExitStack() as c:
            name = "ple"
            pt = sb("p_tokens", [P, TB, PLE], ctx=c)
            phi = sb("p_hi", [P, 2, SEQ], F32R, ctx=c)
            plo = sb("p_lo", [P, 2, SEQ], F32R, ctx=c)
            sg = sb("sigmoid", [P, 2, SEQ], ctx=c)
            p_in, p_t, p_hi, p_lo, sg_d = (sem(f"ple_{x}") for x in ("in", "turned", "hi", "lo", "sigmoid"))
            pro = Prologue(None, half[:, 1, :], squares=False)
            ev0, sq0, acc0, st, t0 = n["ev"], n["sq"], n["acc"], n["stat"], first[name]
            n["ev"] += 2 * DB
            n["sq"] += DB
            n["acc"] += DB - 1
            n["stat"] += 1
            with nc.Block() as block:
                @block.sync
                def _(sp):
                    sp.dma_start(pt[:, :, :], I["p"][0, 0].rearrange("(t p) d -> p t d", p=P)).then_inc(p_in, 16)
                    load_steps(sp, name)

                @block.gpsimd
                def _(pool):
                    sum_squares(pool, sq0, acc0)

                @block.scalar
                def _(act):
                    def split_p(act):
                        for b in range(2):
                            act.wait_ge(p_t, b + 1)
                            nc.scalar.activation(phi[:, b, :], ps[5 + b][:, :], ACT.Copy).then_inc(p_hi, 1)
                    pro.act(act, split_p)

                    def body(i, j):
                        split_hi(act, name, i, j)
                        o = i * 2 + j // 2
                        act.wait_ge(tile_done, i * 4 + (t0 + j + 1))
                        if j % 2 == 0:
                            wait(act, evac, ev0 + 2 * (o - 1) if not (isinstance(o, int) and o < 2) else 0)
                            nc.scalar.activation(sg[:, j // 2, :], ps[j][:, :], ACT.Sigmoid).then_inc(sg_d, 1)
                        else:
                            act.wait_ge(evac, i * 4 + (ev0 + j + 1))
                            wait(act, acc_done, acc0 + o - 1 if not (isinstance(o, int) and o < 2) else 0)
                            nc.scalar.activation(sq[:, j // 2, :].rearrange("p (o q) -> p o q", o=1), F[:, bass.ds(o, 1), :],
                                                 ACT.Square).then_inc(sq_done, 1)
                    steps(act, name, body)
                    root_act(act, st)

                @block.vector
                def _(dve):
                    def split_p(dve):
                        for b in range(2):
                            dve.wait_ge(p_hi, b + 1)
                            nc.vector.tensor_tensor(plo[:, b, :], ps[5 + b][:, :], phi[:, b, :].bitcast(F32), ALU.subtract).then_inc(p_lo, 1)
                    pro.dve(dve, split_p)

                    def body(i, j):
                        split_lo(dve, name, i, j)
                        if j % 2 == 1:
                            o = i * 2 + j // 2
                            dve.wait_ge(tile_done, i * 4 + (t0 + j + 1))
                            dve.wait_ge(sg_d, o + 1)
                            nc.vector.tensor_tensor(F[:, bass.ds(o, 1), :], ps[j][:, :].rearrange("p (o q) -> p o q", o=1),
                                                    sg[:, j // 2, :].rearrange("p (o q) -> p o q", o=1), ALU.mult).then_inc(evac, 2)
                    steps(dve, name, body)
                    inverse_dve(dve, st, D)
                    rstd_dve(dve, st)

                @block.tensor
                def _(pe):
                    pe.wait_ge(p_in, 16)
                    for b in range(2):
                        for t in range(TB):
                            m = pe.transpose(ps[5 + b][:, t * P:t * P + P], pt[:, t, b * P:b * P + P], ident[:, :])
                        m.then_inc(p_t, 1)

                    def body(i, j):
                        r, s, kb, t, got = tile_at(name, i, j, 0)
                        if isinstance(i, int) and i == 0 and j < HEAD:
                            if j:
                                return
                            pe.wait_ge(lo_done, t + HEAD)
                            for b in range(DB):
                                if b == 1:
                                    pe.wait_ge(p_lo, 2)
                                    for q in range(PLE // P):
                                        mm3(pe, ps[1][:, :], (t + 1) % SPLIT, q, phi[:, q, :], plo[:, q, :], q == 0, q == 1)
                                pe.wait_ge(xs_lo, pro.x0 + b + 1)
                                for g in (0, 2):
                                    last = mm3(pe, ps[g][:, :], (t + g) % SPLIT, b, xh[:, b, :], xl[:, b, :], b == 0, b == DB - 1)
                                    if b == DB - 1:
                                        last.then_inc(tile_done, 2 if g == 0 else 1)
                            return
                        pe.wait_ge(lo_done, t + 1)
                        wait(pe, evac, i * 4 + (ev0 + j - 3))
                        a, b_ = (xh, xl) if j % 2 == 0 else (phi, plo)
                        for b in range(kb):
                            last = mm3(pe, ps[j][:, :], s, b, a[:, b, :], b_[:, b, :], b == 0, b == kb - 1)
                        last.then_inc(tile_done, 1)
                    steps(pe, name, body)
                    sums_pe(pe, acc0 + DB - 1, sq0 + DB)
                    spread_pe(pe, st)

        with ExitStack() as c:
            name = "conv_in"
            K = 3
            cv = sb("cv", [P, 2, SEQ + K - 1], ctx=c)
            y = sb("conv_y", [P, 2, SEQ], ctx=c)
            zs = sb("conv_z", [P, 2, SEQ], ctx=c)
            br = sb("conv_b", [P, 2, SEQ], ctx=c)
            yall = sb("conv_yall", [P, DB, SEQ], ctx=c)
            cz, cr, cvd, yd, zd, bd = (sem(f"conv_{x}") for x in ("zeros", "c", "cv", "y", "z", "b"))
            pro = Prologue(gains("norm_w_2"), gains("g_ple_post"))
            ev0, st, t0 = n["ev"], n["stat"], first[name]
            n["ev"] += 4 * DB
            n["stat"] += 1
            wcol = col["conv_w_conv_2"]
            with nc.Block() as block:
                @block.sync
                def _(sp):
                    load_steps(sp, name)

                @block.gpsimd
                def _(pool):
                    for s in range(2):
                        nc.gpsimd.memset(cv[:, s, 0:K - 1], 0.0).then_inc(cz, 1)
                    pro.pool(pool)

                @block.scalar
                def _(act):
                    pro.act(act)

                    def body(i, j):
                        split_hi(act, name, i, j)
                        if isinstance(i, int) and i == 0 and j == 0:
                            root_act(act, st)
                        if j == 3:
                            act.wait_ge(zd, i + 1)
                            nc.scalar.activation(zs[:, 0, :], zs[:, 0, :], ACT.Silu).then_inc(bd, 1)
                    steps(act, name, body)

                @block.vector
                def _(dve):
                    pro.dve(dve)
                    dve.wait_ge(cz, 2)

                    def body(i, j):
                        split_lo(dve, name, i, j)
                        if isinstance(i, int) and i == 0 and j == 0:
                            inverse_dve(dve, st, D)
                            rstd_dve(dve, st)
                            dve.wait_ge(rstd_done, st + 1)
                        dve.wait_ge(tile_done, i * 4 + (t0 + j + 1))
                        if j == 0:
                            nc.vector.tensor_tensor(br[:, 0, :], ps[j][:, :], rstd[:, :], ALU.mult).then_inc(evac, 1)
                        elif j == 1:
                            nc.vector.tensor_tensor(br[:, 1, :], ps[j][:, :], rstd[:, :], ALU.mult).then_inc(evac, 1)
                            dve.wait_ge(evac, i * 4 + (ev0 + 2))
                            nc.vector.tensor_tensor(br[:, 1, :], br[:, 1, :], rstd[:, :], ALU.mult).then_inc(cr, 1)
                        elif j == 2:
                            dve.wait_ge(cr, i + 1)
                            nc.vector.tensor_tensor(cv[:, 0, K - 1:SEQ + K - 1], ps[j][:, :], br[:, 1, :], ALU.mult).then_inc(evac, 1)
                            dve.wait_ge(evac, i * 4 + (ev0 + 3))
                            nc.vector.tensor_scalar(y[:, 0, :], cv[:, 0, 0:SEQ], vA[:, bass.ds(i + wcol, 1)], None, ALU.mult).then_inc(yd, 1)
                            dve.wait_ge(yd, i * 4 + 1)
                            nc.vector.scalar_tensor_tensor(out=y[:, 1, :], in0=cv[:, 0, 1:SEQ + 1], scalar=vA[:, bass.ds(i + (wcol + DB), 1)],
                                                           in1=y[:, 0, :], op0=ALU.mult, op1=ALU.add).then_inc(yd, 1)
                            dve.wait_ge(yd, i * 4 + 2)
                            nc.vector.scalar_tensor_tensor(out=y[:, 0, :], in0=cv[:, 0, 2:SEQ + 2], scalar=vA[:, bass.ds(i + (wcol + 2 * DB), 1)],
                                                           in1=y[:, 1, :], op0=ALU.mult, op1=ALU.add).then_inc(yd, 1)
                            dve.wait_ge(yd, i * 4 + 3)
                            nc.vector.tensor_tensor(y[:, 1, :], y[:, 0, :], br[:, 0, :], ALU.mult).then_inc(yd, 1)
                        else:
                            nc.vector.tensor_tensor(zs[:, 0, :], ps[j][:, :], rstd[:, :], ALU.mult).then_inc(zd, 1)
                            dve.wait_ge(bd, i + 1)
                            dve.wait_ge(yd, i * 4 + 4)
                            nc.vector.tensor_tensor(yall[:, bass.ds(i, 1), :], y[:, 1, :].rearrange("p (o q) -> p o q", o=1),
                                                    zs[:, 0, :].rearrange("p (o q) -> p o q", o=1), ALU.mult).then_inc(evac, 1)
                    steps(dve, name, body)

                @block.tensor
                def _(pe):
                    pe_tiles(pe, name, xh, xl, ev0, x_ready=pro.x0, sums=pro.sums, at=st)

            sums = resid_out("conv_out", *split_x(lambda b: yall[:, b, :]))

        with ExitStack() as c:
            qkv = sb("fox_qkvz", [P, 4 * DB, SEQ], ctx=c)
            vt = sb("fox_v", [P, TB, D], ctx=c)
            fl = sb("fox_f", [H8, 4, SEQ], ctx=c)
            bf = sb("fox_bf", [H8, 1], ctx=c)
            nsel = sb("fox_nsel", [H8, H8, P], ctx=c)
            mask = sb("fox_mask", [P, SEQ], ctx=c)
            f_in, fsel, fm, fd, q_sc, z_silu = (sem(f"fox_{x}") for x in ("bf", "sel", "mask", "f", "q", "z"))
            ev0 = n["ev"]
            turn = token_turn(lambda b: qkv[:, 16 + b, :], 8, vt, lambda b: (evac, ev0 + 16 + b + 1))

            def sp_tail(sp):
                sp.dma_start(bf[:, :], I["fox_b_f_2"].rearrange("a h -> h a")).then_inc(f_in, 16)

            def pool_tail(pool):
                nc.gpsimd.memset(nsel[:, :, :], 0.0).then_inc(fsel, 1)
                nc.gpsimd.memset(fl[:, 3, :], 1.0).then_inc(fsel, 1)
                pool.wait_ge(fsel, 1)
                nc.gpsimd.affine_select(out=nsel[:, :, :], in_=nsel[:, :, :], compare_op=ALU.not_equal, fill=-1.0, base=0,
                                        pattern=[[-1, H8], [0, P]], channel_multiplier=1).then_inc(fsel, 1)
                nc.gpsimd.memset(mask[:, :], 0.0).then_inc(fm, 1)
                pool.wait_ge(fm, 1)
                nc.gpsimd.affine_select(out=mask[:, SEQ - P:SEQ], in_=mask[:, SEQ - P:SEQ], compare_op=ALU.is_ge, fill=NEG,
                                        base=0, pattern=[[-1, P]], channel_multiplier=1).then_inc(fm, 1)

            def f_evac(dve, i, j, ev0_):
                if isinstance(i, int) and 4 * i + j == 28:
                    nc.vector.tensor_tensor(fl[:, 0, :], ps[0][0:H8, :], rstd[0:H8, :], ALU.mult).then_inc(evac, 1)
                else:
                    behind = 1 if isinstance(i, int) and 4 * i + j > 28 else 0
                    nc.vector.tensor_tensor(qkv[:, bass.ds(i * 4 + j - behind, 1), :], ps[j][:, :].rearrange("p (o q) -> p o q", o=1),
                                            rstd[:, :].rearrange("p (o q) -> p o q", o=1), ALU.mult).then_inc(evac, 1)

            def pe_beside(pe, k):
                if 28 <= k < 32:
                    turn[0](pe, 2 * (k - 28), 2 * (k - 28) + 2)

            def dve_beside(dve, k):
                if 28 <= k < 32:
                    turn[1](dve, 2 * (k - 28), 2 * (k - 28) + 2)
                if k in (28, 31):
                    q = qkv[:, 4 * (k > 28):4 * (k > 28) + 4, :]
                    dve.wait_ge(evac, ev0 + 8)
                    nc.vector.tensor_scalar(q, q, P ** -0.5, None, ALU.mult).then_inc(q_sc, 1)
                if k == 29:
                    dve.wait_ge(f_in, 16)
                    dve.wait_ge(evac, ev0 + 29)
                    nc.vector.tensor_scalar(fl[:, 0, :], fl[:, 0, :], bf[:, 0:1], None, ALU.add).then_inc(fd, 1)
                if k == 30:
                    dve.wait_ge(fsel, 3)
                    dve.wait_ge(fd, 4)
                    nc.vector.scalar_tensor_tensor(out=fl[:, 2, :], in0=fl[:, 0, :], scalar=0.0, in1=fl[:, 1, :],
                                                   op0=ALU.min, op1=ALU.subtract).then_inc(fd, 1)
                    dve.wait_ge(fd, 5)
                    nc.vector.tensor_tensor_scan(fl[:, 0, :], fl[:, 3, :], fl[:, 2, :], 0.0, ALU.mult, ALU.add).then_inc(fd, 1)

            def silu_z(act, b0, b1):
                z = qkv[:, b0:b1, :]
                act.wait_ge(evac, ev0 + b1 + (b1 > 28))
                nc.scalar.activation(z, z, ACT.Silu).then_inc(z_silu, 1)

            def act_beside(act, k):
                if k == 28:
                    silu_z(act, 24, 28)
                if k == 29:
                    act.wait_ge(fd, 1)
                    nc.scalar.activation(fl[:, 1, :], fl[:, 0, :], ACT.Abs).then_inc(fd, 1)
                    act.wait_ge(fd, 2)
                    nc.scalar.activation(fl[:, 1, :], fl[:, 1, :], ACT.Exp, scale=-1.0).then_inc(fd, 1)
                    act.wait_ge(fd, 3)
                    nc.scalar.activation(fl[:, 1, :], fl[:, 1, :], ACT.Ln, bias=1.0).then_inc(fd, 1)
                if k == 31:
                    silu_z(act, 28, 30)
                if k == 32:
                    silu_z(act, 30, 32)

            in_proj("fox_in", vA[:, col["norm_w_2"] + DB:col["norm_w_2"] + 2 * DB], None, sums=sums,
                    tails=dict(sp=sp_tail, pool=pool_tail), beside=dict(pe=pe_beside, dve=dve_beside, act=act_beside),
                    evac_dve=f_evac, loop_end=7)
            with ExitStack() as c2:
                units = []
                for qb in range(TB):
                    for hd in range(8):
                        klen = (qb + 1) * P
                        units.append(dict(
                            q=qkv[:, hd, qb * P:qb * P + P], k=qkv[:, 8 + hd, 0:klen], klen=klen,
                            add=[(nsel[:, hd, :], fl[:, 0, 0:klen])], mask=mask[:, SEQ - klen:SEQ], po=0, m=P,
                            oc=(hd % 4) * P, v=[vt[:, x, hd * P:hd * P + P] for x in range(qb + 1)]))
                groups = [(4 * g + 3, F[:, 4 * (g % 2):4 * (g % 2) + 4, (g // 2) * P:(g // 2) * P + P],
                           lambda b: b[:, :].rearrange("p (a q) -> p a q", a=4)) for g in range(2 * TB)]
                pe_p, dve_p, act_p = softmax_attention("fox", units, groups, qkv[:, 16:22, :], c2)
                with nc.Block() as block:
                    @block.tensor
                    def _(pe):
                        pe_p(pe)

                    @block.vector
                    def _(dve):
                        dve_p(dve)

                    @block.scalar
                    def _(act):
                        act_p(act)

            sums = resid_out("fox_out", *gate_x(lambda b: qkv[:, 24 + b, :]))

        with ExitStack() as c:
            G = sb("gdn_qkvz", [P, 4 * DB, SEQ], ctx=c)
            X = sb("gdn_slots", [P, 12, SEQ], ctx=c)
            BG = sb("gdn_bg", [2 * H8, SEQ], ctx=c)
            LV = 7
            TH = [P, TB, H8]
            cc = sb("gdn_cc", [P, TB, 2 * H8], ctx=c)
            tab = sb("gdn_tab", [P, 16, TB, H8], ctx=c)
            (BETA, AX, AE, GG, GC, GL, EGC, EGL, EKD, CKN, CKB, CKBE, CKD, CQN, CQD, TMP) = range(16)
            nrm = sb("gdn_norm", [P, TB, 16], ctx=c)
            al = sb("gdn_al", [P, 3, H8], ctx=c)
            lev = sb("gdn_levels", [P, LV, P], ctx=c)
            triu = sb("gdn_triu", [P, P], ctx=c)
            state = sb("gdn_state", [P, 2, P], ctx=c)
            vn = sb("gdn_vnew", [P, 2, P], ctx=c)
            (a_in, g_const, g_turned, g_ax, g_beta, g_soft, g_al, g_sum, g_dif, g_exp, g_sq, g_ss, g_nrm, g_root, z_silu, g_dv) = (
                sem(f"gdn_{x}") for x in ("ain", "const", "turned", "ax", "beta", "soft", "al", "sum", "dif", "exp",
                                          "sq", "ss", "nrm", "root", "zsilu", "link"))

            K = 4
            ev0 = n["ev"]
            with ExitStack() as c2:
                u = X[:, 0:4, :].rearrange("p a q -> p (a q)")
                W_U = SEQ + K - 1
                ub = [u[:, s * W_U:(s + 1) * W_U] for s in range(2)]
                c_zero, c_first, c_tap, c_silu = sem("gdn_zero"), sem("gdn_first"), sem("gdn_tap"), sem("gdn_silu")

                def one(ap):
                    return ap.rearrange("p (o q) -> p o q", o=1)

                def g_evac(dve, i, j, ev0_):
                    k = i * 4 + j
                    if isinstance(i, int) and k == 24:
                        nc.vector.tensor_tensor(BG[:, :], ps[0][0:2 * H8, :], rstd[0:2 * H8, :], ALU.mult).then_inc(evac, 1)
                        g_tap(dve, i, j, 3)
                        return
                    if isinstance(i, int) and i >= 6:
                        nc.vector.tensor_tensor(G[:, k - 1, :], ps[j][:, :], rstd[:, :], ALU.mult).then_inc(evac, 1)
                        return
                    if isinstance(i, int) and k == 0:
                        dve.wait_ge(c_zero, 2)
                    nc.vector.tensor_tensor(ub[j % 2][:, K - 1:K - 1 + SEQ], ps[j][:, :], rstd[:, :], ALU.mult).then_inc(evac, 1)
                    if not isinstance(i, int) or k:
                        g_tap(dve, i, j, 3)

                def g_tap(dve, i, j, tap):
                    if isinstance(i, int) and not 1 <= 4 * i + j <= 24:
                        return
                    if tap == 1:
                        dve.wait_ge(c_first, i * 4 + j)
                    else:
                        dve.wait_ge(c_tap, i * 12 + (3 * (j - 1) + tap - 1))
                    dst = G[:, bass.ds(i * 4 + (j - 1), 1), :]
                    nc.vector.scalar_tensor_tensor(out=dst, in0=one(ub[(j + 1) % 2][:, tap:tap + SEQ]),
                                                   scalar=vB[:, bass.ds(i * 4 + (j - 1 + 24 * tap), 1)],
                                                   in1=dst, op0=ALU.mult, op1=ALU.add).then_inc(c_tap, 1)

                def g_act(act, i, j, ev0_):
                    k = 4 * i + j
                    silu = not isinstance(i, int) or 2 <= k <= 25
                    if silu:
                        act.wait_ge(c_tap, i * 12 + 3 * (j - 1))
                    if not isinstance(i, int) or k < 24:
                        act.wait_ge(evac, i * 4 + (ev0_ + j + 1))
                        act.wait_ge(c_zero, 2)
                        nc.scalar.activation(G[:, bass.ds(i * 4 + j, 1), :], one(ub[j % 2][:, 0:SEQ]), ACT.Copy,
                                             scale=vB[:, bass.ds(i * 4 + j, 1)]).then_inc(c_first, 1)
                    if silu:
                        dst = G[:, bass.ds(i * 4 + (j - 2), 1), :]
                        nc.scalar.activation(dst, dst, ACT.Silu).then_inc(c_silu, 1)

                def sp_tail(sp):
                    for r, nm in enumerate(("gdn_a_log_2", "gdn_dt_bias_2")):
                        sp.dma_start(al[:, r, :], I[nm].broadcast_to([P, H8])).then_inc(a_in, 16)

                def pool_tail(pool):
                    for s in range(2):
                        nc.gpsimd.memset(ub[s][:, 0:K - 1], 0.0).then_inc(c_zero, 1)
                    nc.gpsimd.affine_select(out=triu[:, :], in_=ones[:, :], compare_op=ALU.is_ge, fill=0.0, base=0,
                                            pattern=[[1, P]], channel_multiplier=-1).then_inc(g_const, 1)
                    nc.gpsimd.memset(lev[:, :, :], 0.0).then_inc(g_const, 1)
                    pool.wait_ge(g_const, 2)
                    for l in range(LV):
                        b = 2 ** l
                        m = P // (2 * b)
                        v = lev[:, l, :].rearrange("p (m s r) -> p m s r", m=m, s=2)[:, :, 1, :]
                        src = ones[:, 0:m * b].rearrange("p (m r) -> p m r", m=m)
                        nc.gpsimd.affine_select(out=v, in_=src, compare_op=ALU.is_ge, fill=0.0, base=0,
                                                pattern=[[-2 * b, m], [0, b]], channel_multiplier=1).then_inc(g_const, 1)
                        pool.wait_ge(g_const, 3 + 2 * l)
                        nc.gpsimd.affine_select(out=v, in_=v, compare_op=ALU.is_ge, fill=0.0, base=b - 1,
                                                pattern=[[2 * b, m], [0, b]], channel_multiplier=-1).then_inc(g_const, 1)

                def pe_beside(pe, k):
                    if k == 25:
                        pe.wait_ge(evac, ev0 + 25)
                        for t in range(TB):
                            m = pe.transpose(ps[4][:, t * 16:t * 16 + 16], BG[:, t * P:t * P + P], ident[0:16, 0:16])
                        m.then_inc(g_turned, 1)
                    if k >= 25:
                        for b in (2 * (k - 25), 2 * (k - 25) + 1):
                            pe.wait_ge(g_sq, b + 1)
                            for t in range(TB):
                                m = pe.matmul(ps[5][:, t * 16 + b:t * 16 + b + 1], X[:, 4 + b % 4, t * P:t * P + P], ones[:, 0:1],
                                              start=True, stop=True)
                            m.then_inc(g_ss, 1)
                    if k == 29:
                        pe.wait_ge(g_al, 3)
                        pe.wait_ge(g_const, 1)
                        g = tab[:, GG, :, :].rearrange("p t h -> p (t h)")
                        pe.matmul(ps[6][:, 0:32], triu[:, :], g, start=True, stop=True)
                        pe.matmul(ps[6][:, 32:64], ones[:, :], g, start=True, stop=True).then_inc(g_sum, 1)

                def act_beside(act, k):
                    if 24 <= k < 32:
                        for b in (2 * (k - 24), 2 * (k - 24) + 1):
                            if b >= 4:
                                act.wait_ge(g_ss, b - 3)
                            act.wait_ge(c_silu, b + 1)
                            nc.scalar.activation(X[:, 4 + b % 4, :], G[:, b, :], ACT.Square).then_inc(g_sq, 1)
                    if k == 27:
                        act.wait_ge(g_ax, 2)
                        nc.scalar.activation(tab[:, BETA, :, :], cc[:, :, 0:H8], ACT.Sigmoid).then_inc(g_beta, 1)
                        nc.scalar.activation(tab[:, AE, :, :], tab[:, AX, :, :], ACT.Abs).then_inc(g_soft, 1)
                        act.wait_ge(g_soft, 1)
                        nc.scalar.activation(tab[:, AE, :, :], tab[:, AE, :, :], ACT.Exp, scale=-1.0).then_inc(g_soft, 1)
                        act.wait_ge(a_in, 32)
                        nc.scalar.activation(al[:, 2, :], al[:, 0, :], ACT.Exp).then_inc(g_al, 1)
                        act.wait_ge(g_soft, 2)
                        nc.scalar.activation(tab[:, AE, :, :], tab[:, AE, :, :], ACT.Ln, bias=1.0).then_inc(g_soft, 1)
                    if k == 30:
                        act.wait_ge(g_dif, 1)
                        nc.scalar.activation(tab[:, EGC:EGC + 3, :, :], tab[:, EGC:EGC + 3, :, :], ACT.Exp).then_inc(g_exp, 1)
                    if k == 32:
                        act.wait_ge(g_nrm, 1)
                        nc.scalar.activation(nrm[:, :, :], nrm[:, :, :], ACT.Sqrt).then_inc(g_root, 1)
                    if k in (29, 32):
                        z = G[:, 24:28, :] if k == 29 else G[:, 28:32, :]
                        act.wait_ge(evac, ev0 + (29 if k == 29 else 33))
                        nc.scalar.activation(z, z, ACT.Silu).then_inc(z_silu, 1)

                def bc(ap):
                    return ap.rearrange("p (o h) -> p o h", o=1).broadcast_to(TH)

                steps_ = [0]

                def dve_beside(dve, k):
                    def link(ins):
                        steps_[0] += 1
                        ins.then_inc(g_dv, 1)
                        dve.wait_ge(g_dv, steps_[0])

                    if k == 26:
                        dve.wait_ge(g_turned, 1)
                        nc.vector.tensor_copy(cc[:, :, :], ps[4][:, 0:64].rearrange("p (t c) -> p t c", t=TB)).then_inc(g_ax, 1)
                        dve.wait_ge(a_in, 32)
                        dve.wait_ge(g_ax, 1)
                        nc.vector.tensor_tensor(tab[:, AX, :, :], cc[:, :, H8:2 * H8], bc(al[:, 1, :]), ALU.add).then_inc(g_ax, 1)
                    if k == 28:
                        dve.wait_ge(g_soft, 3)
                        link(nc.vector.scalar_tensor_tensor(out=tab[:, TMP, :, :], in0=tab[:, AX, :, :], scalar=0.0, in1=tab[:, AE, :, :],
                                                            op0=ALU.max, op1=ALU.add))
                        dve.wait_ge(g_al, 1)
                        nc.vector.tensor_scalar(al[:, 2, :], al[:, 2, :], -1.0, None, ALU.mult).then_inc(g_al, 1)
                        dve.wait_ge(g_al, 2)
                        nc.vector.tensor_tensor(tab[:, GG, :, :], tab[:, TMP, :, :], bc(al[:, 2, :]), ALU.mult).then_inc(g_al, 1)
                    if k == 29:
                        dve.wait_ge(g_sum, 1)
                        link(nc.vector.tensor_copy(tab[:, GC:GC + 2, :, :], ps[6][:, 0:64].rearrange("p (a t h) -> p a t h", a=2, t=TB)))
                        link(nc.vector.tensor_copy(tab[:, EGC:EGC + 2, :, :], tab[:, GC:GC + 2, :, :]))
                        nc.vector.tensor_tensor(tab[:, EKD, :, :], tab[:, GL, :, :], tab[:, GC, :, :], ALU.subtract).then_inc(g_dif, 1)
                    if k == 32:
                        dve.wait_ge(g_ss, 16)
                        nc.vector.tensor_scalar(nrm[:, :, :], ps[5][:, 0:64].rearrange("p (t c) -> p t c", t=TB), EPS, None,
                                                ALU.add).then_inc(g_nrm, 1)
                        dve.wait_ge(g_root, 1)
                        link(nc.vector.reciprocal(nrm[:, :, :], nrm[:, :, :]))
                        dve.wait_ge(g_exp, 1)
                        dve.wait_ge(g_beta, 1)
                        k_, q_ = nrm[:, :, 8:16], nrm[:, :, 0:8]
                        nc.vector.tensor_copy(tab[:, CKN, :, :], k_).then_inc(g_nrm, 1)
                        link(nc.vector.tensor_tensor(tab[:, CKB, :, :], k_, tab[:, BETA, :, :], ALU.mult))
                        nc.vector.tensor_tensor(tab[:, CKBE, :, :], tab[:, CKB, :, :], tab[:, EGC, :, :], ALU.mult).then_inc(g_nrm, 1)
                        nc.vector.tensor_tensor(tab[:, CKD, :, :], k_, tab[:, EKD, :, :], ALU.mult).then_inc(g_nrm, 1)
                        link(nc.vector.tensor_scalar(tab[:, CQN, :, :], q_, P ** -0.5, None, ALU.mult))
                        nc.vector.tensor_tensor(tab[:, CQD, :, :], tab[:, CQN, :, :], tab[:, EGC, :, :], ALU.mult).then_inc(g_nrm, 1)

                in_proj("gdn_in", vA[:, col["norm_w_2"] + 2 * DB:col["norm_w_2"] + 3 * DB], None, sums=sums,
                        tails=dict(sp=sp_tail, pool=pool_tail), beside=dict(pe=pe_beside, act=act_beside, dve=dve_beside),
                        evac_dve=g_evac, evac_act=g_act, between_dve=g_tap, loop_end=6)

            KN, KB, QN, QD, KNT, KBT, QNT, KBE, KD, DD = range(10)
            LT, BT0, BT1, US, T_, TT, QKT = KN, KB, QN, QD, KNT, KBT, QNT

            def slot(s, r):
                return F[:, s, :] if r == 0 and s < 8 else X[:, s - 8 if r == 0 else 2 + s, :]

            def blk(ap, t):
                return ap[:, t * P:t * P + P]

            def v4(ap):
                return ap.rearrange("p (t d) -> p t d", t=TB)

            def colb(row, hd):
                return tab[:, row, :, hd:hd + 1].broadcast_to([P, TB, P])

            (t_in, k_copied, tok_d, tok_p, t_back, back_a, back_d, kk_mm, dif, dif_m, dec, qkt_d, strict, lt_d, bt_d, u_mm,
             us_d, p_mm, t_d, w_mm, w_d, v_mm, vn_d, o_mm, s_mm, s_d, o_tok) = (sem(f"gd_{x}") for x in (
                 "tin", "kcopied", "tokd", "tokp", "tback", "backa", "backd", "kk", "dif", "difm", "dec", "qkt", "strict", "lt",
                 "bt", "u", "us", "p", "t", "w", "wd", "v", "vn", "o", "s", "sd", "otok"))
            NP_ = H8 // 2
            sso = sb("gdn_sso", [P, H8, TB], ctx=c)
            o_sq = sem("gdo_sq")

            def lvl(p, l, r):
                return (p * LV + l) * 2 + r + 1

            with nc.Block() as block:
                @block.tensor
                def _(pe):
                    for p in range(NP_):
                        for r in range(2):
                            m, b = 2 * p + r, 4 * r
                            if p:
                                pe.wait_ge(o_tok, m - 1)
                            for src, bank in ((m, 0), (8 + m, 1), (16 + m, 2)):
                                for t in range(TB):
                                    ins = pe.transpose(blk(ps[b + bank], t), blk(G[:, src, :], t), ident[:, :])
                            ins.then_inc(t_in, 1)
                        for r in range(2):
                            m, b = 2 * p + r, 4 * r
                            pe.wait_ge(tok_d, 5 * m + 5)
                            pe.wait_ge(k_copied, m + 1)
                            for x, s in enumerate((KN, KB, QN, QD)):
                                for t in range(TB):
                                    ins = pe.transpose(blk(ps[b + x], t), blk(slot(s, r), t), ident[:, :])
                            ins.then_inc(t_back, 1)
                        for r in range(2):
                            m, b = 2 * p + r, 4 * r
                            pe.wait_ge(back_a, 2 * m + 2)
                            pe.wait_ge(back_d, 2 * m + 2)
                            for t in range(TB):
                                pe.matmul(blk(ps[b + 2], t), tab[:, GC, t, m:m + 1].broadcast_to([P, P]), ident[:, :],
                                          start=True, stop=True)
                                pe.matmul(blk(ps[b], t), blk(slot(KNT, r), t), blk(slot(KBT, r), t), start=True, stop=True)
                                ins = pe.matmul(blk(ps[b + 1], t), blk(slot(KNT, r), t), blk(slot(QNT, r), t),
                                                start=True, stop=True)
                            ins.then_inc(kk_mm, 1)
                        for l in range(LV):
                            for r in range(2):
                                m, b = 2 * p + r, 4 * r
                                pe.wait_ge(bt_d, lvl(p, l, r))
                                if l:
                                    pe.wait_ge(t_d, 2 * (lvl(p, l - 1, r)))
                                rhs = ident if l == 0 else slot(T_, r)
                                for t in range(TB):
                                    ins = pe.matmul(blk(ps[b], t), blk(slot(BT0 + l % 2, r), t),
                                                    ident[:, :] if l == 0 else blk(slot(T_, r), t), start=True, stop=True)
                                ins.then_inc(u_mm, 1)
                            if l == 0:
                                continue
                            for r in range(2):
                                m, b = 2 * p + r, 4 * r
                                pe.wait_ge(us_d, (p * (LV - 1) + l - 1) * 2 + r + 1)
                                for t in range(TB):
                                    if l < LV - 1:
                                        pe.matmul(blk(ps[b + 1], t), blk(slot(TT, r), t), blk(slot(US, r), t), start=True, stop=True)
                                    ins = pe.matmul(blk(ps[b + 2], t), blk(slot(US, r), t), blk(slot(TT, r), t), start=True, stop=True)
                                ins.then_inc(p_mm, 1)
                        for r in range(2):
                            m, b = 2 * p + r, 4 * r
                            pe.wait_ge(t_d, 2 * lvl(p, LV - 1, r))
                            pe.wait_ge(tok_p, 2 * m + 2)
                            for t in range(TB):
                                ins = pe.matmul(blk(ps[b + 3], t), blk(slot(KBE, r), t), blk(slot(TT, r), t), start=True, stop=True)
                            ins.then_inc(w_mm, 1)
                        for t in range(TB):
                            for r in range(2):
                                m, b = 2 * p + r, 4 * r
                                ins = pe.matmul(blk(ps[b], t), blk(slot(TT, r), t), blk(G[:, 16 + m, :], t), start=True, stop=t == 0)
                                if t:
                                    pe.wait_ge(w_d, m + 1)
                                    pe.wait_ge(s_d, (p * 3 + t - 1) * 2 + r + 1)
                                    ins = pe.matmul(blk(ps[b], t), blk(G[:, 8 + m, :], t), state[:, r, :], start=False, stop=True)
                                ins.then_inc(v_mm, 1)
                            for r in range(2):
                                m, b = 2 * p + r, 4 * r
                                pe.wait_ge(vn_d, (p * TB + t) * 2 + r + 1)
                                if t == 0:
                                    pe.wait_ge(qkt_d, m + 1)
                                ins = pe.matmul(blk(ps[b + 1], t), blk(slot(QKT, r), t), vn[:, r, :], start=True, stop=t == 0)
                                if t:
                                    ins = pe.matmul(blk(ps[b + 1], t), blk(G[:, m, :], t), state[:, r, :], start=False, stop=True)
                                ins.then_inc(o_mm, 1)
                                if t < TB - 1:
                                    pe.matmul(ps[b + 2][:, 0:P], blk(slot(KD, r), t), vn[:, r, :], start=True, stop=True).then_inc(s_mm, 1)

                @block.vector
                def _(dve):
                    for p in range(NP_):
                        for r in range(2):
                            m, b = 2 * p + r, 4 * r
                            dve.wait_ge(t_in, m + 1)
                            for dst, bank, cf in ((slot(KN, r), 1, CKN), (slot(KB, r), 1, CKB), (slot(QN, r), 0, CQN),
                                                  (slot(QD, r), 0, CQD), (G[:, 16 + m, :], 2, BETA)):
                                nc.vector.tensor_tensor(v4(dst), v4(ps[b + bank][:, :]), colb(cf, m), ALU.mult).then_inc(tok_d, 1)
                        for r in range(2):
                            m, b = 2 * p + r, 4 * r
                            dve.wait_ge(t_back, m + 1)
                            nc.vector.tensor_copy(slot(KBT, r), ps[b + 1][:, :]).then_inc(back_d, 1)
                            nc.vector.tensor_copy(G[:, m, :], ps[b + 3][:, :]).then_inc(back_d, 1)
                        for r in range(2):
                            m, b = 2 * p + r, 4 * r
                            dve.wait_ge(kk_mm, m + 1)
                            dve.wait_ge(tok_p, 2 * m + 2)
                            nc.vector.tensor_tensor(v4(slot(DD, r)), v4(ps[b + 2][:, :]), colb(GC, m), ALU.subtract).then_inc(dif, 1)
                        for r in range(2):
                            m, b = 2 * p + r, 4 * r
                            dve.wait_ge(dec, m + 1)
                            nc.vector.tensor_tensor(slot(QKT, r), ps[b + 1][:, :], slot(DD, r), ALU.mult).then_inc(qkt_d, 1)
                        for r in range(2):
                            m, b = 2 * p + r, 4 * r
                            dve.wait_ge(strict, m + 1)
                            nc.vector.tensor_tensor(slot(LT, r), ps[b][:, :], slot(DD, r), ALU.mult).then_inc(lt_d, 1)
                        idb = ident[:, :].rearrange("p (o d) -> p o d", o=1).broadcast_to([P, TB, P])
                        for l in range(LV):
                            for r in range(2):
                                m, b = 2 * p + r, 4 * r
                                if l == 0:
                                    dve.wait_ge(u_mm, lvl(p, l, r))
                                    nc.vector.tensor_tensor(v4(slot(T_, r)), idb, v4(ps[b][:, :]), ALU.subtract).then_inc(t_d, 1)
                                    nc.vector.tensor_tensor(v4(slot(TT, r)), idb, v4(slot(BT0, r)), ALU.subtract).then_inc(t_d, 1)
                                    continue
                                dve.wait_ge(p_mm, (p * (LV - 1) + l - 1) * 2 + r + 1)
                                if l < LV - 1:
                                    nc.vector.tensor_tensor(slot(T_, r), slot(T_, r), ps[b + 1][:, :], ALU.subtract).then_inc(t_d, 1)
                                    nc.vector.tensor_tensor(slot(TT, r), slot(TT, r), ps[b + 2][:, :], ALU.subtract).then_inc(t_d, 1)
                                else:
                                    nc.vector.tensor_tensor(slot(TT, r), slot(TT, r), ps[b + 2][:, :], ALU.subtract).then_inc(t_d, 2)
                        for t in range(TB - 1):
                            for r in range(2):
                                m, b = 2 * p + r, 4 * r
                                dve.wait_ge(s_mm, (p * 3 + t) * 2 + r + 1)
                                dve.wait_ge(o_mm, (p * TB + t) * 2 + r + 1)
                                if t == 0:
                                    nc.vector.tensor_copy(state[:, r, :], ps[b + 2][:, 0:P]).then_inc(s_d, 1)
                                else:
                                    nc.vector.scalar_tensor_tensor(out=state[:, r, :], in0=state[:, r, :], scalar=tab[:, EGL, t, m:m + 1],
                                                                   in1=ps[b + 2][:, 0:P], op0=ALU.mult, op1=ALU.add).then_inc(s_d, 1)
                        for r in range(2):
                            m, b = 2 * p + r, 4 * r
                            dve.wait_ge(o_mm, (p * TB + TB - 1) * 2 + r + 1)
                            nc.vector.tensor_copy(G[:, m, :], ps[b + 1][:, :]).then_inc(o_tok, 1)

                @block.scalar
                def _(act):
                    for p in range(NP_):
                        for r in range(2):
                            m, b = 2 * p + r, 4 * r
                            act.wait_ge(t_in, m + 1)
                            act.wait_ge(tok_d, 5 * m + 5)
                            nc.scalar.activation(slot(DD, r), ps[b + 1][:, :], ACT.Copy).then_inc(k_copied, 1)
                        for r in range(2):
                            m, b = 2 * p + r, 4 * r
                            act.wait_ge(t_back, m + 1)
                            nc.scalar.activation(slot(KNT, r), ps[b][:, :], ACT.Copy).then_inc(back_a, 1)
                            nc.scalar.activation(slot(QNT, r), ps[b + 2][:, :], ACT.Copy).then_inc(back_a, 1)
                        for r in range(2):
                            m = 2 * p + r
                            act.wait_ge(dif_m, m + 1)
                            nc.scalar.activation(slot(DD, r), slot(DD, r), ACT.Exp).then_inc(dec, 1)
                        for l in range(1, LV):
                            for r in range(2):
                                b = 4 * r
                                act.wait_ge(u_mm, lvl(p, l, r))
                                nc.scalar.activation(slot(US, r), ps[b][:, :], ACT.Copy).then_inc(us_d, 1)
                        for r in range(2):
                            m, b = 2 * p + r, 4 * r
                            act.wait_ge(w_mm, m + 1)
                            nc.scalar.activation(G[:, 8 + m, :], ps[b + 3][:, :], ACT.Copy, scale=-1.0).then_inc(w_d, 1)
                        for t in range(TB):
                            for r in range(2):
                                b = 4 * r
                                act.wait_ge(v_mm, (p * TB + t) * 2 + r + 1)
                                nc.scalar.activation(vn[:, r, :], blk(ps[b], t), ACT.Copy).then_inc(vn_d, 1)
                        for r in range(2):
                            m = 2 * p + r
                            act.wait_ge(o_tok, m + 1)
                            if p:
                                act.wait_ge(o_sq, (m - 2) * TB + TB)
                            for t in range(TB):
                                nc.scalar.activation(blk(sq[:, r, :], t), blk(G[:, m, :], t), ACT.Square,
                                                     accum_out=sso[:, m, t:t + 1]).then_inc(o_sq, 1)

                @block.gpsimd
                def _(pool):
                    for p in range(NP_):
                        for r in range(2):
                            m = 2 * p + r
                            pool.wait_ge(k_copied, m + 1)
                            for dst, cf in ((KBE, CKBE), (KD, CKD)):
                                nc.gpsimd.tensor_tensor(v4(slot(dst, r)), v4(slot(DD, r)), colb(cf, m), ALU.mult).then_inc(tok_p, 1)
                        for r in range(2):
                            m = 2 * p + r
                            pool.wait_ge(dif, m + 1)
                            nc.gpsimd.affine_select(out=v4(slot(DD, r)), in_=v4(slot(DD, r)), compare_op=ALU.is_ge, fill=NEG, base=0,
                                                    pattern=[[0, TB], [1, P]], channel_multiplier=-1).then_inc(dif_m, 1)
                        for r in range(2):
                            m = 2 * p + r
                            pool.wait_ge(qkt_d, m + 1)
                            nc.gpsimd.affine_select(out=v4(slot(DD, r)), in_=v4(slot(DD, r)), compare_op=ALU.is_gt, fill=0.0, base=0,
                                                    pattern=[[0, TB], [1, P]], channel_multiplier=-1).then_inc(strict, 1)
                        for l in range(LV):
                            for r in range(2):
                                m = 2 * p + r
                                if l == 0:
                                    pool.wait_ge(lt_d, m + 1)
                                if l >= 2:
                                    pool.wait_ge(u_mm, lvl(p, l - 2, r))
                                    if l == 2:
                                        pool.wait_ge(t_d, 2 * lvl(p, 0, r))
                                nc.gpsimd.tensor_tensor(v4(slot(BT0 + l % 2, r)), v4(slot(LT, r)),
                                                        lev[:, l, :].rearrange("p (o d) -> p o d", o=1).broadcast_to([P, TB, P]),
                                                        ALU.mult).then_inc(bt_d, 1)

            (o_ms, o_rt, o_in, o_n, o_t, o_y) = (sem(f"gdo_{x}") for x in ("ms", "rt", "inv", "n", "t", "y"))
            x0 = n["x"]
            n["x"] += DB
            OB = 4

            def x_act(act):
                act.wait_ge(o_ms, 1)
                nc.scalar.activation(sso[:, :, :], sso[:, :, :], ACT.Sqrt).then_inc(o_rt, 1)
                for hd in range(H8):
                    act.wait_ge(o_y, hd + 1)
                    nc.scalar.activation(xh[:, hd, :], F[:, hd, :], ACT.Copy).then_inc(xs_hi, 1)

            def x_dve(dve):
                nc.vector.tensor_scalar(sso[:, :, :], sso[:, :, :], 1.0 / P, EPS, ALU.mult, ALU.add).then_inc(o_ms, 1)
                dve.wait_ge(o_rt, 1)
                nc.vector.reciprocal(sso[:, :, :], sso[:, :, :]).then_inc(o_in, 1)
                dve.wait_ge(o_in, 1)
                for s in range(H8 + 3):
                    if s < H8:
                        nc.vector.tensor_tensor(v4(G[:, s, :]), v4(G[:, s, :]),
                                                sso[:, s, :].rearrange("p (t o) -> p t o", o=1).broadcast_to([P, TB, P]),
                                                ALU.mult).then_inc(o_n, 1)
                    if 2 <= s < H8 + 2:
                        hd = s - 2
                        dve.wait_ge(o_t, hd + 1)
                        nc.vector.scalar_tensor_tensor(out=F[:, hd, :], in0=ps[OB + hd % 3][:, :], scalar=vB[:, 96:97],
                                                       in1=G[:, 24 + hd, :], op0=ALU.mult, op1=ALU.mult).then_inc(o_y, 1)
                    if s >= 3:
                        hd = s - 3
                        dve.wait_ge(xs_hi, x0 + hd + 1)
                        nc.vector.tensor_tensor(xl[:, hd, :], F[:, hd, :], xh[:, hd, :].bitcast(F32), ALU.subtract).then_inc(xs_lo, 1)

            def x_pe(pe, b):
                for hd in ((0, 1, 2) if b == 0 else (b + 2,)):
                    if hd >= H8:
                        continue
                    pe.wait_ge(o_n, hd + 1)
                    if hd >= 3:
                        pe.wait_ge(o_y, hd - 2)
                    for t in range(TB):
                        ins = pe.transpose(blk(ps[OB + hd % 3], t), blk(G[:, hd, :], t), ident[:, :])
                    ins.then_inc(o_t, 1)

            sums = resid_out("gdn_out", x_act, x_dve, x_pe)

        with ExitStack() as c:
            qkv = sb("swa_qkvz", [P, 20, SEQ], ctx=c)
            vt = sb("swa_v", [P, TB, 2 * P], ctx=c)
            mask = sb("swa_mask", [P, 2 * P], ctx=c)
            snk = sb("swa_sinks", [P, 16], ctx=c)
            zp = sb("swa_zp", [P, 6, SEQ], ctx=c)
            ev0 = n["ev"]
            turn = token_turn(lambda b: qkv[:, 10 + b, :], 2, vt, lambda b: (evac, ev0 + 10 + b + 1))
            (p_in, w_con, ang_d, trig, rot_mm, rp, rope_d, z_d) = (sem(f"swa_{x}") for x in ("pin", "con", "ang", "trig", "rot", "rp", "rope", "zd"))
            with ExitStack() as c2:
                pos = sb("swa_pos", [P, SEQ], I32, ctx=c2)
                inv = sb("swa_inv", [P, 1], ctx=c2)
                tg = sb("swa_trig", [P, 4, SEQ], ctx=c2)
                rot = sb("swa_rot", [P, P], ctx=c2)
                TWO_PI = 2 * np.pi
                C1 = 6.28125
                C2 = float(np.float32(round((TWO_PI - C1) * 2 ** 20) / 2 ** 20))
                C3 = float(np.float32(TWO_PI - C1 - C2))
                MAGIC = 1.5 * 2 ** 23
                LIM = 3.1415925
                RB = 10

                def sp_tail(sp):
                    sp.dma_start(pos[:, :], I["positions_2"].broadcast_to([P, SEQ])).then_inc(p_in, 16)
                    sp.dma_start(inv[:, :], I["rope_inv_freq"]).then_inc(p_in, 16)
                    sp.dma_start(snk[:, :], I["swa_sinks_2"].broadcast_to([P, 16])).then_inc(p_in, 16)

                def pool_tail(pool):
                    nc.gpsimd.memset(rot[:, :], 0.0).then_inc(w_con, 1)
                    nc.gpsimd.memset(mask[:, :], 0.0).then_inc(w_con, 1)
                    pool.wait_ge(w_con, 2)
                    r4 = rot[:, :].rearrange("p (a b r) -> p a b r", a=2, b=2)
                    nc.gpsimd.affine_select(out=r4[:, :, 0, :], in_=r4[:, :, 0, :], compare_op=ALU.not_equal, fill=-1.0, base=-32,
                                            pattern=[[-64, 2], [-1, 32]], channel_multiplier=1).then_inc(w_con, 1)
                    nc.gpsimd.affine_select(out=r4[:, :, 1, :], in_=r4[:, :, 1, :], compare_op=ALU.not_equal, fill=1.0, base=0,
                                            pattern=[[-64, 2], [-1, 32]], channel_multiplier=1).then_inc(w_con, 1)
                    nc.gpsimd.affine_select(out=mask[:, :], in_=mask[:, :], compare_op=ALU.is_gt, fill=NEG, base=0,
                                            pattern=[[1, 2 * P]], channel_multiplier=-1).then_inc(w_con, 1)
                    pool.wait_ge(w_con, 5)
                    nc.gpsimd.affine_select(out=mask[:, :], in_=mask[:, :], compare_op=ALU.is_ge, fill=NEG, base=P,
                                            pattern=[[-1, 2 * P]], channel_multiplier=1).then_inc(w_con, 1)
                    for b in range(RB):
                        pool.wait_ge(trig, 2)
                        pool.wait_ge(evac, ev0 + b + 1)
                        pool.wait_ge(rot_mm, b + 1)
                        nc.gpsimd.tensor_tensor(qkv[:, b, :], qkv[:, b, :], tg[:, 1, :], ALU.mult).then_inc(rp, 1)

                def pe_beside(pe, k):
                    if 4 <= k < 4 + RB:
                        b = k - 4
                        pe.wait_ge(w_con, 4)
                        if b >= 2:
                            pe.wait_ge(rope_d, 2 * (b - 2) + 1)
                        pe.wait_ge(evac, ev0 + b + 1)
                        pe.matmul(ps[6 + b % 2][:, :], rot[:, :], qkv[:, b, :], start=True, stop=True).then_inc(rot_mm, 1)
                    if 14 <= k < 18:
                        turn[0](pe, k - 14, k - 13)

                def act_start(act):
                    act.wait_ge(ang_d, 7)
                    nc.scalar.activation(tg[:, 0, :], tg[:, 0, :], ACT.Sin).then_inc(trig, 1)
                    nc.scalar.activation(tg[:, 1, :], tg[:, 1, :], ACT.Sin).then_inc(trig, 1)

                def act_beside(act, k):
                    if k in (17, 19):
                        b0, b1 = (12, 16) if k == 17 else (16, 20)
                        z = qkv[:, b0:b1, :]
                        act.wait_ge(evac, ev0 + b1)
                        nc.scalar.activation(z, z, ACT.Silu).then_inc(z_d, 1)

                def dve_start(dve):
                    k_ = [0]

                    def link(ins):
                        k_[0] += 1
                        ins.then_inc(ang_d, 1)
                        dve.wait_ge(ang_d, k_[0])
                    dve.wait_ge(p_in, 48)
                    a, b_, c_, d_ = (tg[:, q, :] for q in range(4))
                    link(nc.vector.tensor_scalar(a, pos[:, :], inv[:, 0:1], None, ALU.mult))
                    link(nc.vector.tensor_scalar(c_, a, float(1 / TWO_PI), MAGIC, ALU.mult, ALU.add))
                    link(nc.vector.tensor_scalar(c_, c_, MAGIC, None, ALU.subtract))
                    for C in (C1, C2, C3):
                        nc.vector.scalar_tensor_tensor(out=a, in0=c_, scalar=-C, in1=a, op0=ALU.mult, op1=ALU.add).then_inc(rr, 1)
                        rr_n[0] += 1
                        dve.wait_ge(rr, rr_n[0])
                    link(nc.vector.tensor_scalar(b_, a, float(np.pi / 2), None, ALU.add))
                    link(nc.vector.tensor_scalar(d_, b_, float(np.pi), TWO_PI, ALU.is_gt, ALU.mult))
                    link(nc.vector.tensor_tensor(b_, b_, d_, ALU.subtract))
                    link(nc.vector.tensor_scalar(tg[:, 0:2, :], tg[:, 0:2, :], LIM, -LIM, ALU.min, ALU.max))

                def dve_beside(dve, k):
                    if 5 <= k < 5 + RB:
                        b = k - 5
                        dve.wait_ge(trig, 2)
                        dve.wait_ge(rot_mm, b + 1)
                        t = tg[:, 2 + b % 2, :]
                        scale = HD ** -0.5 if b < 8 else 1.0
                        nc.vector.scalar_tensor_tensor(out=t, in0=ps[6 + b % 2][:, :], scalar=scale, in1=tg[:, 0, :],
                                                       op0=ALU.mult, op1=ALU.mult).then_inc(rope_d, 1)
                        dve.wait_ge(rope_d, 2 * b + 1)
                        dve.wait_ge(rp, b + 1)
                        nc.vector.scalar_tensor_tensor(out=qkv[:, b, :], in0=qkv[:, b, :], scalar=scale, in1=t,
                                                       op0=ALU.mult, op1=ALU.add).then_inc(rope_d, 1)
                    if 14 <= k < 18:
                        turn[1](dve, k - 14, k - 13)

                rr = sem("swa_rr")
                rr_n = [0]
                in_proj("swa_in", vA[:, col["norm_w_2"] + 3 * DB:col["norm_w_2"] + 4 * DB], qkv, sums=sums,
                        tails=dict(sp=sp_tail, pool=pool_tail),
                        beside=dict(pe=pe_beside, act=act_beside, dve=dve_beside, act_start=act_start, dve_start=dve_start))
            with ExitStack() as c2:
                units = []
                for qb in range(TB):
                    for b in range(DB):
                        for s in range(2):
                            k0, k1 = max(qb - 1, 0), qb + 1
                            klen = (k1 - k0) * P
                            kv, hd = 2 * (b // 4) + s, 8 * (b // 4) + 4 * s + b % 4
                            units.append(dict(
                                q=qkv[HD * s:HD * s + HD, b, qb * P:qb * P + P], k=qkv[HD * s:HD * s + HD, 8 + b // 4, k0 * P:k1 * P],
                                klen=klen, add=[], mask=mask[:, 2 * P - klen:2 * P], po=HD * s, m=HD, oc=(b % 4) * P,
                                v=[vt[:, x, kv * HD:kv * HD + HD] for x in range(k0, k1)], sink=snk[:, hd:hd + 1]))
                groups = [(8 * g + 7, F[:, 4 * (g % 2):4 * (g % 2) + 4, (g // 2) * P:(g // 2) * P + P],
                           lambda b: b[:, :].rearrange("p (a q) -> p a q", a=4)) for g in range(2 * TB)]
                pe_p, dve_p, act_p = softmax_attention("swa", units, groups, zp, c2)
                with nc.Block() as block:
                    @block.tensor
                    def _(pe):
                        pe_p(pe)

                    @block.vector
                    def _(dve):
                        dve_p(dve)

                    @block.scalar
                    def _(act):
                        act_p(act)
            sums = resid_out("swa_out", *gate_x(lambda b: qkv[:, 12 + b, :]))
        final(sums)


_NAMES = ["x", "p", "g_ffn1_pre", "g_ffn1_post", "w_ffn1_gate", "w_ffn1_up", "w_ffn1_down", "g_mix_pre", "g_mix_post",
          "w_in", "g_out_sb", "g_out_ch", "rel_bias", "w_out", "g_ffn2_pre", "g_ffn2_post", "w_ffn2_gate", "w_ffn2_up",
          "w_ffn2_down", "w_ple_proj", "w_ple_gate", "g_ple_post", "positions_2", "norm_w_2", "final_norm_w_2",
          "conv_w_in_2", "conv_w_conv_2", "conv_w_out_2", "fox_w_in_2", "fox_b_f_2", "fox_w_out_2", "gdn_w_in_2",
          "gdn_w_conv_2", "gdn_a_log_2", "gdn_dt_bias_2", "gdn_norm_w_2", "gdn_w_out_2", "swa_w_in_2", "swa_sinks_2",
          "swa_w_out_2"]


def kernel(**inputs):
    import concourse.bacc as bacc
    from concourse.bass_utils import run_bass_kernel_spmd

    nc = bacc.Bacc("TRN2", target_bir_lowering=False, num_devices=1, dynamic_dma_scratch_size=1024)
    arrays, I = {}, {}
    for name in _NAMES:
        a = np.ascontiguousarray(inputs[name])
        arrays[f"in_{name}"] = a
        I[name] = nc.dram_tensor(f"in_{name}", a.shape, mybir.dt.from_np(a.dtype), kind="ExternalInput").ap()
    out = nc.dram_tensor("out", (1, SEQ, D), F32, kind="ExternalOutput").ap()
    half = HD // 2
    freq = (10000.0 ** (-(np.arange(P) % half) / half)).astype(np.float32).reshape(P, 1)
    arrays["in_rope_inv_freq"] = freq
    I["rope_inv_freq"] = nc.dram_tensor("in_rope_inv_freq", freq.shape, F32, kind="ExternalInput").ap()
    kernel_program(nc, I, out)
    r = run_bass_kernel_spmd(nc, [arrays], core_ids=[0])
    return r.results[0]["out"]
```

```python
from contextlib import ExitStack

import numpy as np
import concourse.bass as bass
from concourse import mybir

F32 = mybir.dt.float32
F32R = mybir.dt.float32r
I32 = mybir.dt.int32
ALU = mybir.AluOpType
ACT = mybir.ActivationFunctionType

P = 128
SEQ = 512
D = 1024
DB = D // P
TB = SEQ // P
D_FF = 2816
FB = D_FF // P
WB = 8
DOWN = -(-FB // WB)
PLE = 256
EPS = 1e-6
NEG = -1e30
REL = 128
HD = 64
H8 = 8
RAW = 4
SPLIT = 4
HEAD = 3
BAND_W = SEQ + P


def kernel_program(nc, I, out):
    top = ExitStack()
    with top:
        def sem(name):
            return top.enter_context(nc.semaphore(name))

        def sb(name, shape, dt=F32, ctx=top):
            return ctx.enter_context(nc.sbuf_tensor(name, shape, dt))

        def rows(w, kb0=0, kbn=None):
            v = w.rearrange("(k p) n -> p k n", p=P)
            return v if kbn is None else v[:, kb0:kb0 + kbn, :]

        w1g, w1u, w1d = (I[n][0] for n in ("w_ffn1_gate", "w_ffn1_up", "w_ffn1_down"))
        w2g, w2u, w2d = (I[n][0] for n in ("w_ffn2_gate", "w_ffn2_up", "w_ffn2_down"))
        conv_in, conv_out = I["conv_w_in_2"][0], I["conv_w_out_2"][0]
        fox_in, fox_out = I["fox_w_in_2"][0], I["fox_w_out_2"][0]
        gdn_in, gdn_out = I["gdn_w_in_2"][0], I["gdn_w_out_2"][0]
        swa_in, swa_out = I["swa_w_in_2"][0], I["swa_w_out_2"][0]

        def ffn_up_src(wg, wu):
            g, u = rows(wg), rows(wu)
            return lambda i, j: [(0, P, (g, u)[j % 2], i * (2 * P) + (j // 2) * P)]

        def ffn_down_src(wd):
            v = [rows(wd, WB * q, min(WB, FB - WB * q)) for q in range(DOWN)]
            return lambda i, j: [(0, P, v[(4 * i + j) % DOWN], (4 * i + j) // DOWN * P)]

        def plain_src(w):
            v = rows(w)
            return lambda i, j: [(0, P, v, i * (4 * P) + j * P)]

        def mix_block(i, j):
            return 4 * {4: 5, 5: 4}.get(i, i) + j if isinstance(i, int) else i * 4 + j

        def mix_src():
            v = rows(I["w_in"][0])
            return lambda i, j: [(0, P, v, mix_block(i, j) * P)]

        def ple_src():
            g, q = rows(I["w_ple_gate"][0]), rows(I["w_ple_proj"][0])
            return lambda i, j: [(0, P, (g, q)[j % 2], i * (2 * P) + (j // 2) * P)]

        def conv_src():
            v = rows(conv_in)
            return lambda i, j: [(0, P, v, i * P + j * D)]

        def fox_src():
            v = rows(fox_in)

            def src(i, j):
                if isinstance(i, int) and 4 * i + j >= 28:
                    if j == 0 and i == 7:
                        return [(0, H8, v, 4 * D)]
                    return [(0, P, v, (4 * i + j - 1) * P)]
                return [(0, P, v, i * (4 * P) + j * P)]
            return src

        def gdn_src():
            v = rows(gdn_in)

            def src(i, j):
                if isinstance(i, int) and i >= 6:
                    if i == 6 and j == 0:
                        return [(0, 2 * H8, v, 4 * D)]
                    return [(0, P, v, (4 * i + j - 1) * P)]
                return [(0, P, v, i * (4 * P) + j * P)]
            return src

        def swa_cols(b):
            kvp, m = b // 4, b % 4
            return (8 * kvp + m) * HD, (8 * kvp + 4 + m) * HD

        def swa_src():
            v = rows(swa_in)

            def src(i, j):
                k = 4 * i + j
                if k < 8:
                    a, b = swa_cols(k)
                    return [(0, HD, v, a), (HD, HD, v, b)]
                if k < 12:
                    return [(0, P, v, D + (k - 8) * P)]
                a, b = swa_cols(k - 12)
                return [(0, HD, v, D + 512 + a), (HD, HD, v, D + 512 + b)]
            return src

        stages = [
            ("ffn1_up", 2 * FB, ffn_up_src(w1g, w1u)),
            ("ffn1_down", DOWN * DB, ffn_down_src(w1d)),
            ("mix_in", 24, mix_src()),
            ("mix_out", DB, plain_src(I["w_out"][0])),
            ("ffn2_up", 2 * FB, ffn_up_src(w2g, w2u)),
            ("ffn2_down", DOWN * DB, ffn_down_src(w2d)),
            ("ple", 2 * DB, ple_src()),
            ("conv_in", 4 * DB, conv_src()),
            ("conv_out", DB, plain_src(conv_out)),
            ("fox_in", 4 * DB + 1, fox_src()),
            ("fox_out", DB, plain_src(fox_out)),
            ("gdn_in", 4 * DB + 1, gdn_src()),
            ("gdn_out", DB, plain_src(gdn_out)),
            ("swa_in", 20, swa_src()),
            ("swa_out", DB, plain_src(swa_out)),
        ]
        swa_out_halves = swa_out.rearrange("(h d) n -> d h n", d=HD)

        sources = {s[0]: s[2] for s in stages}
        tile_stage, first = [], {}
        loaded_at, slot_count = [], [0] * RAW
        for name, n, src in stages:
            first[name] = len(tile_stage)
            for k in range(n):
                slot = len(tile_stage) % RAW
                n_dma = 4 if name == "swa_out" else len(src(k // 4, k % 4))
                slot_count[slot] += 16 * n_dma
                loaded_at.append(slot_count[slot])
                if name == "ple" and k % 2:
                    kb = PLE // P
                elif name.endswith("_down"):
                    kb = min(WB, FB - WB * (k % DOWN))
                else:
                    kb = DB
                tile_stage.append((name, k, kb))
        n_tiles = len(tile_stage)
        tiles_of = {s[0]: s[1] for s in stages}

        h = sb("h", [P, DB, SEQ])
        xh = sb("xh", [P, DB, SEQ], F32R)
        xl = sb("xl", [P, DB, SEQ], F32R)
        F = sb("F", [P, DB, SEQ])
        raw = [sb(f"raw{s}", [P, WB, P]) for s in range(RAW)]
        wh = [sb(f"wh{s}", [P, WB, P], F32R) for s in range(SPLIT)]
        wl = [sb(f"wl{s}", [P, WB, P], F32R) for s in range(SPLIT)]
        acc = sb("acc", [P, SEQ])
        sq = sb("sq", [P, 2, SEQ])
        rcol = sb("rms_col", [P, TB])
        rstd = sb("rstd", [P, SEQ])
        ident = sb("ident", [P, P])
        ones = sb("ones", [P, P])
        vA = sb("vA", [P, P])
        vB = sb("vB", [P, 97])
        half = sb("half", [P, 2, DB])
        ps = [top.enter_context(nc.psum_tensor(f"ps{b}", [P, SEQ], F32)) for b in range(8)]
        STAT = 7

        loaded = [sem(f"loaded{s}") for s in range(RAW)]
        hi_done, lo_done, tile_done = sem("hi_done"), sem("lo_done"), sem("tile_done")

        def wait(eng, s, v):
            if not isinstance(v, int) or v > 0:
                eng.wait_ge(s, v)

        def load(sp, name, i, j, k_ahead=0, split_at=None):
            t0 = first[name]
            if isinstance(i, int):
                t = t0 + 4 * i + j + k_ahead
                if t >= n_tiles:
                    return
                name, k, kb = tile_stage[t]
                i, j = k // 4, k % 4
                slot = t % RAW
            else:
                j += k_ahead
                slot, kb = (t0 + j) % RAW, tile_stage[t0 + j][2]
                i, j = i + j // 4, j % 4
            if name == "swa_out":
                if split_at is not None:
                    sp.wait_ge(lo_done, split_at)
                n0 = (4 * i + j) * P
                for kvp in range(2):
                    for upper in range(2):
                        h0 = 8 * kvp + 4 * upper
                        sp.dma_start(raw[slot][upper * HD:upper * HD + HD, 4 * kvp:4 * kvp + 4, :],
                                     swa_out_halves[:, h0:h0 + 4, n0:n0 + P]).then_inc(loaded[slot], 16)
                return
            parts = [(c0, w, view, c if isinstance(c, int) else sp.snap(c)) for c0, w, view, c in sources[name](i, j)]
            if split_at is not None:
                sp.wait_ge(lo_done, split_at)
            for c0, w, view, c in parts:
                sp.dma_start(raw[slot][:, 0:kb, c0:c0 + w], view[:, :, bass.ds(c, w)]).then_inc(loaded[slot], 16)

        def tile_at(name, i, j, ahead):
            t0 = first[name]
            if isinstance(i, int):
                t = t0 + 4 * i + j + ahead
                if t >= n_tiles:
                    return None
                return t % RAW, t % SPLIT, tile_stage[t][2], t, loaded_at[t]
            s = t0 + j + ahead
            return s % RAW, s % SPLIT, tile_stage[s][2], i * 4 + s, i * 16 + loaded_at[s]

        def split_hi(act, name, i, j, ahead=HEAD):
            at = tile_at(name, i, j, ahead)
            if at is None:
                return
            r, s, kb, t, got = at
            act.wait_ge(loaded[r], got)
            wait(act, tile_done, t - SPLIT + 1)
            nc.scalar.activation(wh[s][:, 0:kb, :], raw[r][:, 0:kb, :], ACT.Copy).then_inc(hi_done, 1)

        def split_lo(dve, name, i, j, ahead=HEAD):
            at = tile_at(name, i, j, ahead)
            if at is None:
                return
            r, s, kb, t, got = at
            dve.wait_ge(loaded[r], got)
            dve.wait_ge(hi_done, t + 1)
            nc.vector.tensor_tensor(wl[s][:, 0:kb, :], raw[r][:, 0:kb, :], wh[s][:, 0:kb, :].bitcast(F32),
                                    ALU.subtract).then_inc(lo_done, 1)

        def load_steps(sp, name, loop_end=None, beside=None):
            def body(i, j):
                load(sp, name, i, j, RAW, i * 4 + (first[name] + j + 1))
                if beside is not None and isinstance(i, int):
                    beside(sp, 4 * i + j)
            steps(sp, name, body, None if loop_end is None else loop_end - 1)

        def steps(eng, name, body, loop_end=None):
            n = tiles_of[name]
            full = n // 4
            if full < 4 or name == "swa_in" or name.endswith("_down"):
                for k in range(n):
                    body(k // 4, k % 4)
                return
            for j in range(4):
                body(0, j)
            end = full - 1 if loop_end is None else loop_end
            with eng.Fori(1, end) as i:
                for j in range(4):
                    body(i, j)
            for k in range(4 * end, n):
                body(k // 4, k % 4)

        def mm3(pe, o, s, kb, x_hi, x_lo, start, stop):
            pe.matmul(o, wh[s][:, kb, :], x_hi, start=start, stop=False)
            pe.matmul(o, wh[s][:, kb, :], x_lo, start=False, stop=False)
            return pe.matmul(o, wl[s][:, kb, :], x_hi, start=False, stop=stop)

        xs_hi, xs_lo = sem("x_hi_done"), sem("x_lo_done")
        h_new = sem("h_new")
        f_scaled = sem("f_scaled")
        sq_done, acc_done = sem("sq_done"), sem("acc_done")
        stat_mm, ms_done, inv_done, root_done = sem("stat_mm"), sem("ms_done"), sem("inv_done"), sem("root_done")
        spread, rstd_done = sem("rstd_spread"), sem("rstd_done")
        evac = sem("psum_evacuated")
        n = dict(x=0, h=0, fs=0, sq=0, acc=0, stat=0, ev=0, units=0, groups=0, lots=0, ffn=0)

        def sums_pe(pe, acc_at, sq_at):
            for q, src in enumerate((acc[:, :], sq[:, 1, :])):
                pe.wait_ge(*((acc_done, acc_at) if q == 0 else (sq_done, sq_at)))
                for t in range(TB):
                    m = pe.matmul(ps[STAT][:, q * TB + t:q * TB + t + 1], src[:, t * P:t * P + P], ones[:, 0:1],
                                  start=True, stop=True)
                m.then_inc(stat_mm, 1)

        def inverse_dve(dve, at, width):
            dve.wait_ge(stat_mm, 2 * at + 2)
            nc.vector.tensor_scalar(rcol[:, :], ps[STAT][:, 0:TB], 1.0 / width, EPS, ALU.mult, ALU.add).then_inc(ms_done, 1)
            dve.wait_ge(ms_done, 2 * at + 1)
            nc.vector.scalar_tensor_tensor(out=rcol[:, :], in0=ps[STAT][:, TB:2 * TB], scalar=1.0 / width, in1=rcol[:, :],
                                           op0=ALU.mult, op1=ALU.add).then_inc(ms_done, 1)
            dve.wait_ge(ms_done, 2 * at + 2)
            nc.vector.reciprocal(rcol[:, :], rcol[:, :]).then_inc(inv_done, 1)

        def root_act(act, at):
            act.wait_ge(inv_done, at + 1)
            nc.scalar.activation(rcol[:, :], rcol[:, :], ACT.Sqrt).then_inc(root_done, 1)

        def spread_pe(pe, at):
            pe.wait_ge(root_done, at + 1)
            for t in range(TB):
                m = pe.matmul(ps[STAT][:, t * P:t * P + P], rcol[:, t:t + 1].broadcast_to([P, P]), ident[:, :],
                              start=True, stop=True)
            m.then_inc(spread, 1)

        def rstd_dve(dve, at):
            dve.wait_ge(spread, at + 1)
            nc.vector.tensor_copy(rstd[:, :], ps[STAT][:, :]).then_inc(rstd_done, 1)

        class Prologue:

            def __init__(self, gain=None, update=None, squares=True):
                self.gain, self.update, self.squares = gain, update, squares
                self.x0, self.h0, self.fs0 = n["x"], n["h"], n["fs"]
                self.sq0, self.acc0, self.stat0 = n["sq"], n["acc"], n["stat"]
                n["x"] += DB
                if update is not None:
                    n["h"] += DB
                    n["fs"] += DB
                if squares:
                    n["sq"] += DB
                    n["acc"] += DB - 1
                self.sums = (n["acc"], n["sq"])

            def act(self, act, after=()):
                after = dict(after)
                for b in range(DB):
                    if b in after:
                        after[b](act)
                    if self.update is not None:
                        act.wait_ge(h_new, self.h0 + b + 1)
                    g = 1.0 if self.gain is None else self.gain[:, b:b + 1]
                    nc.scalar.activation(xh[:, b, :], h[:, b, :], ACT.Copy, scale=g).then_inc(xs_hi, 1)
                    if self.squares:
                        if b >= 2:
                            act.wait_ge(acc_done, self.acc0 + b - 1)
                        nc.scalar.activation(sq[:, b % 2, :], h[:, b, :], ACT.Square).then_inc(sq_done, 1)

            def dve(self, dve, after=()):
                after = dict(after)
                for b in range(DB):
                    if b in after:
                        after[b](dve)
                    if self.update is not None:
                        nc.vector.tensor_tensor(F[:, b, :], F[:, b, :], rstd[:, :], ALU.mult).then_inc(f_scaled, 1)
                        dve.wait_ge(f_scaled, self.fs0 + b + 1)
                        nc.vector.scalar_tensor_tensor(out=h[:, b, :], in0=F[:, b, :], scalar=self.update[:, b:b + 1],
                                                       in1=h[:, b, :], op0=ALU.mult, op1=ALU.add).then_inc(h_new, 1)
                        if b == 0:
                            continue
                        self.low(dve, b - 1)
                    else:
                        self.low(dve, b)
                if self.update is not None:
                    self.low(dve, DB - 1)

            def low(self, dve, b):
                dve.wait_ge(xs_hi, self.x0 + b + 1)
                if self.gain is None:
                    nc.vector.tensor_tensor(xl[:, b, :], h[:, b, :], xh[:, b, :].bitcast(F32),
                                            ALU.subtract).then_inc(xs_lo, 1)
                else:
                    nc.vector.scalar_tensor_tensor(out=xl[:, b, :], in0=h[:, b, :], scalar=self.gain[:, b:b + 1],
                                                   in1=xh[:, b, :].bitcast(F32), op0=ALU.mult,
                                                   op1=ALU.subtract).then_inc(xs_lo, 1)

            def pool(self, pool):
                if self.squares:
                    sum_squares(pool, self.sq0, self.acc0)

        def sum_squares(pool, sq0, acc0):
            for b in range(DB - 1):
                pool.wait_ge(sq_done, sq0 + b + 1)
                if b == 0:
                    nc.gpsimd.tensor_copy(acc[:, :], sq[:, 0, :]).then_inc(acc_done, 1)
                else:
                    pool.wait_ge(acc_done, acc0 + b)
                    nc.gpsimd.tensor_tensor(acc[:, :], acc[:, :], sq[:, b % 2, :], ALU.add).then_inc(acc_done, 1)

        def head_mm(pe, tiles, t, b, x_ready, x_hi, x_lo):
            pe.wait_ge(xs_hi, x_ready + b + 1)
            for g in tiles:
                s = (t + g) % SPLIT
                pe.matmul(ps[g][:, :], wh[s][:, b, :], x_hi[:, b, :], start=b == 0, stop=False)
                pe.matmul(ps[g][:, :], wl[s][:, b, :], x_hi[:, b, :], start=False, stop=False)
            pe.wait_ge(xs_lo, x_ready + b + 1)
            for g in tiles:
                last = pe.matmul(ps[g][:, :], wh[(t + g) % SPLIT][:, b, :], x_lo[:, b, :], start=False, stop=b == DB - 1)
                if b == DB - 1:
                    last.then_inc(tile_done, 1 if len(tiles) == HEAD or g else 2)

        def output_of(i, j, parts):
            if parts == 1:
                return i * 4 + j, j, 0
            k = 4 * i + j
            return k // parts, k // parts % 4, k % parts

        def pe_tiles(pe, name, x_hi, x_lo, ev0, x_ready=None, parts=1, sums=None, at=None,
                     beside=None, loop_end=None, x_pe=None):
            def body(i, j):
                r, s, kb, t, got = tile_at(name, i, j, 0)
                o, bank, part = output_of(i, j, parts)
                first_i = isinstance(i, int) and i == 0
                if first_i and x_ready is not None and j < HEAD:
                    if j:
                        return
                    pe.wait_ge(lo_done, t + HEAD)
                    for b in range(kb):
                        if at is not None and sums is None and b == 4:
                            spread_pe(pe, at)
                        if x_pe is not None:
                            x_pe(pe, b)
                        head_mm(pe, range(HEAD), t, b, x_ready, x_hi, x_lo)
                    if sums is not None:
                        sums_pe(pe, *sums)
                    return
                pe.wait_ge(lo_done, t + 1)
                if part == 0:
                    wait(pe, evac, ev0 + o - 3)
                for b in range(kb):
                    if first_i and j == HEAD and b == 2 and sums is not None:
                        spread_pe(pe, at)
                    xb = part * WB + b
                    last = mm3(pe, ps[bank][:, :], s, b, x_hi[:, xb, :], x_lo[:, xb, :],
                               xb == 0, part == parts - 1 and b == kb - 1)
                last.then_inc(tile_done, 1)
                if beside is not None and isinstance(i, int):
                    beside(pe, 4 * i + j)
            steps(pe, name, body, loop_end)

        def in_proj(name, gain, dst, update=None, sums=None, tails=(), evac_dve=None, evac_act=None, loop_end=None,
                    beside=(), between_dve=None):
            pro = Prologue(gain, update, squares=sums is None)
            st = n["stat"]
            n["stat"] += 1
            ev0 = n["ev"]
            n["ev"] += tiles_of[name]
            t0 = first[name]
            tails, beside = dict(tails), dict(beside)
            with nc.Block() as block:
                @block.sync
                def _(sp):
                    if "sp" in tails:
                        tails["sp"](sp)
                    load_steps(sp, name, loop_end, beside.get("sp"))

                @block.gpsimd
                def _(pool):
                    pro.pool(pool)
                    if "pool" in tails:
                        tails["pool"](pool)

                @block.scalar
                def _(act):
                    pro.act(act, {} if sums is None else {2: lambda e: root_act(e, st)})
                    if "act_start" in beside:
                        beside["act_start"](act)

                    def body(i, j):
                        split_hi(act, name, i, j)
                        if sums is None and isinstance(i, int) and i == 0 and j == 0:
                            root_act(act, st)
                        if evac_act is not None:
                            evac_act(act, i, j, ev0)
                        if "act" in beside and isinstance(i, int):
                            beside["act"](act, 4 * i + j)
                    steps(act, name, body, loop_end)
                    if "act" in tails:
                        tails["act"](act, ev0)

                @block.vector
                def _(dve):
                    pro.dve(dve, {} if sums is None else {2: lambda e: inverse_dve(e, st, D), 6: lambda e: rstd_dve(e, st)})
                    if "dve_start" in beside:
                        beside["dve_start"](dve)

                    def body(i, j):
                        if between_dve is not None:
                            between_dve(dve, i, j, 1)
                        split_lo(dve, name, i, j)
                        if between_dve is not None:
                            between_dve(dve, i, j, 2)
                        if isinstance(i, int) and i == 0 and j == 0:
                            if sums is None:
                                inverse_dve(dve, st, D)
                                rstd_dve(dve, st)
                            dve.wait_ge(rstd_done, st + 1)
                        dve.wait_ge(tile_done, i * 4 + (t0 + j + 1))
                        if evac_dve is not None:
                            evac_dve(dve, i, j, ev0)
                        else:
                            k = i * 4 + j
                            nc.vector.tensor_tensor(dst[:, bass.ds(k, 1), :],
                                                    ps[j][:, :].rearrange("p (o q) -> p o q", o=1),
                                                    rstd[:, :].rearrange("p (o q) -> p o q", o=1), ALU.mult).then_inc(evac, 1)
                        if "dve" in beside and isinstance(i, int):
                            beside["dve"](dve, 4 * i + j)
                    steps(dve, name, body, loop_end)
                    if "dve" in tails:
                        tails["dve"](dve, ev0)

                @block.tensor
                def _(pe):
                    if sums is not None:
                        sums_pe(pe, *sums)
                    pe_tiles(pe, name, xh, xl, ev0, x_ready=pro.x0, sums=None if sums is not None else pro.sums, at=st,
                             beside=beside.get("pe"), loop_end=loop_end)
                    if "pe" in tails:
                        tails["pe"](pe, ev0)
            return ev0

        vec_rows = []
        for nm in ("g_ffn1_pre", "g_ffn1_post", "g_mix_pre", "g_mix_post", "g_ffn2_pre", "g_ffn2_post", "g_ple_post",
                   "g_out_sb", "g_out_ch", "norm_w_2", "final_norm_w_2", "conv_w_conv_2"):
            a = I[nm]
            if len(a.shape) == 1:
                v = a.rearrange("(r c) -> r c", c=P)
            elif len(a.shape) == 2:
                v = a.rearrange("a (r c) -> (a r) c", c=P)
            else:
                v = a.rearrange("a k (r c) -> (a k r) c", c=P)
            vec_rows.append((nm, v))
        col = {}
        at = 0
        for nm, v in vec_rows:
            col[nm] = at
            at += v.shape[0]
        assert at == P
        gdn_conv_rows = I["gdn_w_conv_2"].rearrange("a k (r c) -> (a k r) c", c=P)

        def gains(nm, first_=0, m=DB):
            return vA[:, col[nm] + first_:col[nm] + first_ + m]

        boot = ExitStack()
        with boot:
            xt = sb("xt", [P, TB, D], ctx=boot)
            vrow = sb("vrow", [P, 2, P], ctx=boot)
            vec_in, x_in = sem("vec_in"), [sem(f"x_in{t}") for t in range(TB)]
            const = sem("const_ready")
            tr, tr_out = sem("boot_transposed"), sem("boot_copied")
            n_vec = 16 * (len(vec_rows) + 2)
            with nc.Block() as block:
                @block.sync
                def _(sp):
                    for t in range(TB):
                        sp.dma_start(xt[:, t, :], I["x"][0, t * P:t * P + P, :]).then_inc(x_in[t], 16)
                    for nm, v in vec_rows:
                        sp.dma_start(vrow[col[nm]:col[nm] + v.shape[0], 0, :], v).then_inc(vec_in, 16)
                    sp.dma_start(vrow[0:96, 1, :], gdn_conv_rows).then_inc(vec_in, 16)
                    sp.dma_start(vrow[96:97, 1, :], I["gdn_norm_w_2"]).then_inc(vec_in, 16)
                    for k in range(RAW):
                        load(sp, "ffn1_up", 0, k)

                @block.gpsimd
                def _(pool):
                    nc.gpsimd.memset(ones[:, :], 1.0).then_inc(const, 1)
                    nc.gpsimd.memset(ident[:, :], 0.0).then_inc(const, 1)
                    pool.wait_ge(const, 2)
                    nc.gpsimd.affine_select(out=ident[:, :], in_=ident[:, :], compare_op=ALU.not_equal, fill=1.0,
                                            base=0, pattern=[[-1, P]], channel_multiplier=1).then_inc(const, 1)

                @block.tensor
                def _(pe):
                    pe.wait_ge(const, 3)
                    for t in range(TB):
                        pe.wait_ge(x_in[t], 16)
                        for b in range(DB):
                            m = pe.transpose(ps[b][:, t * P:t * P + P], xt[:, t, b * P:b * P + P], ident[:, :])
                            if t == TB - 1:
                                m.then_inc(tr, 1)
                    pe.wait_ge(vec_in, n_vec)
                    pe.wait_ge(tr_out, 6)
                    pe.transpose(ps[4][:, 0:P], vrow[:, 0, :], ident[:, :]).then_inc(tr, 1)
                    pe.transpose(ps[5][:, 0:97], vrow[0:97, 1, :], ident[0:97, 0:97]).then_inc(tr, 1)

                @block.vector
                def _(dve):
                    for b in range(DB):
                        dve.wait_ge(tr, b + 1)
                        nc.vector.tensor_copy(h[:, b, :], ps[b][:, :]).then_inc(tr_out, 1)
                    dve.wait_ge(tr, DB + 1)
                    nc.vector.tensor_copy(vA[:, :], ps[4][:, 0:P]).then_inc(tr_out, 1)
                    dve.wait_ge(tr, DB + 2)
                    nc.vector.tensor_copy(vB[:, :], ps[5][:, 0:97]).then_inc(tr_out, 1)
                    dve.wait_ge(tr_out, DB + 1)
                    nc.vector.tensor_scalar(half[:, 0, :], gains("g_ffn1_post"), 0.5, None, ALU.mult)
                    nc.vector.tensor_scalar(half[:, 1, :], gains("g_ffn2_post"), 0.5, None, ALU.mult)
                    for k in range(HEAD):
                        split_lo(dve, "ffn1_up", 0, k, 0)

                @block.scalar
                def _(act):
                    for k in range(HEAD):
                        split_hi(act, "ffn1_up", 0, k, 0)

        g_done, silu_done, sr_done, prod, up_hi = (sem(f"ffn_{x}") for x in ("gate", "silu", "silur", "prod", "ahi"))

        def ffn_up(name, gain, update, act_hi, act_lo, ctx):
            S = F[:, 0:2, :]
            SR = F[:, 2:4, :]
            p0 = n["ffn"]
            n["ffn"] += FB
            pro = Prologue(gain, update)
            st = n["stat"]
            n["stat"] += 1
            ev0 = n["ev"]
            n["ev"] += 2 * FB
            t0 = first[name]
            with nc.Block() as block:
                @block.sync
                def _(sp):
                    load_steps(sp, name)

                @block.gpsimd
                def _(pool):
                    pro.pool(pool)

                    def body(i, j):
                        if j % 2 == 1:
                            p, s = i * 2 + j // 2, (j // 2) % 2
                            pool.wait_ge(silu_done, p + (p0 + 1))
                            wait(pool, prod, p + (p0 - 1))
                            nc.gpsimd.tensor_tensor(SR[:, s, :], S[:, s, :], rstd[:, :], ALU.mult).then_inc(sr_done, 1)
                    steps(pool, name, body)

                @block.scalar
                def _(act):
                    pro.act(act)

                    def body(i, j):
                        split_hi(act, name, i, j)
                        if isinstance(i, int) and i == 0 and j == 0:
                            root_act(act, st)
                        p, s = i * 2 + j // 2, (j // 2) % 2
                        if j % 2 == 0:
                            act.wait_ge(g_done, p + (p0 + 1))
                            wait(act, sr_done, p + (p0 - 1))
                            nc.scalar.activation(S[:, s, :], ps[j][:, :], ACT.Silu).then_inc(silu_done, 1)
                        else:
                            act.wait_ge(prod, p + (p0 + 1))
                            nc.scalar.activation(act_hi[:, bass.ds(p, 1), :], ps[j][:, :].rearrange("p (o q) -> p o q", o=1),
                                                 ACT.Copy).then_inc(up_hi, 1)
                    steps(act, name, body)

                @block.vector
                def _(dve):
                    pro.dve(dve)

                    def body(i, j):
                        split_lo(dve, name, i, j)
                        if isinstance(i, int) and i == 0 and j == 0:
                            inverse_dve(dve, st, D)
                            rstd_dve(dve, st)
                            dve.wait_ge(rstd_done, st + 1)
                        p, s = i * 2 + j // 2, (j // 2) % 2
                        dve.wait_ge(tile_done, i * 4 + (t0 + j + 1))
                        if j % 2 == 0:
                            nc.vector.tensor_tensor(ps[j][:, :], ps[j][:, :], rstd[:, :], ALU.mult).then_inc(g_done, 1)
                        else:
                            dve.wait_ge(sr_done, p + (p0 + 1))
                            nc.vector.tensor_tensor(ps[j][:, :], ps[j][:, :], SR[:, s, :], ALU.mult).then_inc(prod, 1)
                            dve.wait_ge(up_hi, p + (p0 + 1))
                            nc.vector.tensor_tensor(act_lo[:, bass.ds(p, 1), :], ps[j][:, :].rearrange("p (o q) -> p o q", o=1),
                                                    act_hi[:, bass.ds(p, 1), :].bitcast(F32), ALU.subtract).then_inc(evac, 2)
                    steps(dve, name, body)

                @block.tensor
                def _(pe):
                    pe_tiles(pe, name, xh, xl, ev0, x_ready=pro.x0, sums=pro.sums, at=st)

        def post_out(name, x_hi, x_lo, parts=1, x=None):
            x_act, x_dve, x_pe = (None, None, None) if x is None else x
            x_ready = None if x is None else n["x"] - DB
            ev0, sq0, acc0, st = n["ev"], n["sq"], n["acc"], n["stat"]
            n["ev"] += DB
            n["sq"] += DB
            n["acc"] += DB - 1
            n["stat"] += 1
            t0 = first[name]
            with nc.Block() as block:
                @block.sync
                def _(sp):
                    load_steps(sp, name)

                @block.gpsimd
                def _(pool):
                    sum_squares(pool, sq0, acc0)

                @block.scalar
                def _(act):
                    if x_act is not None:
                        x_act(act)

                    def body(i, j):
                        split_hi(act, name, i, j)
                        o, bank, part = output_of(i, j, parts)
                        if part == parts - 1:
                            act.wait_ge(tile_done, i * 4 + (t0 + j + 1))
                            wait(act, acc_done, acc0 + o - 1 if not (isinstance(o, int) and o < 2) else 0)
                            nc.scalar.activation(sq[:, bank % 2, :], ps[bank][:, :], ACT.Square).then_inc(sq_done, 1)
                            nc.scalar.activation(F[:, o:o + 1, :] if isinstance(o, int) else F[:, bass.ds(o, 1), :],
                                                 ps[bank][:, :].rearrange("p (o q) -> p o q", o=1), ACT.Copy).then_inc(evac, 1)
                    steps(act, name, body)
                    root_act(act, st)

                @block.vector
                def _(dve):
                    if x_dve is not None:
                        x_dve(dve)

                    def body(i, j):
                        split_lo(dve, name, i, j)
                    steps(dve, name, body)
                    inverse_dve(dve, st, D)
                    rstd_dve(dve, st)

                @block.tensor
                def _(pe):
                    pe_tiles(pe, name, x_hi, x_lo, ev0, x_ready=x_ready, parts=parts, x_pe=x_pe)
                    sums_pe(pe, acc0 + DB - 1, sq0 + DB)
                    spread_pe(pe, st)

        def resid_out(name, x_act, x_dve, x_pe=None):
            ev0, sq0, acc0 = n["ev"], n["sq"], n["acc"]
            n["ev"] += DB
            n["sq"] += DB
            n["acc"] += DB - 1
            t0 = first[name]
            x_ready = n["x"] - DB
            with nc.Block() as block:
                @block.sync
                def _(sp):
                    load_steps(sp, name)

                @block.gpsimd
                def _(pool):
                    sum_squares(pool, sq0, acc0)

                @block.scalar
                def _(act):
                    x_act(act)

                    def body(i, j):
                        k = 4 * i + j
                        split_hi(act, name, i, j)
                        act.wait_ge(evac, ev0 + k + 1)
                        wait(act, acc_done, acc0 + k - 1 if k >= 2 else 0)
                        nc.scalar.activation(sq[:, k % 2, :], h[:, k, :], ACT.Square).then_inc(sq_done, 1)
                    steps(act, name, body)

                @block.vector
                def _(dve):
                    x_dve(dve)

                    def body(i, j):
                        k = 4 * i + j
                        split_lo(dve, name, i, j)
                        dve.wait_ge(tile_done, t0 + k + 1)
                        nc.vector.tensor_tensor(h[:, k, :], ps[j][:, :], h[:, k, :], ALU.add).then_inc(evac, 1)
                    steps(dve, name, body)

                @block.tensor
                def _(pe):
                    pe_tiles(pe, name, xh, xl, ev0, x_ready=x_ready, x_pe=x_pe)
            return acc0 + DB - 1, sq0 + DB

        def split_x(src):
            x0 = n["x"]
            n["x"] += DB

            def x_act(act):
                for b in range(DB):
                    nc.scalar.activation(xh[:, b, :], src(b), ACT.Copy).then_inc(xs_hi, 1)

            def x_dve(dve):
                for b in range(DB):
                    dve.wait_ge(xs_hi, x0 + b + 1)
                    nc.vector.tensor_tensor(xl[:, b, :], src(b), xh[:, b, :].bitcast(F32), ALU.subtract).then_inc(xs_lo, 1)
            return x_act, x_dve

        def gate_x(zb):
            x0, f0 = n["x"], n["fs"]
            n["x"] += DB
            n["fs"] += DB

            def x_act(act):
                for b in range(DB):
                    act.wait_ge(f_scaled, f0 + b + 1)
                    nc.scalar.activation(xh[:, b, :], F[:, b, :], ACT.Copy).then_inc(xs_hi, 1)

            def x_dve(dve):
                for b in range(DB + 1):
                    if b < DB:
                        nc.vector.tensor_tensor(F[:, b, :], F[:, b, :], zb(b), ALU.mult).then_inc(f_scaled, 1)
                    if b >= 1:
                        dve.wait_ge(xs_hi, x0 + b)
                        nc.vector.tensor_tensor(xl[:, b - 1, :], F[:, b - 1, :], xh[:, b - 1, :].bitcast(F32),
                                                ALU.subtract).then_inc(xs_lo, 1)
            return x_act, x_dve

        def final(sums):
            with ExitStack() as c:
                fo = sb("final_o", [P, DB, SEQ], ctx=c)
                res = sb("final_res", [P, TB, D], ctx=c)
                g_act, g_dve, ft, e_act, e_dve, stored = (sem(f"final_{x}") for x in (
                    "gained_act", "gained_dve", "turned", "copied_act", "copied_dve", "stored"))
                st = n["stat"]
                n["stat"] += 1
                g = gains("final_norm_w_2")

                def place(q):
                    return res[:, q % TB, q // TB * SEQ:q // TB * SEQ + SEQ]

                with nc.Block() as block:
                    @block.tensor
                    def _(pe):
                        sums_pe(pe, *sums)
                        for q in range(2 * TB):
                            if q % TB == 0:
                                pe.wait_ge(g_act, 2 * (q // TB) + 2)
                                pe.wait_ge(g_dve, 2 * (q // TB) + 2)
                            if q == STAT:
                                pe.wait_ge(e_dve, 1)
                            for c in range(4):
                                m = pe.transpose(ps[q % STAT][:, c * P:c * P + P],
                                                 fo[:, 4 * (q // TB) + c, (q % TB) * P:(q % TB) * P + P], ident[:, :])
                            m.then_inc(ft, 1)

                    @block.vector
                    def _(dve):
                        for b in range(1, DB, 2):
                            nc.vector.tensor_scalar(fo[:, b, :], h[:, b, :], g[:, b:b + 1], None, ALU.mult).then_inc(g_dve, 1)
                        inverse_dve(dve, st, D)
                        dve.wait_ge(root_done, st + 1)
                        for q in range(0, 2 * TB, 2):
                            dve.wait_ge(ft, q + 1)
                            nc.vector.tensor_scalar(place(q), ps[q % STAT][:, :], rcol[:, q % TB:q % TB + 1], None,
                                                    ALU.mult).then_inc(e_dve, 1)

                    @block.scalar
                    def _(act):
                        for b in range(0, DB, 2):
                            nc.scalar.activation(fo[:, b, :], h[:, b, :], ACT.Copy, scale=g[:, b:b + 1]).then_inc(g_act, 1)
                        root_act(act, st)
                        act.wait_ge(root_done, st + 1)
                        for q in range(1, 2 * TB, 2):
                            act.wait_ge(ft, q + 1)
                            nc.scalar.activation(place(q), ps[q % STAT][:, :], ACT.Copy, scale=rcol[:, q % TB:q % TB + 1]).then_inc(e_act, 1)

                    @block.sync
                    def _(sp):
                        for q in range(2 * TB):
                            sp.wait_ge(*((e_act, q // 2 + 1) if q % 2 else (e_dve, q // 2 + 1)))
                            sp.dma_start(out[0, (q % TB) * P:(q % TB) * P + P, q // TB * SEQ:q // TB * SEQ + SEQ],
                                         place(q)).then_inc(stored, 16)
                        sp.wait_ge(stored, 16 * 2 * TB)

        with ExitStack() as c:
            a_hi = sb("a_hi1", [P, FB, SEQ], F32R, ctx=c)
            a_lo = sb("a_lo1", [P, FB, SEQ], F32R, ctx=c)
            with ExitStack() as c2:
                ffn_up("ffn1_up", gains("g_ffn1_pre"), None, a_hi, a_lo, c2)
            post_out("ffn1_down", a_hi, a_lo, DOWN)

        turned, taken = sem("values_turned"), sem("values_taken")

        def token_turn(v_of, blocks, dst, v_ready, bank=4):
            lots = [(t, g) for g in range(-(-blocks // 4)) for t in range(TB)]
            q00 = n["lots"]
            n["lots"] += len(lots)

            def pe_part(pe, q0=0, q1=len(lots)):
                for q in range(q0, q1):
                    t, g = lots[q]
                    if q == 0 or lots[q - 1][1] != g:
                        pe.wait_ge(*v_ready(min(4 * g + 4, blocks) - 1))
                    if q >= 2:
                        pe.wait_ge(taken, q00 + q - 1)
                    for b in range(4 * g, min(4 * g + 4, blocks)):
                        m = pe.transpose(ps[bank + q % 2][:, (b % 4) * P:(b % 4) * P + P],
                                         v_of(b)[:, t * P:t * P + P], ident[:, :])
                    m.then_inc(turned, 1)

            def dve_part(dve, q0=0, q1=len(lots)):
                for q in range(q0, q1):
                    t, g = lots[q]
                    w = (min(4 * g + 4, blocks) - 4 * g) * P
                    dve.wait_ge(turned, q00 + q + 1)
                    nc.vector.tensor_copy(dst[:, t, g * 4 * P:g * 4 * P + w], ps[bank + q % 2][:, 0:w]).then_inc(taken, 1)
            return pe_part, dve_part

        (scored, z_done, nm_done, p_done, ri_done, p_scaled, t_done, pt_done, pv_done, o_taken) = (
            sem(f"att_{x}") for x in ("scored", "z", "negmax", "exp", "inv", "scaled", "turned", "pt", "pv", "otaken"))
        e_sink, den_done = sem("att_expsink"), sem("att_den")

        def softmax_attention(name, units, groups, room, ctx, pe_first=None, act_first=None):
            U = len(units)
            Z, PT = room[:, 0:4, :], room[:, 4:6, :]
            cols = sb(f"{name}_cols", [P, 5, U], ctx=ctx)
            MX, NM, RS, RI, ES = range(5)
            B, BG = n["units"], n["groups"]
            n["units"] += U
            n["groups"] += len(groups)
            sinks = units[0].get("sink") is not None
            group_of, start = {}, 0
            for g, (last, _, _) in enumerate(groups):
                for u in range(start, last + 1):
                    group_of[u] = g
                start = last + 1
            last_of = {last: g for g, (last, _, _) in enumerate(groups)}

            def pe_part(pe):
                for s in range(U + 3):
                    if pe_first is not None:
                        pe_first(pe, s)
                    if s < U:
                        u, d = s, units[s]
                        if u >= 3:
                            pe.wait_ge(z_done, B + u - 2)
                        o = ps[u % 3][:, 0:d["klen"]]
                        pe.matmul(o, d["q"], d["k"], start=True, stop=True).then_inc(scored, 1)
                    if 2 <= s < U + 2:
                        u, d = s - 2, units[s - 2]
                        pe.wait_ge(p_scaled, B + u + 1)
                        if u >= 2:
                            pe.wait_ge(pt_done, B + u - 1)
                        for x in range(d["klen"] // P):
                            m = pe.transpose(ps[3 + u % 2][:, x * P:x * P + P], Z[:, u % 4, x * P:x * P + P], ident[:, :])
                        m.then_inc(t_done, 1)
                    if s >= 3:
                        u, d = s - 3, units[s - 3]
                        g = group_of[u]
                        pe.wait_ge(pt_done, B + u + 1)
                        if g >= 2:
                            pe.wait_ge(o_taken, BG + g - 1)
                        o = ps[5 + g % 2][d["po"]:d["po"] + d["m"], d["oc"]:d["oc"] + P]
                        nk = d["klen"] // P
                        for x in range(nk):
                            m = pe.matmul(o, d["v"][x], PT[:, u % 2, x * P:x * P + P], start=x == 0, stop=x == nk - 1)
                        m.then_inc(pv_done, 1)

            def dve_part(dve):
                for s in range(U + 5):
                    if s < U:
                        u, d = s, units[s]
                        dve.wait_ge(scored, B + u + 1)
                        if "mask_ready" in d:
                            dve.wait_ge(*d["mask_ready"])
                        if u >= 4:
                            dve.wait_ge(t_done, B + u - 3)
                        nc.vector.tensor_tensor_reduce(Z[:, u % 4, 0:d["klen"]], ps[u % 3][:, 0:d["klen"]], d["mask"],
                                                       1.0, NEG, ALU.add, ALU.max, cols[:, MX, u:u + 1]).then_inc(z_done, 1)
                        dve.wait_ge(z_done, B + u + 1)
                        if sinks:
                            nc.vector.tensor_scalar(cols[:, NM, u:u + 1], cols[:, MX, u:u + 1], d["sink"], -1.0,
                                                    ALU.max, ALU.mult).then_inc(nm_done, 1)
                        else:
                            nc.vector.tensor_scalar(cols[:, NM, u:u + 1], cols[:, MX, u:u + 1], -1.0, None,
                                                    ALU.mult).then_inc(nm_done, 1)
                    if 1 <= s < U + 1:
                        u, d = s - 1, units[s - 1]
                        dve.wait_ge(p_done, B + u + 1)
                        den = cols[:, RS, u:u + 1]
                        if sinks:
                            dve.wait_ge(e_sink, u + 1)
                            nc.vector.tensor_tensor(den, den, cols[:, ES, u:u + 1], ALU.add).then_inc(den_done, 1)
                            dve.wait_ge(den_done, u + 1)
                        nc.vector.reciprocal(cols[:, RI, u:u + 1], den).then_inc(ri_done, 1)
                        dve.wait_ge(ri_done, B + u + 1)
                        nc.vector.tensor_scalar(Z[:, u % 4, 0:d["klen"]], Z[:, u % 4, 0:d["klen"]], cols[:, RI, u:u + 1],
                                                None, ALU.mult).then_inc(p_scaled, 1)
                    if s - 4 in last_of:
                        g = last_of[s - 4]
                        dve.wait_ge(pv_done, B + s - 3)
                        nc.vector.tensor_copy(groups[g][1], groups[g][2](ps[5 + g % 2])).then_inc(o_taken, 1)

            def act_part(act):
                for s in range(U + 2):
                    if act_first is not None:
                        act_first(act, s)
                    if s < U:
                        u, d = s, units[s]
                        act.wait_ge(nm_done, B + u + 1)
                        z = Z[:, u % 4, 0:d["klen"]]
                        nc.scalar.activation(z, z, ACT.Exp, bias=cols[:, NM, u:u + 1],
                                             accum_out=cols[:, RS, u:u + 1]).then_inc(p_done, 1)
                        if sinks:
                            nc.scalar.activation(cols[:, ES, u:u + 1], d["sink"], ACT.Exp,
                                                 bias=cols[:, NM, u:u + 1]).then_inc(e_sink, 1)
                    if s >= 2:
                        u, d = s - 2, units[s - 2]
                        act.wait_ge(t_done, B + u + 1)
                        if u >= 2:
                            act.wait_ge(pv_done, B + u - 1)
                        nc.scalar.activation(PT[:, u % 2, 0:d["klen"]], ps[3 + u % 2][:, 0:d["klen"]],
                                             ACT.Copy).then_inc(pt_done, 1)
            return pe_part, dve_part, act_part

        with ExitStack() as c:
            qkv = sb("qkv", [P, 24, SEQ], ctx=c)
            va = sb("va", [P, TB, 4 * P], ctx=c)
            vb = sb("vb", [P, TB, 4 * P], ctx=c)
            bias = sb("bias", [P, H8, SEQ], ctx=c)
            scratch = nc.dram_tensor("bias_rows", (H8, P, BAND_W), F32, kind="Internal").ap()
            b_in, b_rev, b_out, b_back = (sem(f"bias_{x}") for x in ("in", "reversed", "out", "back"))
            ev_mix = n["ev"]
            turn_a = token_turn(lambda b: qkv[:, 8 + b, :], 4, va, lambda b: (evac, ev_mix + 8 + b + 1))
            turn_b = token_turn(lambda b: qkv[:, 20 + b, :], 4, vb, lambda b: (evac, ev_mix + 16 + b + 1), 6)
            with ExitStack() as c2:
                rb = sb("rb", [H8, 2 * REL + 1], ctx=c2)
                ext = sb("ext", [H8, BAND_W], ctx=c2)
                far = BAND_W - 2 * REL

                def sp_beside(sp, k):
                    if k == 0:
                        sp.dma_start(rb[:, :], I["rel_bias"][0]).then_inc(b_in, 16)
                    if k != 3:
                        return
                    sp.wait_ge(b_rev, 2)
                    sp.dma_start(scratch, ext[:, :].rearrange("h (o n) -> h o n", o=1).broadcast_to([H8, P, BAND_W])).then_inc(b_out, 16)
                    sp.wait_ge(b_out, 16)
                    for hd in range(H8):
                        src = bass.AP(scratch.tensor, hd * P * BAND_W + P - 1, [[BAND_W - 1, P], [1, SEQ]])
                        sp.dma_start(bias[:, hd, :], src).then_inc(b_back, 16)

                def pool_tail(pool):
                    pool.wait_ge(b_in, 16)
                    nc.gpsimd.tensor_copy(ext[:, far:BAND_W], rb[:, 2 * REL - 1::-1]).then_inc(b_rev, 1)
                    nc.gpsimd.tensor_copy(ext[:, 0:far], rb[:, 2 * REL:2 * REL + 1].broadcast_to([H8, far])).then_inc(b_rev, 1)
                    pool.wait_ge(b_back, 16 * H8)
                    nc.gpsimd.memset(bias[0:HD, :, SEQ - HD:SEQ], NEG)

                def mix_evac(dve, i, j, ev0):
                    k = mix_block(i, j)
                    nc.vector.tensor_tensor(qkv[:, bass.ds(k, 1), :], ps[j][:, :].rearrange("p (o q) -> p o q", o=1),
                                            rstd[:, :].rearrange("p (o q) -> p o q", o=1), ALU.mult).then_inc(evac, 1)

                def pe_beside(pe, k):
                    if k >= 16:
                        (turn_a if k < 20 else turn_b)[0](pe, k % 4, k % 4 + 1)

                def dve_beside(dve, k):
                    if k >= 16:
                        (turn_a if k < 20 else turn_b)[1](dve, k % 4, k % 4 + 1)
                    if k in (17, 18):
                        g = k - 17
                        dve.wait_ge(evac, ev_mix + 12 * g + 4)
                        q = qkv[:, 12 * g:12 * g + 4, :]
                        nc.vector.tensor_scalar(q, q, HD ** -0.5, None, ALU.mult)

                in_proj("mix_in", gains("g_mix_pre"), qkv, update=half[:, 0, :], evac_dve=mix_evac, loop_end=4,
                        tails=dict(pool=pool_tail), beside=dict(sp=sp_beside, pe=pe_beside, dve=dve_beside))
            with ExitStack() as c2:
                off = {3: 0, 2: P, 1: 3 * P, 0: 6 * P}
                wide = 10 * P
                SP_ = sb("softplus", [P, 2, wide], ctx=c2)
                A = sb("weights", [P, 2, wide], ctx=c2)
                tmp = qkv[:, 8:11, :]
                ntri, nones = sq[:, 0, 0:P], sq[:, 1, 0:P]
                (sbc, z_mm, abs_d, exp_d, ln_d, sp_raw, sp_d, c_mm, a_raw, a_d, av_mm, o_d) = (sem(f"sb_{x}") for x in (
                    "const", "z", "abs", "exp", "ln", "spraw", "sp", "c", "araw", "a", "av", "o"))
                units = [(hd, kb) for hd in range(H8) for kb in (3, 2, 1, 0)]
                U = len(units)
                ZB = 6

                with nc.Block() as block:
                    @block.gpsimd
                    def _(pool):
                        nc.gpsimd.memset(nones[:, :], -1.0).then_inc(sbc, 1)
                        pool.wait_ge(sbc, 1)
                        nc.gpsimd.affine_select(out=ntri[:, :], in_=nones[:, :], compare_op=ALU.is_ge, fill=0.0,
                                                base=0, pattern=[[-1, P]], channel_multiplier=1).then_inc(sbc, 1)
                        for s in range(U + 2):
                            if s < U:
                                hd, kb = units[s]
                                v = SP_[:, hd % 2, off[kb]:off[kb] + P]
                                pool.wait_ge(sp_raw, s + 1)
                                nc.gpsimd.affine_select(out=v, in_=v, compare_op=ALU.is_gt, fill=0.0, base=0,
                                                        pattern=[[1, P]], channel_multiplier=-1).then_inc(sp_d, 1)
                            if s >= 2:
                                hd, kb = units[s - 2]
                                v = A[:, hd % 2, off[kb]:off[kb] + P]
                                pool.wait_ge(a_raw, s - 1)
                                nc.gpsimd.affine_select(out=v, in_=v, compare_op=ALU.is_gt, fill=0.0, base=0,
                                                        pattern=[[1, P]], channel_multiplier=-1).then_inc(a_d, 1)

                    @block.tensor
                    def _(pe):
                        pe.wait_ge(sbc, 2)
                        for s in range(U + 4):
                            if s < U:
                                hd, kb = units[s]
                                po = HD * (hd % 2)
                                if s >= ZB:
                                    pe.wait_ge(a_raw, s - ZB + 1)
                                pe.matmul(ps[s % ZB][:, 0:SEQ - kb * P],
                                          qkv[po:po + HD, 4 + hd // 2, kb * P:kb * P + P],
                                          qkv[po:po + HD, hd // 2, kb * P:SEQ], start=True, stop=True).then_inc(z_mm, 1)
                            if 2 <= s < U + 2:
                                u = s - 2
                                hd, kb = units[u]
                                pe.wait_ge(sp_d, u + 1)
                                for k2 in range(kb, TB):
                                    m = pe.matmul(ps[u % ZB][:, (k2 - kb) * P:SEQ - kb * P], (ntri if k2 == kb else nones)[:, :],
                                                  SP_[:, hd % 2, off[k2]:off[k2] + SEQ - k2 * P],
                                                  start=False, stop=True, skip_group_check=True)
                                m.then_inc(c_mm, 1)
                            if s >= 4:
                                u = s - 4
                                hd, kb = units[u]
                                po, pair = HD * (hd % 2), hd // 2
                                pe.wait_ge(a_d, u + 1)
                                if kb == 3 and pair >= 2:
                                    pe.wait_ge(o_d, pair - 1)
                                pe.matmul(ps[6 + pair % 2][po:po + HD, kb * P:SEQ], va[:, kb, hd * HD:hd * HD + HD],
                                          A[:, hd % 2, off[kb]:off[kb] + SEQ - kb * P],
                                          start=kb == 3, stop=kb == 0, skip_group_check=True).then_inc(av_mm, 1)

                    @block.vector
                    def _(dve):
                        for s in range(U + 7):
                            if 1 <= s < U + 1:
                                u = s - 1
                                hd, kb = units[u]
                                w = SEQ - kb * P
                                dve.wait_ge(ln_d, u + 1)
                                if hd >= 2:
                                    dve.wait_ge(c_mm, 4 * (hd - 1))
                                nc.vector.scalar_tensor_tensor(out=SP_[:, hd % 2, off[kb]:off[kb] + w], in0=ps[u % ZB][:, 0:w],
                                                               scalar=0.0, in1=tmp[:, u % 3, 0:w], op0=ALU.max,
                                                               op1=ALU.add).then_inc(sp_raw, 1)
                            if s >= 7 and (s - 7) % 8 == 7:
                                pair = (s - 7) // 8
                                dve.wait_ge(av_mm, 8 * pair + 8)
                                nc.vector.tensor_copy(F[:, pair, :], ps[6 + pair % 2][:, :]).then_inc(o_d, 1)

                    @block.scalar
                    def _(act):
                        act.preload_act_table_set("natural_log_exp_and_others")
                        for s in range(U + 3):
                            if s < U:
                                hd, kb = units[s]
                                w = SEQ - kb * P
                                t = tmp[:, s % 3, 0:w]
                                act.wait_ge(z_mm, s + 1)
                                if s >= 3:
                                    act.wait_ge(sp_raw, s - 2)
                                nc.scalar.activation(t, ps[s % ZB][:, 0:w], ACT.Abs).then_inc(abs_d, 1)
                                act.wait_ge(abs_d, s + 1)
                                nc.scalar.activation(t, t, ACT.Exp, scale=-1.0).then_inc(exp_d, 1)
                                act.wait_ge(exp_d, s + 1)
                                nc.scalar.activation(t, t, ACT.Ln, bias=1.0).then_inc(ln_d, 1)
                            if s >= 3:
                                u = s - 3
                                hd, kb = units[u]
                                w = SEQ - kb * P
                                act.wait_ge(c_mm, u + 1)
                                if hd >= 2:
                                    act.wait_ge(av_mm, 4 * (hd - 1))
                                nc.scalar.activation(A[:, hd % 2, off[kb]:off[kb] + w], ps[u % ZB][:, 0:w],
                                                     ACT.Exp).then_inc(a_raw, 1)

            (n_sq, n_sum, n_mm, n_ms, n_inv, n_rt, n_sp, n_rs, n_f) = (sem(f"mixnorm_{x}") for x in (
                "sq", "sum", "mm", "ms", "inv", "root", "spread", "rstd", "f"))
            osq = sb("out_squares", [P, 4, SEQ], ctx=c)
            osum = sb("out_square_sums", [P, 2, SEQ], ctx=c)

            with ExitStack() as c2:
                units = []
                for qb in range(TB):
                    for hd in range(H8):
                        po, klen = HD * (hd % 2), (qb + 1) * P
                        units.append(dict(
                            q=qkv[po:po + HD, 12 + hd // 2, qb * P:qb * P + P], k=qkv[po:po + HD, 16 + hd // 2, 0:klen],
                            klen=klen, mask=bias[:, hd, SEQ - klen:SEQ], po=po, m=HD, oc=(hd // 2) * P,
                            v=[vb[:, x, hd * HD:hd * HD + HD] for x in range(qb + 1)]))
                groups = [(8 * qb + 7, F[:, 4:8, qb * P:qb * P + P],
                           lambda b: b[:, :].rearrange("p (a q) -> p a q", a=4)) for qb in range(TB)]
                pe_p, dve_p, act_p = softmax_attention("ch", units, groups, qkv[:, 6:12, :], c2)
                g_ch = n["groups"] - TB
                with nc.Block() as block:
                    @block.gpsimd
                    def _(pool):
                        for b in range(4):
                            nc.gpsimd.tensor_tensor(osq[:, b, :], F[:, b, :], F[:, b, :], ALU.mult).then_inc(n_sq, 1)
                        for b in range(1, 4):
                            pool.wait_ge(n_sq, 4)
                            if b > 1:
                                pool.wait_ge(n_sum, b - 1)
                            nc.gpsimd.tensor_tensor(osum[:, 0, :], osum[:, 0, :] if b > 1 else osq[:, 0, :], osq[:, b, :],
                                                    ALU.add).then_inc(n_sum, 1)
                        pool.wait_ge(n_sum, 3)
                        for qb in range(TB):
                            q = slice(qb * P, qb * P + P)
                            pool.wait_ge(o_taken, g_ch + qb + 1)
                            nc.gpsimd.tensor_tensor(osq[:, :, q], F[:, 4:8, q], F[:, 4:8, q], ALU.mult).then_inc(n_sq, 1)
                            pool.wait_ge(n_sq, 4 + qb + 1)
                            for b in range(1, 4):
                                if b > 1:
                                    pool.wait_ge(n_sum, 3 + 3 * qb + b - 1)
                                nc.gpsimd.tensor_tensor(osum[:, 1, q], osum[:, 1, q] if b > 1 else osq[:, 0, q], osq[:, b, q],
                                                        ALU.add).then_inc(n_sum, 1)

                    @block.tensor
                    def _(pe):
                        pe_p(pe)

                    @block.vector
                    def _(dve):
                        dve_p(dve)

                    @block.scalar
                    def _(act):
                        act_p(act)

            rs2, rc2 = bias[:, 0:2, :], bias[:, 2, 0:2 * TB]
            x0 = n["x"]
            n["x"] += DB

            def x_pe(pe, b):
                if b:
                    return
                pe.wait_ge(n_sum, 3 + 3 * TB)
                for g in range(2):
                    for t in range(TB):
                        m = pe.matmul(ps[6][:, g * TB + t:g * TB + t + 1], osum[:, g, t * P:t * P + P], ones[:, 0:1],
                                      start=True, stop=True)
                m.then_inc(n_mm, 1)
                pe.wait_ge(n_rt, 1)
                for g in range(2):
                    for t in range(TB):
                        m = pe.matmul(ps[4 + g][:, t * P:t * P + P], rc2[:, g * TB + t:g * TB + t + 1].broadcast_to([P, P]),
                                      ident[:, :], start=True, stop=True)
                    m.then_inc(n_sp, 1)

            def x_dve(dve):
                dve.wait_ge(n_mm, 1)
                nc.vector.tensor_scalar(rc2, ps[6][:, 0:2 * TB], 1.0 / (4 * P), EPS, ALU.mult, ALU.add).then_inc(n_ms, 1)
                dve.wait_ge(n_ms, 1)
                nc.vector.reciprocal(rc2, rc2).then_inc(n_inv, 1)
                for b in range(DB + 1):
                    if b < DB:
                        if b % 4 == 0:
                            dve.wait_ge(n_sp, b // 4 + 1)
                            nc.vector.tensor_copy(rs2[:, b // 4, :], ps[4 + b // 4][:, :]).then_inc(n_rs, 1)
                            dve.wait_ge(n_rs, b // 4 + 1)
                        nc.vector.tensor_tensor(F[:, b, :], F[:, b, :], rs2[:, b // 4, :], ALU.mult).then_inc(n_f, 1)
                    if b >= 1:
                        q = b - 1
                        dve.wait_ge(xs_hi, x0 + q + 1)
                        nc.vector.scalar_tensor_tensor(out=xl[:, q, :], in0=F[:, q, :], scalar=vA[:, col["g_out_sb"] + q:col["g_out_sb"] + q + 1],
                                                       in1=xh[:, q, :].bitcast(F32), op0=ALU.mult, op1=ALU.subtract).then_inc(xs_lo, 1)

            def x_act(act):
                act.wait_ge(n_inv, 1)
                nc.scalar.activation(rc2, rc2, ACT.Sqrt).then_inc(n_rt, 1)
                for b in range(DB):
                    act.wait_ge(n_f, b + 1)
                    nc.scalar.activation(xh[:, b, :], F[:, b, :], ACT.Copy,
                                         scale=vA[:, col["g_out_sb"] + b:col["g_out_sb"] + b + 1]).then_inc(xs_hi, 1)

            post_out("mix_out", xh, xl, x=(x_act, x_dve, x_pe))

        with ExitStack() as c:
            a_hi = sb("a_hi2", [P, FB, SEQ], F32R, ctx=c)
            a_lo = sb("a_lo2", [P, FB, SEQ], F32R, ctx=c)
            ffn_up("ffn2_up", gains("g_ffn2_pre"), gains("g_mix_post"), a_hi, a_lo, c)
            post_out("ffn2_down", a_hi, a_lo, DOWN)
        with ExitStack() as c:
            name = "ple"
            pt = sb("p_tokens", [P, TB, PLE], ctx=c)
            phi = sb("p_hi", [P, 2, SEQ], F32R, ctx=c)
            plo = sb("p_lo", [P, 2, SEQ], F32R, ctx=c)
            sg = sb("sigmoid", [P, 2, SEQ], ctx=c)
            p_in, p_t, p_hi, p_lo, sg_d = (sem(f"ple_{x}") for x in ("in", "turned", "hi", "lo", "sigmoid"))
            pro = Prologue(None, half[:, 1, :], squares=False)
            ev0, sq0, acc0, st, t0 = n["ev"], n["sq"], n["acc"], n["stat"], first[name]
            n["ev"] += 2 * DB
            n["sq"] += DB
            n["acc"] += DB - 1
            n["stat"] += 1
            with nc.Block() as block:
                @block.sync
                def _(sp):
                    sp.dma_start(pt[:, :, :], I["p"][0, 0].rearrange("(t p) d -> p t d", p=P)).then_inc(p_in, 16)
                    load_steps(sp, name)

                @block.gpsimd
                def _(pool):
                    sum_squares(pool, sq0, acc0)

                @block.scalar
                def _(act):
                    def split_p(act):
                        for b in range(2):
                            act.wait_ge(p_t, b + 1)
                            nc.scalar.activation(phi[:, b, :], ps[5 + b][:, :], ACT.Copy).then_inc(p_hi, 1)
                    pro.act(act, {2: split_p})

                    def body(i, j):
                        split_hi(act, name, i, j)
                        o = i * 2 + j // 2
                        act.wait_ge(tile_done, i * 4 + (t0 + j + 1))
                        if j % 2 == 0:
                            wait(act, evac, ev0 + 2 * (o - 1) if not (isinstance(o, int) and o < 2) else 0)
                            nc.scalar.activation(sg[:, j // 2, :], ps[j][:, :], ACT.Sigmoid).then_inc(sg_d, 1)
                        else:
                            act.wait_ge(evac, i * 4 + (ev0 + j + 1))
                            wait(act, acc_done, acc0 + o - 1 if not (isinstance(o, int) and o < 2) else 0)
                            nc.scalar.activation(sq[:, j // 2, :].rearrange("p (o q) -> p o q", o=1), F[:, bass.ds(o, 1), :],
                                                 ACT.Square).then_inc(sq_done, 1)
                    steps(act, name, body)
                    root_act(act, st)

                @block.vector
                def _(dve):
                    def split_p(dve):
                        for b in range(2):
                            dve.wait_ge(p_hi, b + 1)
                            nc.vector.tensor_tensor(plo[:, b, :], ps[5 + b][:, :], phi[:, b, :].bitcast(F32), ALU.subtract).then_inc(p_lo, 1)
                    pro.dve(dve, {2: split_p})

                    def body(i, j):
                        split_lo(dve, name, i, j)
                        if j % 2 == 1:
                            o = i * 2 + j // 2
                            dve.wait_ge(tile_done, i * 4 + (t0 + j + 1))
                            dve.wait_ge(sg_d, o + 1)
                            nc.vector.tensor_tensor(F[:, bass.ds(o, 1), :], ps[j][:, :].rearrange("p (o q) -> p o q", o=1),
                                                    sg[:, j // 2, :].rearrange("p (o q) -> p o q", o=1), ALU.mult).then_inc(evac, 2)
                    steps(dve, name, body)
                    inverse_dve(dve, st, D)
                    rstd_dve(dve, st)

                @block.tensor
                def _(pe):
                    pe.wait_ge(p_in, 16)
                    for b in range(2):
                        for t in range(TB):
                            m = pe.transpose(ps[5 + b][:, t * P:t * P + P], pt[:, t, b * P:b * P + P], ident[:, :])
                        m.then_inc(p_t, 1)

                    def body(i, j):
                        r, s, kb, t, got = tile_at(name, i, j, 0)
                        if isinstance(i, int) and i == 0 and j < HEAD:
                            if j:
                                return
                            pe.wait_ge(lo_done, t + HEAD)
                            for b in range(DB):
                                if b == 1:
                                    pe.wait_ge(p_lo, 2)
                                    for q in range(PLE // P):
                                        mm3(pe, ps[1][:, :], (t + 1) % SPLIT, q, phi[:, q, :], plo[:, q, :], q == 0, q == 1)
                                head_mm(pe, (0, 2), t, b, pro.x0, xh, xl)
                            return
                        pe.wait_ge(lo_done, t + 1)
                        wait(pe, evac, i * 4 + (ev0 + j - 3))
                        a, b_ = (xh, xl) if j % 2 == 0 else (phi, plo)
                        for b in range(kb):
                            last = mm3(pe, ps[j][:, :], s, b, a[:, b, :], b_[:, b, :], b == 0, b == kb - 1)
                        last.then_inc(tile_done, 1)
                    steps(pe, name, body)
                    sums_pe(pe, acc0 + DB - 1, sq0 + DB)
                    spread_pe(pe, st)

        with ExitStack() as c:
            name = "conv_in"
            K = 3
            cv = sb("cv", [P, 2, SEQ + K - 1], ctx=c)
            y = sb("conv_y", [P, 2, SEQ], ctx=c)
            zs = sb("conv_z", [P, 2, SEQ], ctx=c)
            br = sb("conv_b", [P, 2, SEQ], ctx=c)
            yall = sb("conv_yall", [P, DB, SEQ], ctx=c)
            cz, cr, yd, zd, bd = (sem(f"conv_{x}") for x in ("zeros", "c", "y", "z", "b"))
            pro = Prologue(gains("norm_w_2"), gains("g_ple_post"))
            ev0, st, t0 = n["ev"], n["stat"], first[name]
            n["ev"] += 4 * DB
            n["stat"] += 1
            wcol = col["conv_w_conv_2"]
            with nc.Block() as block:
                @block.sync
                def _(sp):
                    load_steps(sp, name)

                @block.gpsimd
                def _(pool):
                    for s in range(2):
                        nc.gpsimd.memset(cv[:, s, 0:K - 1], 0.0).then_inc(cz, 1)
                    pro.pool(pool)

                @block.scalar
                def _(act):
                    pro.act(act)

                    def body(i, j):
                        split_hi(act, name, i, j)
                        if isinstance(i, int) and i == 0 and j == 0:
                            root_act(act, st)
                        if j == 3:
                            act.wait_ge(zd, i + 1)
                            nc.scalar.activation(zs[:, 0, :], zs[:, 0, :], ACT.Silu).then_inc(bd, 1)
                    steps(act, name, body)

                @block.vector
                def _(dve):
                    pro.dve(dve)
                    dve.wait_ge(cz, 2)

                    def body(i, j):
                        split_lo(dve, name, i, j)
                        if isinstance(i, int) and i == 0 and j == 0:
                            inverse_dve(dve, st, D)
                            rstd_dve(dve, st)
                            dve.wait_ge(rstd_done, st + 1)
                        dve.wait_ge(tile_done, i * 4 + (t0 + j + 1))
                        if j == 0:
                            nc.vector.tensor_tensor(br[:, 0, :], ps[j][:, :], rstd[:, :], ALU.mult).then_inc(evac, 1)
                        elif j == 1:
                            nc.vector.tensor_tensor(br[:, 1, :], ps[j][:, :], rstd[:, :], ALU.mult).then_inc(evac, 1)
                            dve.wait_ge(evac, i * 4 + (ev0 + 2))
                            nc.vector.tensor_tensor(br[:, 1, :], br[:, 1, :], rstd[:, :], ALU.mult).then_inc(cr, 1)
                        elif j == 2:
                            dve.wait_ge(cr, i + 1)
                            nc.vector.tensor_tensor(cv[:, 0, K - 1:SEQ + K - 1], ps[j][:, :], br[:, 1, :], ALU.mult).then_inc(evac, 1)
                            dve.wait_ge(evac, i * 4 + (ev0 + 3))
                            nc.vector.tensor_scalar(y[:, 0, :], cv[:, 0, 0:SEQ], vA[:, bass.ds(i + wcol, 1)], None, ALU.mult).then_inc(yd, 1)
                            dve.wait_ge(yd, i * 4 + 1)
                            nc.vector.scalar_tensor_tensor(out=y[:, 1, :], in0=cv[:, 0, 1:SEQ + 1], scalar=vA[:, bass.ds(i + (wcol + DB), 1)],
                                                           in1=y[:, 0, :], op0=ALU.mult, op1=ALU.add).then_inc(yd, 1)
                            dve.wait_ge(yd, i * 4 + 2)
                            nc.vector.scalar_tensor_tensor(out=y[:, 0, :], in0=cv[:, 0, 2:SEQ + 2], scalar=vA[:, bass.ds(i + (wcol + 2 * DB), 1)],
                                                           in1=y[:, 1, :], op0=ALU.mult, op1=ALU.add).then_inc(yd, 1)
                            dve.wait_ge(yd, i * 4 + 3)
                            nc.vector.tensor_tensor(y[:, 1, :], y[:, 0, :], br[:, 0, :], ALU.mult).then_inc(yd, 1)
                        else:
                            nc.vector.tensor_tensor(zs[:, 0, :], ps[j][:, :], rstd[:, :], ALU.mult).then_inc(zd, 1)
                            dve.wait_ge(bd, i + 1)
                            dve.wait_ge(yd, i * 4 + 4)
                            nc.vector.tensor_tensor(yall[:, bass.ds(i, 1), :], y[:, 1, :].rearrange("p (o q) -> p o q", o=1),
                                                    zs[:, 0, :].rearrange("p (o q) -> p o q", o=1), ALU.mult).then_inc(evac, 1)
                    steps(dve, name, body)

                @block.tensor
                def _(pe):
                    pe_tiles(pe, name, xh, xl, ev0, x_ready=pro.x0, sums=pro.sums, at=st)

            sums = resid_out("conv_out", *split_x(lambda b: yall[:, b, :]))

        with ExitStack() as c:
            qkv = sb("fox_qkvz", [P, 4 * DB, SEQ], ctx=c)
            vt = sb("fox_v", [P, TB, D], ctx=c)
            fl = sb("fox_f", [H8, 4, SEQ], ctx=c)
            bf = sb("fox_bf", [H8, 1], ctx=c)
            nsel = sb("fox_nsel", [H8, H8, P], ctx=c)
            decay = sb("fox_decay", [P, 4, SEQ], ctx=c)
            f_in, fsel, fd, decay_mm, decay_in, bias_in = (sem(f"fox_{x}") for x in ("bf", "sel", "f", "rows", "decay", "bias"))
            ev0 = n["ev"]
            turn = token_turn(lambda b: qkv[:, 16 + b, :], 8, vt, lambda b: (evac, ev0 + 16 + b + 1))

            def sp_tail(sp):
                sp.dma_start(bf[:, :], I["fox_b_f_2"].rearrange("a h -> h a")).then_inc(f_in, 16)

            def pool_tail(pool):
                nc.gpsimd.memset(nsel[:, :, :], 0.0).then_inc(fsel, 1)
                nc.gpsimd.memset(fl[:, 3, :], 1.0).then_inc(fsel, 1)
                pool.wait_ge(fsel, 1)
                nc.gpsimd.affine_select(out=nsel[:, :, :], in_=nsel[:, :, :], compare_op=ALU.not_equal, fill=-1.0, base=0,
                                        pattern=[[-1, H8], [0, P]], channel_multiplier=1).then_inc(fsel, 1)

            def f_evac(dve, i, j, ev0_):
                if isinstance(i, int) and 4 * i + j == 28:
                    nc.vector.tensor_tensor(fl[:, 0, :], ps[0][0:H8, :], rstd[0:H8, :], ALU.mult).then_inc(evac, 1)
                else:
                    behind = 1 if isinstance(i, int) and 4 * i + j > 28 else 0
                    nc.vector.tensor_tensor(qkv[:, bass.ds(i * 4 + j - behind, 1), :], ps[j][:, :].rearrange("p (o q) -> p o q", o=1),
                                            rstd[:, :].rearrange("p (o q) -> p o q", o=1), ALU.mult).then_inc(evac, 1)

            def pe_beside(pe, k):
                if 28 <= k < 32:
                    turn[0](pe, 2 * (k - 28), 2 * (k - 28) + 2)
                if k >= 31:
                    pe.wait_ge(fd, 6)
                    for hd in (2 * (k - 31), 2 * (k - 31) + 1):
                        spread_decay(pe, hd)

            def dve_beside(dve, k):
                if 28 <= k < 32:
                    turn[1](dve, 2 * (k - 28), 2 * (k - 28) + 2)
                if k in (28, 31):
                    q = qkv[:, 4 * (k > 28):4 * (k > 28) + 4, :]
                    dve.wait_ge(evac, ev0 + 8)
                    nc.vector.tensor_scalar(q, q, P ** -0.5, None, ALU.mult)
                if k == 29:
                    dve.wait_ge(f_in, 16)
                    dve.wait_ge(evac, ev0 + 29)
                    nc.vector.tensor_scalar(fl[:, 0, :], fl[:, 0, :], bf[:, 0:1], None, ALU.add).then_inc(fd, 1)
                if k == 30:
                    dve.wait_ge(fsel, 3)
                    dve.wait_ge(fd, 4)
                    nc.vector.scalar_tensor_tensor(out=fl[:, 2, :], in0=fl[:, 0, :], scalar=0.0, in1=fl[:, 1, :],
                                                   op0=ALU.min, op1=ALU.subtract).then_inc(fd, 1)
                    dve.wait_ge(fd, 5)
                    nc.vector.tensor_tensor_scan(fl[:, 0, :], fl[:, 3, :], fl[:, 2, :], 0.0, ALU.mult, ALU.add).then_inc(fd, 1)

            def spread_decay(pe, hd):
                if hd >= 2:
                    pe.wait_ge(decay_in, hd - 1 if hd < 5 else hd)
                pe.matmul(ps[7 if hd > 3 else 6 + hd % 2][:, :], nsel[:, hd, :], fl[:, 0, :], start=True, stop=True).then_inc(decay_mm, 1)

            def copy_decay(act, hd):
                act.wait_ge(decay_mm, hd + 1)
                nc.scalar.activation(decay[:, hd % 4, :], ps[7 if hd > 3 else 6 + hd % 2][:, :], ACT.Copy).then_inc(decay_in, 1)

            def silu_z(act, b0, b1):
                z = qkv[:, b0:b1, :]
                act.wait_ge(evac, ev0 + b1 + (b1 > 28))
                nc.scalar.activation(z, z, ACT.Silu)

            def act_beside(act, k):
                if k == 28:
                    silu_z(act, 24, 28)
                if k == 29:
                    act.wait_ge(fd, 1)
                    nc.scalar.activation(fl[:, 1, :], fl[:, 0, :], ACT.Abs).then_inc(fd, 1)
                    act.wait_ge(fd, 2)
                    nc.scalar.activation(fl[:, 1, :], fl[:, 1, :], ACT.Exp, scale=-1.0).then_inc(fd, 1)
                    act.wait_ge(fd, 3)
                    nc.scalar.activation(fl[:, 1, :], fl[:, 1, :], ACT.Ln, bias=1.0).then_inc(fd, 1)
                if k >= 31:
                    silu_z(act, 28 + 2 * (k - 31), 30 + 2 * (k - 31))
                    for hd in (2 * (k - 31), 2 * (k - 31) + 1):
                        copy_decay(act, hd)

            in_proj("fox_in", vA[:, col["norm_w_2"] + DB:col["norm_w_2"] + 2 * DB], None, sums=sums,
                    tails=dict(sp=sp_tail, pool=pool_tail), beside=dict(pe=pe_beside, dve=dve_beside, act=act_beside),
                    evac_dve=f_evac, loop_end=7)
            with ExitStack() as c2:
                order = [(half, qb, hd) for half in range(2) for qb in range(TB) for hd in range(4 * half, 4 * half + 4)]
                bias_slot = [qkv[:, 22 + x, :] for x in range(2)]
                units = []
                for u, (half, qb, hd) in enumerate(order):
                    klen = (qb + 1) * P
                    units.append(dict(
                        q=qkv[:, hd, qb * P:qb * P + P], k=qkv[:, 8 + hd, 0:klen], klen=klen,
                        mask=bias_slot[u % 2][:, 0:klen], mask_ready=(bias_in, u + 1), po=0, m=P,
                        oc=(hd % 4) * P, v=[vt[:, x, hd * P:hd * P + P] for x in range(qb + 1)]))

                second = {4 * TB + x - 2: 4 + x for x in range(4)}

                def spread_second(pe, s):
                    if s in second:
                        spread_decay(pe, second[s])

                def copy_second(act, s):
                    if s in second:
                        act.wait_ge(bias_in, s + 2)
                        copy_decay(act, second[s])
                groups = [(4 * g + 3, F[:, 4 * (g // TB):4 * (g // TB) + 4, (g % TB) * P:(g % TB) * P + P],
                           lambda b: b[:, :].rearrange("p (a q) -> p a q", a=4)) for g in range(2 * TB)]
                u_fox = n["units"]
                pe_p, dve_p, act_p = softmax_attention("fox", units, groups, qkv[:, 16:22, :], c2, spread_second, copy_second)
                with nc.Block() as block:
                    @block.gpsimd
                    def _(pool):
                        for u, (half, qb, hd) in enumerate(order):
                            w = (qb + 1) * P
                            pool.wait_ge(decay_in, hd + 1)
                            if u >= 2:
                                pool.wait_ge(z_done, u_fox + u - 1)
                            nc.gpsimd.affine_select(out=bias_slot[u % 2][:, 0:w], in_=decay[:, hd % 4, 0:w], compare_op=ALU.is_ge,
                                                    fill=NEG, base=qb * P, pattern=[[-1, w]], channel_multiplier=1).then_inc(bias_in, 1)

                    @block.tensor
                    def _(pe):
                        pe_p(pe)

                    @block.vector
                    def _(dve):
                        dve_p(dve)

                    @block.scalar
                    def _(act):
                        act_p(act)

            sums = resid_out("fox_out", *gate_x(lambda b: qkv[:, 24 + b, :]))

        with ExitStack() as c:
            G = sb("gdn_qkvz", [P, 4 * DB, SEQ], ctx=c)
            X = sb("gdn_slots", [P, 12, SEQ], ctx=c)
            BG = sb("gdn_bg", [2 * H8, SEQ], ctx=c)
            LV = 7
            TH = [P, TB, H8]
            cc = sb("gdn_cc", [P, TB, 2 * H8], ctx=c)
            tab = sb("gdn_tab", [P, 14, TB, H8], ctx=c)
            (BETA, AX, AE, GG, GC, GL, EGC, EGL, EKD, CKN, CKB, BEGC, CQN, TMP) = range(14)
            nrm = sb("gdn_norm", [P, TB, 16], ctx=c)
            al = sb("gdn_al", [P, 3, H8], ctx=c)
            lev = sb("gdn_levels", [P, LV, P], ctx=c)
            triu = sb("gdn_triu", [P, P], ctx=c)
            state = sb("gdn_state", [P, 2, P], ctx=c)
            vn = sb("gdn_vnew", [P, 2, P], ctx=c)
            (a_in, g_const, g_turned, g_ax, g_beta, g_soft, g_al, g_sum, g_dif, g_exp, g_sq, g_ss, g_nrm, g_root, dve_link) = (
                sem(f"gdn_{x}") for x in ("ain", "const", "turned", "ax", "beta", "soft", "al", "sum", "dif", "exp",
                                          "sq", "ss", "nrm", "root", "dvelink"))

            K = 4
            ev0 = n["ev"]
            with ExitStack() as c2:
                u = X[:, 0:4, :].rearrange("p a q -> p (a q)")
                W_U = SEQ + K - 1
                ub = [u[:, s * W_U:(s + 1) * W_U] for s in range(2)]
                c_zero, c_first, c_tap, c_silu = sem("gdn_zero"), sem("gdn_first"), sem("gdn_tap"), sem("gdn_silu")

                def one(ap):
                    return ap.rearrange("p (o q) -> p o q", o=1)

                def g_evac(dve, i, j, ev0_):
                    k = i * 4 + j
                    if isinstance(i, int) and k == 24:
                        nc.vector.tensor_tensor(BG[:, :], ps[0][0:2 * H8, :], rstd[0:2 * H8, :], ALU.mult).then_inc(evac, 1)
                        g_tap(dve, i, j, 3)
                        return
                    if isinstance(i, int) and i >= 6:
                        nc.vector.tensor_tensor(G[:, k - 1, :], ps[j][:, :], rstd[:, :], ALU.mult).then_inc(evac, 1)
                        return
                    if isinstance(i, int) and k == 0:
                        dve.wait_ge(c_zero, 2)
                    nc.vector.tensor_tensor(ub[j % 2][:, K - 1:K - 1 + SEQ], ps[j][:, :], rstd[:, :], ALU.mult).then_inc(evac, 1)
                    if not isinstance(i, int) or k:
                        g_tap(dve, i, j, 3)

                def g_tap(dve, i, j, tap):
                    if isinstance(i, int) and not 1 <= 4 * i + j <= 24:
                        return
                    if tap == 1:
                        dve.wait_ge(c_first, i * 4 + j)
                    else:
                        dve.wait_ge(c_tap, i * 12 + (3 * (j - 1) + tap - 1))
                    dst = G[:, bass.ds(i * 4 + (j - 1), 1), :]
                    nc.vector.scalar_tensor_tensor(out=dst, in0=one(ub[(j + 1) % 2][:, tap:tap + SEQ]),
                                                   scalar=vB[:, bass.ds(i * 4 + (j - 1 + 24 * tap), 1)],
                                                   in1=dst, op0=ALU.mult, op1=ALU.add).then_inc(c_tap, 1)

                def g_act(act, i, j, ev0_):
                    k = 4 * i + j
                    silu = not isinstance(i, int) or 2 <= k <= 25
                    if silu:
                        act.wait_ge(c_tap, i * 12 + 3 * (j - 1))
                    if not isinstance(i, int) or k < 24:
                        act.wait_ge(evac, i * 4 + (ev0_ + j + 1))
                        act.wait_ge(c_zero, 2)
                        nc.scalar.activation(G[:, bass.ds(i * 4 + j, 1), :], one(ub[j % 2][:, 0:SEQ]), ACT.Copy,
                                             scale=vB[:, bass.ds(i * 4 + j, 1)]).then_inc(c_first, 1)
                    if silu:
                        dst = G[:, bass.ds(i * 4 + (j - 2), 1), :]
                        nc.scalar.activation(dst, dst, ACT.Silu).then_inc(c_silu, 1)

                def sp_tail(sp):
                    for r, nm in enumerate(("gdn_a_log_2", "gdn_dt_bias_2")):
                        sp.dma_start(al[:, r, :], I[nm].broadcast_to([P, H8])).then_inc(a_in, 16)

                def pool_tail(pool):
                    for s in range(2):
                        nc.gpsimd.memset(ub[s][:, 0:K - 1], 0.0).then_inc(c_zero, 1)
                    nc.gpsimd.affine_select(out=triu[:, :], in_=ones[:, :], compare_op=ALU.is_ge, fill=0.0, base=0,
                                            pattern=[[1, P]], channel_multiplier=-1).then_inc(g_const, 1)
                    nc.gpsimd.memset(lev[:, :, :], 0.0).then_inc(g_const, 1)
                    pool.wait_ge(g_const, 2)
                    for l in range(LV):
                        b = 2 ** l
                        m = P // (2 * b)
                        v = lev[:, l, :].rearrange("p (m s r) -> p m s r", m=m, s=2)[:, :, 1, :]
                        src = ones[:, 0:m * b].rearrange("p (m r) -> p m r", m=m)
                        nc.gpsimd.affine_select(out=v, in_=src, compare_op=ALU.is_ge, fill=0.0, base=0,
                                                pattern=[[-2 * b, m], [0, b]], channel_multiplier=1).then_inc(g_const, 1)
                        pool.wait_ge(g_const, 3 + 2 * l)
                        nc.gpsimd.affine_select(out=v, in_=v, compare_op=ALU.is_ge, fill=0.0, base=b - 1,
                                                pattern=[[2 * b, m], [0, b]], channel_multiplier=-1).then_inc(g_const, 1)

                def pe_beside(pe, k):
                    if k == 25:
                        pe.wait_ge(evac, ev0 + 25)
                        for t in range(TB):
                            m = pe.transpose(ps[4][:, t * 16:t * 16 + 16], BG[:, t * P:t * P + P], ident[0:16, 0:16])
                        m.then_inc(g_turned, 1)
                    if k >= 25:
                        for b in (2 * (k - 25), 2 * (k - 25) + 1):
                            pe.wait_ge(g_sq, b + 1)
                            for t in range(TB):
                                m = pe.matmul(ps[5][:, t * 16 + b:t * 16 + b + 1], X[:, 4 + b % 4, t * P:t * P + P], ones[:, 0:1],
                                              start=True, stop=True)
                            m.then_inc(g_ss, 1)
                    if k == 29:
                        pe.wait_ge(g_al, 3)
                        pe.wait_ge(g_const, 1)
                        g = tab[:, GG, :, :].rearrange("p t h -> p (t h)")
                        pe.matmul(ps[6][:, 0:32], triu[:, :], g, start=True, stop=True)
                        pe.matmul(ps[6][:, 32:64], ones[:, :], g, start=True, stop=True).then_inc(g_sum, 1)

                def act_beside(act, k):
                    if 24 <= k < 32:
                        for b in (2 * (k - 24), 2 * (k - 24) + 1):
                            if b >= 4:
                                act.wait_ge(g_ss, b - 3)
                            act.wait_ge(c_silu, b + 1)
                            nc.scalar.activation(X[:, 4 + b % 4, :], G[:, b, :], ACT.Square).then_inc(g_sq, 1)
                    if k == 27:
                        act.wait_ge(g_ax, 2)
                        nc.scalar.activation(tab[:, BETA, :, :], cc[:, :, 0:H8], ACT.Sigmoid).then_inc(g_beta, 1)
                        nc.scalar.activation(tab[:, AE, :, :], tab[:, AX, :, :], ACT.Abs).then_inc(g_soft, 1)
                        act.wait_ge(g_soft, 1)
                        nc.scalar.activation(tab[:, AE, :, :], tab[:, AE, :, :], ACT.Exp, scale=-1.0).then_inc(g_soft, 1)
                        act.wait_ge(a_in, 32)
                        nc.scalar.activation(al[:, 2, :], al[:, 0, :], ACT.Exp).then_inc(g_al, 1)
                        act.wait_ge(g_soft, 2)
                        nc.scalar.activation(tab[:, AE, :, :], tab[:, AE, :, :], ACT.Ln, bias=1.0).then_inc(g_soft, 1)
                    if k == 30:
                        act.wait_ge(g_dif, 1)
                        nc.scalar.activation(tab[:, EGC:EGC + 3, :, :], tab[:, EGC:EGC + 3, :, :], ACT.Exp).then_inc(g_exp, 1)
                    if k == 32:
                        act.wait_ge(g_nrm, 1)
                        nc.scalar.activation(nrm[:, :, :], nrm[:, :, :], ACT.Sqrt).then_inc(g_root, 1)
                    if k in (29, 32):
                        z = G[:, 24:28, :] if k == 29 else G[:, 28:32, :]
                        act.wait_ge(evac, ev0 + (29 if k == 29 else 33))
                        nc.scalar.activation(z, z, ACT.Silu)

                def bc(ap):
                    return ap.rearrange("p (o h) -> p o h", o=1).broadcast_to(TH)

                steps_ = [0]

                def dve_beside(dve, k):
                    def link(ins):
                        steps_[0] += 1
                        ins.then_inc(dve_link, 1)
                        dve.wait_ge(dve_link, steps_[0])

                    if k == 26:
                        dve.wait_ge(g_turned, 1)
                        nc.vector.tensor_copy(cc[:, :, :], ps[4][:, 0:64].rearrange("p (t c) -> p t c", t=TB)).then_inc(g_ax, 1)
                        dve.wait_ge(a_in, 32)
                        dve.wait_ge(g_ax, 1)
                        nc.vector.tensor_tensor(tab[:, AX, :, :], cc[:, :, H8:2 * H8], bc(al[:, 1, :]), ALU.add).then_inc(g_ax, 1)
                    if k == 28:
                        dve.wait_ge(g_soft, 3)
                        link(nc.vector.scalar_tensor_tensor(out=tab[:, TMP, :, :], in0=tab[:, AX, :, :], scalar=0.0, in1=tab[:, AE, :, :],
                                                            op0=ALU.max, op1=ALU.add))
                        dve.wait_ge(g_al, 1)
                        nc.vector.tensor_scalar(al[:, 2, :], al[:, 2, :], -1.0, None, ALU.mult).then_inc(g_al, 1)
                        dve.wait_ge(g_al, 2)
                        nc.vector.tensor_tensor(tab[:, GG, :, :], tab[:, TMP, :, :], bc(al[:, 2, :]), ALU.mult).then_inc(g_al, 1)
                    if k == 29:
                        dve.wait_ge(g_sum, 1)
                        link(nc.vector.tensor_copy(tab[:, GC:GC + 2, :, :], ps[6][:, 0:64].rearrange("p (a t h) -> p a t h", a=2, t=TB)))
                        link(nc.vector.tensor_copy(tab[:, EGC:EGC + 2, :, :], tab[:, GC:GC + 2, :, :]))
                        nc.vector.tensor_tensor(tab[:, EKD, :, :], tab[:, GL, :, :], tab[:, GC, :, :], ALU.subtract).then_inc(g_dif, 1)
                    if k == 32:
                        dve.wait_ge(g_ss, 16)
                        nc.vector.tensor_scalar(nrm[:, :, :], ps[5][:, 0:64].rearrange("p (t c) -> p t c", t=TB), EPS, None,
                                                ALU.add).then_inc(g_nrm, 1)
                        dve.wait_ge(g_root, 1)
                        link(nc.vector.reciprocal(nrm[:, :, :], nrm[:, :, :]))
                        dve.wait_ge(g_exp, 1)
                        dve.wait_ge(g_beta, 1)
                        k_, q_ = nrm[:, :, 8:16], nrm[:, :, 0:8]
                        nc.vector.tensor_copy(tab[:, CKN, :, :], k_).then_inc(g_nrm, 1)
                        nc.vector.tensor_tensor(tab[:, CKB, :, :], k_, tab[:, BETA, :, :], ALU.mult).then_inc(g_nrm, 1)
                        nc.vector.tensor_tensor(tab[:, BEGC, :, :], tab[:, BETA, :, :], tab[:, EGC, :, :], ALU.mult).then_inc(g_nrm, 1)
                        nc.vector.tensor_scalar(tab[:, CQN, :, :], q_, P ** -0.5, None, ALU.mult).then_inc(g_nrm, 1)

                in_proj("gdn_in", vA[:, col["norm_w_2"] + 2 * DB:col["norm_w_2"] + 3 * DB], None, sums=sums,
                        tails=dict(sp=sp_tail, pool=pool_tail), beside=dict(pe=pe_beside, act=act_beside, dve=dve_beside),
                        evac_dve=g_evac, evac_act=g_act, between_dve=g_tap, loop_end=6)

            KN, KB, BT1, QE, KNT, KBT, QNT, KBE, KD, DD = range(10)
            LT, BT0, US, T_, TT, QKT = KN, KB, QE, KNT, KBT, QNT

            def slot(s, r):
                return F[:, s, :] if r == 0 and s < 8 else X[:, s - 8 if r == 0 else 2 + s, :]

            def blk(ap, t):
                return ap[:, t * P:t * P + P]

            def v4(ap):
                return ap.rearrange("p (t d) -> p t d", t=TB)

            def columns(ap, l, odd):
                return ap.rearrange("p (m s r) -> p m s r", s=2, r=2 ** l)[:, :, odd, :]

            def level(l):
                return lev[:, l, :].rearrange("p (o d) -> p o d", o=1).broadcast_to([P, TB, P])

            def colb(row, hd):
                return tab[:, row, :, hd:hd + 1].broadcast_to([P, TB, P])

            (t_in, rows_mm, tok_d, v_d, tok_p, qd_p, egc, t_back, back_a, back_d, kk_mm, dif, dec, qkt_d, qkt_m, lt_d,
             bt_0, bt_d, u_mm, us_d, p_mm, t_d, w_mm, w_d, v_mm, vn_d, o_mm, s_mm, s_d, o_tok) = (sem(f"gd_{x}") for x in (
                "tin", "rows", "tokd", "vd", "tokp", "qdp", "egc", "tback", "backa", "backd", "kk", "dif", "dec", "qkt", "qktm",
                "lt", "bt0", "bt", "u", "us", "p", "t", "w", "wd", "v", "vn", "o", "s", "sd", "otok"))
            NP_ = H8 // 2
            sso = sb("gdn_sso", [P, H8, TB], ctx=c)
            o_sq = sem("gdo_sq")

            def lvl(p, l, r):
                return (p * LV + l) * 2 + r + 1

            with nc.Block() as block:
                @block.tensor
                def _(pe):
                    for p in range(NP_):
                        for r in range(2):
                            m, b = 2 * p + r, 4 * r
                            if p:
                                pe.wait_ge(o_tok, m - 1)
                            for src, bank in ((8 + m, 3), (16 + m, 1)):
                                for t in range(TB):
                                    ins = pe.transpose(blk(ps[b + bank], t), blk(G[:, src, :], t), ident[:, :])
                                ins.then_inc(t_in, 1)
                            for row, bank in ((CQN, 0), (GC, 2)):
                                for t in range(TB):
                                    ins = pe.matmul(blk(ps[b + bank], t), tab[:, row, t, m:m + 1].broadcast_to([P, P]), ident[:, :],
                                                    start=True, stop=True)
                                ins.then_inc(rows_mm, 1)
                        for r in range(2):
                            m, b = 2 * p + r, 4 * r
                            for s, bank, at in ((KN, 0, 2), (KB, 3, 3)):
                                pe.wait_ge(tok_d, 3 * m + at)
                                for t in range(TB):
                                    ins = pe.transpose(blk(ps[b + bank], t), blk(slot(s, r), t), ident[:, :])
                                ins.then_inc(t_back, 1)
                        for r in range(2):
                            m, b = 2 * p + r, 4 * r
                            pe.wait_ge(back_a, m + 1)
                            pe.wait_ge(back_d, m + 1)
                            pe.wait_ge(v_d, m + 1)
                            for t in range(TB):
                                pe.matmul(blk(ps[b], t), blk(slot(KNT, r), t), blk(slot(KBT, r), t), start=True, stop=True)
                                ins = pe.matmul(blk(ps[b + 1], t), blk(slot(KNT, r), t), blk(slot(QNT, r), t),
                                                start=True, stop=True)
                            ins.then_inc(kk_mm, 1)
                        for l in range(LV):
                            for r in range(2):
                                m, b = 2 * p + r, 4 * r
                                if l == 0:
                                    pe.wait_ge(bt_0, m + 1)
                                else:
                                    pe.wait_ge(bt_d, (p * (LV - 1) + l - 1) * 2 + r + 1)
                                if l:
                                    pe.wait_ge(t_d, 2 * lvl(p, l - 1, r) - 1)
                                for t in range(TB):
                                    ins = pe.matmul(blk(ps[b], t), blk(slot(BT0 + l % 2, r), t),
                                                    ident[:, :] if l == 0 else blk(slot(T_, r), t), start=True, stop=True)
                                ins.then_inc(u_mm, 1)
                            if l == 0:
                                continue
                            for r in range(2):
                                m, b = 2 * p + r, 4 * r
                                pe.wait_ge(us_d, (p * (LV - 1) + l - 1) * 2 + r + 1)
                                pe.wait_ge(t_d, 2 * lvl(p, l - 1, r))
                                if l < LV - 1:
                                    for t in range(TB):
                                        ins = pe.matmul(ps[b + 1][:, t * HD:t * HD + HD], blk(slot(TT, r), t),
                                                        columns(blk(slot(US, r), t), l, 0), start=True, stop=True)
                                    ins.then_inc(p_mm, 1)
                                for t in range(TB):
                                    ins = pe.matmul(ps[b + 2][:, t * HD:t * HD + HD], blk(slot(US, r), t),
                                                    columns(blk(slot(TT, r), t), l, 1), start=True, stop=True)
                                ins.then_inc(p_mm, 1 if l < LV - 1 else 2)
                        for r in range(2):
                            m, b = 2 * p + r, 4 * r
                            pe.wait_ge(t_d, 2 * lvl(p, LV - 1, r))
                            pe.wait_ge(tok_p, 2 * m + 2)
                            for t in range(TB):
                                ins = pe.matmul(blk(ps[b + 3], t), blk(slot(KBE, r), t), blk(slot(TT, r), t), start=True, stop=True)
                            ins.then_inc(w_mm, 1)
                        for t in range(TB):
                            for r in range(2):
                                m, b = 2 * p + r, 4 * r
                                ins = pe.matmul(blk(ps[b], t), blk(slot(TT, r), t), blk(G[:, 16 + m, :], t), start=True, stop=t == 0)
                                if t:
                                    pe.wait_ge(w_d, m + 1)
                                    pe.wait_ge(s_d, (p * 3 + t - 1) * 2 + r + 1)
                                    ins = pe.matmul(blk(ps[b], t), blk(G[:, 8 + m, :], t), state[:, r, :], start=False, stop=True)
                                ins.then_inc(v_mm, 1)
                            for r in range(2):
                                m, b = 2 * p + r, 4 * r
                                pe.wait_ge(vn_d, (p * TB + t) * 2 + r + 1)
                                if t == 0:
                                    pe.wait_ge(qkt_m, m + 1)
                                ins = pe.matmul(blk(ps[b + 1], t), blk(slot(QKT, r), t), vn[:, r, :], start=True, stop=t == 0)
                                if t == 1:
                                    pe.wait_ge(qd_p, m + 1)
                                if t:
                                    ins = pe.matmul(blk(ps[b + 1], t), blk(G[:, m, :], t), state[:, r, :], start=False, stop=True)
                                ins.then_inc(o_mm, 1)
                                if t < TB - 1:
                                    pe.matmul(ps[b + 2][:, 0:P], blk(slot(KD, r), t), vn[:, r, :], start=True, stop=True).then_inc(s_mm, 1)

                @block.vector
                def _(dve):
                    for p in range(NP_):
                        for r in range(2):
                            m, b = 2 * p + r, 4 * r
                            dve.wait_ge(t_in, 2 * m + 1)
                            nc.vector.tensor_tensor(v4(slot(KN, r)), v4(ps[b + 3][:, :]), colb(CKN, m), ALU.mult).then_inc(tok_d, 1)
                            dve.wait_ge(rows_mm, 2 * m + 1)
                            nc.vector.tensor_tensor(slot(QNT, r), G[:, m, :], ps[b][:, :], ALU.mult).then_inc(tok_d, 1)
                            nc.vector.tensor_tensor(v4(slot(KB, r)), v4(ps[b + 3][:, :]), colb(CKB, m), ALU.mult).then_inc(tok_d, 1)
                        for r in range(2):
                            m, b = 2 * p + r, 4 * r
                            dve.wait_ge(rows_mm, 2 * m + 2)
                            for t in range(TB):
                                nc.vector.tensor_scalar(blk(slot(DD, r), t), blk(ps[b + 2], t), tab[:, GC, t, m:m + 1], 0.0,
                                                        ALU.subtract, ALU.min).then_inc(dif, 1)
                            dve.wait_ge(t_back, 2 * m + 2)
                            nc.vector.tensor_copy(slot(KBT, r), ps[b + 3][:, :]).then_inc(back_d, 1)
                            nc.vector.tensor_tensor(v4(G[:, 16 + m, :]), v4(ps[b + 1][:, :]), colb(BETA, m), ALU.mult).then_inc(v_d, 1)
                        for r in range(2):
                            m, b = 2 * p + r, 4 * r
                            dve.wait_ge(kk_mm, m + 1)
                            dve.wait_ge(dec, m + 1)
                            dve.wait_ge(tok_p, 2 * m + 2)
                            nc.vector.tensor_tensor(slot(LT, r), ps[b][:, :], slot(DD, r), ALU.mult).then_inc(lt_d, 1)
                            dve.wait_ge(lt_d, m + 1)
                            nc.vector.tensor_tensor(v4(slot(BT0, r)), v4(slot(LT, r)), level(0), ALU.mult).then_inc(bt_0, 1)
                        for r in range(2):
                            m, b = 2 * p + r, 4 * r
                            dve.wait_ge(qd_p, m + 1)
                            nc.vector.tensor_tensor(slot(QKT, r), ps[b + 1][:, :], slot(DD, r), ALU.mult).then_inc(qkt_d, 1)
                        idb = ident[:, :].rearrange("p (o d) -> p o d", o=1).broadcast_to([P, TB, P])
                        for l in range(LV):
                            for r in range(2):
                                m, b = 2 * p + r, 4 * r
                                if l == 0:
                                    dve.wait_ge(u_mm, lvl(p, l, r))
                                    nc.vector.tensor_tensor(v4(slot(T_, r)), idb, v4(ps[b][:, :]), ALU.subtract).then_inc(t_d, 1)
                                    nc.vector.tensor_tensor(v4(slot(TT, r)), idb, v4(slot(BT0, r)), ALU.subtract).then_inc(t_d, 1)
                                    continue
                                at = 2 * ((p * (LV - 1) + l - 1) * 2 + r)
                                if l < LV - 1:
                                    dve.wait_ge(p_mm, at + 1)
                                    T = columns(slot(T_, r), l, 0)
                                    nc.vector.tensor_tensor(T, T, ps[b + 1][:, 0:SEQ // 2].rearrange("p (m r) -> p m r", r=2 ** l),
                                                            ALU.subtract).then_inc(t_d, 1)
                                dve.wait_ge(p_mm, at + 2)
                                T = columns(slot(TT, r), l, 1)
                                nc.vector.tensor_tensor(T, T, ps[b + 2][:, 0:SEQ // 2].rearrange("p (m r) -> p m r", r=2 ** l),
                                                        ALU.subtract).then_inc(t_d, 1 if l < LV - 1 else 2)
                        for t in range(TB - 1):
                            for r in range(2):
                                m, b = 2 * p + r, 4 * r
                                dve.wait_ge(s_mm, (p * 3 + t) * 2 + r + 1)
                                dve.wait_ge(o_mm, (p * TB + t) * 2 + r + 1)
                                if t == 0:
                                    nc.vector.tensor_copy(state[:, r, :], ps[b + 2][:, 0:P]).then_inc(s_d, 1)
                                else:
                                    nc.vector.scalar_tensor_tensor(out=state[:, r, :], in0=state[:, r, :], scalar=tab[:, EGL, t, m:m + 1],
                                                                   in1=ps[b + 2][:, 0:P], op0=ALU.mult, op1=ALU.add).then_inc(s_d, 1)
                        for r in range(2):
                            m, b = 2 * p + r, 4 * r
                            dve.wait_ge(o_mm, (p * TB + TB - 1) * 2 + r + 1)
                            nc.vector.tensor_copy(G[:, m, :], ps[b + 1][:, :]).then_inc(o_tok, 1)

                @block.scalar
                def _(act):
                    for p in range(NP_):
                        for r in range(2):
                            m, b = 2 * p + r, 4 * r
                            act.wait_ge(dif, 4 * m + 4)
                            nc.scalar.activation(slot(DD, r), slot(DD, r), ACT.Exp).then_inc(dec, 1)
                            act.wait_ge(t_back, 2 * m + 1)
                            nc.scalar.activation(slot(KNT, r), ps[b][:, :], ACT.Copy).then_inc(back_a, 1)
                            nc.scalar.activation(slot(QE, r), ps[b + 2][:, :], ACT.Exp).then_inc(egc, 1)
                        for l in range(1, LV):
                            for r in range(2):
                                b = 4 * r
                                act.wait_ge(u_mm, lvl(p, l, r))
                                nc.scalar.activation(slot(US, r), ps[b][:, :], ACT.Copy).then_inc(us_d, 1)
                        for r in range(2):
                            m, b = 2 * p + r, 4 * r
                            act.wait_ge(w_mm, m + 1)
                            nc.scalar.activation(G[:, 8 + m, :], ps[b + 3][:, :], ACT.Copy, scale=-1.0).then_inc(w_d, 1)
                        for t in range(TB):
                            for r in range(2):
                                b = 4 * r
                                act.wait_ge(v_mm, (p * TB + t) * 2 + r + 1)
                                nc.scalar.activation(vn[:, r, :], blk(ps[b], t), ACT.Copy).then_inc(vn_d, 1)
                        for r in range(2):
                            m = 2 * p + r
                            act.wait_ge(o_tok, m + 1)
                            if p:
                                act.wait_ge(o_sq, (m - 2) * TB + TB)
                            for t in range(TB):
                                nc.scalar.activation(blk(sq[:, r, :], t), blk(G[:, m, :], t), ACT.Square,
                                                     accum_out=sso[:, m, t:t + 1]).then_inc(o_sq, 1)

                @block.gpsimd
                def _(pool):
                    for p in range(NP_):
                        for r in range(2):
                            m = 2 * p + r
                            pool.wait_ge(tok_d, 3 * m + 1)
                            for dst, cf in ((KBE, BEGC), (KD, EKD)):
                                nc.gpsimd.tensor_tensor(v4(slot(dst, r)), v4(slot(KN, r)), colb(cf, m), ALU.mult).then_inc(tok_p, 1)
                        for r in range(2):
                            m = 2 * p + r
                            pool.wait_ge(egc, m + 1)
                            pool.wait_ge(tok_d, 3 * m + 2)
                            nc.gpsimd.tensor_tensor(G[:, m, :], slot(QNT, r), slot(QE, r), ALU.mult).then_inc(qd_p, 1)
                        for l in range(1, LV):
                            for r in range(2):
                                m = 2 * p + r
                                if l == 1:
                                    pool.wait_ge(lt_d, m + 1)
                                if l >= 2:
                                    pool.wait_ge(u_mm, lvl(p, l - 2, r))
                                    if l == 2:
                                        pool.wait_ge(t_d, 2 * lvl(p, 0, r))
                                nc.gpsimd.tensor_tensor(v4(slot(BT0 + l % 2, r)), v4(slot(LT, r)), level(l), ALU.mult).then_inc(bt_d, 1)
                            if l == 1:
                                for r in range(2):
                                    m = 2 * p + r
                                    pool.wait_ge(qkt_d, m + 1)
                                    q = v4(slot(QKT, r))
                                    nc.gpsimd.affine_select(out=q, in_=q, compare_op=ALU.is_ge, fill=0.0, base=0,
                                                            pattern=[[0, TB], [1, P]], channel_multiplier=-1).then_inc(qkt_m, 1)

            (o_ms, o_rt, o_in, o_n, o_t, o_y) = (sem(f"gdo_{x}") for x in ("ms", "rt", "inv", "n", "t", "y"))
            x0 = n["x"]
            n["x"] += DB
            OB = 4

            def x_act(act):
                act.wait_ge(o_ms, 1)
                nc.scalar.activation(sso[:, :, :], sso[:, :, :], ACT.Sqrt).then_inc(o_rt, 1)
                for hd in range(H8):
                    act.wait_ge(o_y, hd + 1)
                    nc.scalar.activation(xh[:, hd, :], F[:, hd, :], ACT.Copy).then_inc(xs_hi, 1)

            def x_dve(dve):
                nc.vector.tensor_scalar(sso[:, :, :], sso[:, :, :], 1.0 / P, EPS, ALU.mult, ALU.add).then_inc(o_ms, 1)
                dve.wait_ge(o_rt, 1)
                nc.vector.reciprocal(sso[:, :, :], sso[:, :, :]).then_inc(o_in, 1)
                dve.wait_ge(o_in, 1)
                for s in range(H8 + 3):
                    if s < H8:
                        nc.vector.tensor_tensor(v4(G[:, s, :]), v4(G[:, s, :]),
                                                sso[:, s, :].rearrange("p (t o) -> p t o", o=1).broadcast_to([P, TB, P]),
                                                ALU.mult).then_inc(o_n, 1)
                    if 2 <= s < H8 + 2:
                        hd = s - 2
                        dve.wait_ge(o_t, hd + 1)
                        nc.vector.scalar_tensor_tensor(out=F[:, hd, :], in0=ps[OB + hd % 3][:, :], scalar=vB[:, 96:97],
                                                       in1=G[:, 24 + hd, :], op0=ALU.mult, op1=ALU.mult).then_inc(o_y, 1)
                    if s >= 3:
                        hd = s - 3
                        dve.wait_ge(xs_hi, x0 + hd + 1)
                        nc.vector.tensor_tensor(xl[:, hd, :], F[:, hd, :], xh[:, hd, :].bitcast(F32), ALU.subtract).then_inc(xs_lo, 1)

            def x_pe(pe, b):
                for hd in ((0, 1, 2) if b == 0 else (b + 2,)):
                    if hd >= H8:
                        continue
                    pe.wait_ge(o_n, hd + 1)
                    if hd >= 3:
                        pe.wait_ge(o_y, hd - 2)
                    for t in range(TB):
                        ins = pe.transpose(blk(ps[OB + hd % 3], t), blk(G[:, hd, :], t), ident[:, :])
                    ins.then_inc(o_t, 1)

            sums = resid_out("gdn_out", x_act, x_dve, x_pe)

        with ExitStack() as c:
            qkv = sb("swa_qkvz", [P, 20, SEQ], ctx=c)
            vt = sb("swa_v", [P, TB, 2 * P], ctx=c)
            mask = sb("swa_mask", [P, 2 * P], ctx=c)
            snk = sb("swa_sinks", [P, 16], ctx=c)
            zp = sb("swa_zp", [P, 6, SEQ], ctx=c)
            ev0 = n["ev"]
            turn = token_turn(lambda b: qkv[:, 10 + b, :], 2, vt, lambda b: (evac, ev0 + 10 + b + 1))
            (p_in, w_con, ang_d, trig, rot_mm, rp, rope_d) = (sem(f"swa_{x}") for x in ("pin", "con", "ang", "trig", "rot", "rp", "rope"))
            with ExitStack() as c2:
                pos = sb("swa_pos", [P, SEQ], I32, ctx=c2)
                inv = sb("swa_inv", [P, 1], ctx=c2)
                tg = sb("swa_trig", [P, 4, SEQ], ctx=c2)
                rot = sb("swa_rot", [P, P], ctx=c2)
                TWO_PI = 2 * np.pi
                C1 = 6.28125
                C2 = float(np.float32(round((TWO_PI - C1) * 2 ** 20) / 2 ** 20))
                C3 = float(np.float32(TWO_PI - C1 - C2))
                MAGIC = 1.5 * 2 ** 23
                LIM = 3.1415925
                RB = 10

                def sp_tail(sp):
                    sp.dma_start(pos[:, :], I["positions_2"].broadcast_to([P, SEQ])).then_inc(p_in, 16)
                    sp.dma_start(inv[:, :], I["rope_inv_freq"]).then_inc(p_in, 16)
                    sp.dma_start(snk[:, :], I["swa_sinks_2"].broadcast_to([P, 16])).then_inc(p_in, 16)

                def pool_tail(pool):
                    nc.gpsimd.memset(rot[:, :], 0.0).then_inc(w_con, 1)
                    nc.gpsimd.memset(mask[:, :], 0.0).then_inc(w_con, 1)
                    pool.wait_ge(w_con, 2)
                    r4 = rot[:, :].rearrange("p (a b r) -> p a b r", a=2, b=2)
                    nc.gpsimd.affine_select(out=r4[:, :, 0, :], in_=r4[:, :, 0, :], compare_op=ALU.not_equal, fill=-1.0, base=-32,
                                            pattern=[[-64, 2], [-1, 32]], channel_multiplier=1).then_inc(w_con, 1)
                    nc.gpsimd.affine_select(out=r4[:, :, 1, :], in_=r4[:, :, 1, :], compare_op=ALU.not_equal, fill=1.0, base=0,
                                            pattern=[[-64, 2], [-1, 32]], channel_multiplier=1).then_inc(w_con, 1)
                    nc.gpsimd.affine_select(out=mask[:, :], in_=mask[:, :], compare_op=ALU.is_gt, fill=NEG, base=0,
                                            pattern=[[1, 2 * P]], channel_multiplier=-1).then_inc(w_con, 1)
                    pool.wait_ge(w_con, 5)
                    nc.gpsimd.affine_select(out=mask[:, :], in_=mask[:, :], compare_op=ALU.is_ge, fill=NEG, base=P,
                                            pattern=[[-1, 2 * P]], channel_multiplier=1).then_inc(w_con, 1)
                    for b in range(RB):
                        pool.wait_ge(trig, 2)
                        pool.wait_ge(evac, ev0 + b + 1)
                        pool.wait_ge(rot_mm, b + 1)
                        nc.gpsimd.tensor_tensor(qkv[:, b, :], qkv[:, b, :], tg[:, 1, :], ALU.mult).then_inc(rp, 1)

                def pe_beside(pe, k):
                    if 4 <= k < 4 + RB:
                        b = k - 4
                        pe.wait_ge(w_con, 4)
                        if b >= 2:
                            pe.wait_ge(rope_d, 2 * (b - 2) + 1)
                        pe.wait_ge(evac, ev0 + b + 1)
                        pe.matmul(ps[6 + b % 2][:, :], rot[:, :], qkv[:, b, :], start=True, stop=True).then_inc(rot_mm, 1)
                    if 14 <= k < 18:
                        turn[0](pe, k - 14, k - 13)

                def act_start(act):
                    act.wait_ge(ang_d, 7)
                    nc.scalar.activation(tg[:, 0, :], tg[:, 0, :], ACT.Sin).then_inc(trig, 1)
                    nc.scalar.activation(tg[:, 1, :], tg[:, 1, :], ACT.Sin).then_inc(trig, 1)

                def act_beside(act, k):
                    if k in (17, 19):
                        b0, b1 = (12, 16) if k == 17 else (16, 20)
                        z = qkv[:, b0:b1, :]
                        act.wait_ge(evac, ev0 + b1)
                        nc.scalar.activation(z, z, ACT.Silu)

                def dve_start(dve):
                    k_ = [0]

                    def link(ins):
                        k_[0] += 1
                        ins.then_inc(ang_d, 1)
                        dve.wait_ge(ang_d, k_[0])
                    dve.wait_ge(p_in, 48)
                    a, b_, c_, d_ = (tg[:, q, :] for q in range(4))
                    link(nc.vector.tensor_scalar(a, pos[:, :], inv[:, 0:1], None, ALU.mult))
                    link(nc.vector.tensor_scalar(c_, a, float(1 / TWO_PI), MAGIC, ALU.mult, ALU.add))
                    link(nc.vector.tensor_scalar(c_, c_, MAGIC, None, ALU.subtract))
                    for C in (C1, C2, C3):
                        nc.vector.scalar_tensor_tensor(out=a, in0=c_, scalar=-C, in1=a, op0=ALU.mult, op1=ALU.add).then_inc(rr, 1)
                        rr_n[0] += 1
                        dve.wait_ge(rr, rr_n[0])
                    link(nc.vector.tensor_scalar(b_, a, float(np.pi / 2), None, ALU.add))
                    link(nc.vector.tensor_scalar(d_, b_, float(np.pi), TWO_PI, ALU.is_gt, ALU.mult))
                    link(nc.vector.tensor_tensor(b_, b_, d_, ALU.subtract))
                    link(nc.vector.tensor_scalar(tg[:, 0:2, :], tg[:, 0:2, :], LIM, -LIM, ALU.min, ALU.max))

                def dve_beside(dve, k):
                    if 5 <= k < 5 + RB:
                        b = k - 5
                        dve.wait_ge(trig, 2)
                        dve.wait_ge(rot_mm, b + 1)
                        t = tg[:, 2 + b % 2, :]
                        scale = HD ** -0.5 if b < 8 else 1.0
                        nc.vector.scalar_tensor_tensor(out=t, in0=ps[6 + b % 2][:, :], scalar=scale, in1=tg[:, 0, :],
                                                       op0=ALU.mult, op1=ALU.mult).then_inc(rope_d, 1)
                        dve.wait_ge(rope_d, 2 * b + 1)
                        dve.wait_ge(rp, b + 1)
                        nc.vector.scalar_tensor_tensor(out=qkv[:, b, :], in0=qkv[:, b, :], scalar=scale, in1=t,
                                                       op0=ALU.mult, op1=ALU.add).then_inc(rope_d, 1)
                    if 14 <= k < 18:
                        turn[1](dve, k - 14, k - 13)

                rr, rr_n = dve_link, steps_
                in_proj("swa_in", vA[:, col["norm_w_2"] + 3 * DB:col["norm_w_2"] + 4 * DB], qkv, sums=sums,
                        tails=dict(sp=sp_tail, pool=pool_tail),
                        beside=dict(pe=pe_beside, act=act_beside, dve=dve_beside, act_start=act_start, dve_start=dve_start))
            with ExitStack() as c2:
                units = []
                for qb in range(TB):
                    for b in range(DB):
                        for s in range(2):
                            k0, k1 = max(qb - 1, 0), qb + 1
                            klen = (k1 - k0) * P
                            kv, hd = 2 * (b // 4) + s, 8 * (b // 4) + 4 * s + b % 4
                            units.append(dict(
                                q=qkv[HD * s:HD * s + HD, b, qb * P:qb * P + P], k=qkv[HD * s:HD * s + HD, 8 + b // 4, k0 * P:k1 * P],
                                klen=klen, mask=mask[:, 2 * P - klen:2 * P], po=HD * s, m=HD, oc=(b % 4) * P,
                                v=[vt[:, x, kv * HD:kv * HD + HD] for x in range(k0, k1)], sink=snk[:, hd:hd + 1]))
                groups = [(8 * g + 7, F[:, 4 * (g % 2):4 * (g % 2) + 4, (g // 2) * P:(g // 2) * P + P],
                           lambda b: b[:, :].rearrange("p (a q) -> p a q", a=4)) for g in range(2 * TB)]
                pe_p, dve_p, act_p = softmax_attention("swa", units, groups, zp, c2)
                with nc.Block() as block:
                    @block.tensor
                    def _(pe):
                        pe_p(pe)

                    @block.vector
                    def _(dve):
                        dve_p(dve)

                    @block.scalar
                    def _(act):
                        act_p(act)
            sums = resid_out("swa_out", *gate_x(lambda b: qkv[:, 12 + b, :]))
        final(sums)


_NAMES = ["x", "p", "g_ffn1_pre", "g_ffn1_post", "w_ffn1_gate", "w_ffn1_up", "w_ffn1_down", "g_mix_pre", "g_mix_post",
          "w_in", "g_out_sb", "g_out_ch", "rel_bias", "w_out", "g_ffn2_pre", "g_ffn2_post", "w_ffn2_gate", "w_ffn2_up",
          "w_ffn2_down", "w_ple_proj", "w_ple_gate", "g_ple_post", "positions_2", "norm_w_2", "final_norm_w_2",
          "conv_w_in_2", "conv_w_conv_2", "conv_w_out_2", "fox_w_in_2", "fox_b_f_2", "fox_w_out_2", "gdn_w_in_2",
          "gdn_w_conv_2", "gdn_a_log_2", "gdn_dt_bias_2", "gdn_norm_w_2", "gdn_w_out_2", "swa_w_in_2", "swa_sinks_2",
          "swa_w_out_2"]


def kernel(**inputs):
    import concourse.bacc as bacc
    from concourse.bass_utils import run_bass_kernel_spmd

    nc = bacc.Bacc("TRN2", target_bir_lowering=False, num_devices=1, dynamic_dma_scratch_size=1024)
    arrays, I = {}, {}
    for name in _NAMES:
        a = np.ascontiguousarray(inputs[name])
        arrays[f"in_{name}"] = a
        I[name] = nc.dram_tensor(f"in_{name}", a.shape, mybir.dt.from_np(a.dtype), kind="ExternalInput").ap()
    out = nc.dram_tensor("out", (1, SEQ, D), F32, kind="ExternalOutput").ap()
    half = HD // 2
    freq = (10000.0 ** (-(np.arange(P) % half) / half)).astype(np.float32).reshape(P, 1)
    arrays["in_rope_inv_freq"] = freq
    I["rope_inv_freq"] = nc.dram_tensor("in_rope_inv_freq", freq.shape, F32, kind="ExternalInput").ap()
    kernel_program(nc, I, out)
    r = run_bass_kernel_spmd(nc, [arrays], core_ids=[0])
    return r.results[0]["out"]
```
